# Optimizing a Trainium2 kernel written in Bass

```python
import math
import jax, jax.numpy as jnp
from jax import lax
import numpy as np

D_MODEL = 1024
BATCH = 1
SEQ = 256
DEPTH = 1

ATT_HEADS = 16
ATT_KV_HEADS = 2
ATT_HEAD_DIM = 64
WINDOW = 128
ROPE_DIM = ATT_HEAD_DIM // 4
ROPE_THETA = 500000.0
ML_HEADS = 8
ML_QK_DIM = 64
ML_V_DIM = 128
ML_CHUNK = 64
GATE_CAP = 15.0
PEER_HEADS = 8
PEER_KEY_DIM = 128
N_KEYS = 128
N_EXPERTS = N_KEYS * N_KEYS
PEER_TOPK = 16
PEER_TOKEN_BLOCK = 128
EPS = 1e-6

ATT_Q_W = ATT_HEADS * ATT_HEAD_DIM
ATT_KV_W = ATT_KV_HEADS * ATT_HEAD_DIM
ML_QK_W = ML_HEADS * ML_QK_DIM
ML_V_W = ML_HEADS * ML_V_DIM
IN_SPLITS = (ATT_Q_W, ATT_KV_W, ATT_KV_W, ML_QK_W, ML_QK_W, ML_V_W, ML_HEADS, ML_HEADS, ML_V_W, D_MODEL, D_MODEL)
IN_WIDTH = ATT_Q_W + 2 * ATT_KV_W + 2 * ML_QK_W + 2 * ML_V_W + 2 * ML_HEADS + 2 * D_MODEL


def rmsnorm(x, gain):
    xf = x.astype(jnp.float32)
    r = lax.rsqrt(jnp.mean(xf * xf, axis=-1, keepdims=True) + EPS)
    return (xf * r * gain.astype(jnp.float32)).astype(x.dtype)

def partial_rope(x, positions):
    half = ROPE_DIM // 2
    inv_freq = ROPE_THETA ** (-jnp.arange(0, ROPE_DIM, 2, dtype=jnp.float32) / ROPE_DIM)
    ang = positions.astype(jnp.float32)[..., None] * inv_freq
    cos = jnp.cos(ang)[:, :, None, :]
    sin = jnp.sin(ang)[:, :, None, :]
    xf = x.astype(jnp.float32)
    x1 = xf[..., :half]
    x2 = xf[..., half:ROPE_DIM]
    rot = jnp.concatenate([x1 * cos - x2 * sin, x2 * cos + x1 * sin], axis=-1)
    return jnp.concatenate([rot, xf[..., ROPE_DIM:]], axis=-1).astype(x.dtype)

def sliding_window_attention(q, k, v, sinks):
    B, S = q.shape[0], q.shape[1]
    nb = S // WINDOW
    G = ATT_HEADS // ATT_KV_HEADS
    qb = q.reshape(B, nb, WINDOW, ATT_KV_HEADS, G, ATT_HEAD_DIM)
    kb = k.reshape(B, nb, WINDOW, ATT_KV_HEADS, ATT_HEAD_DIM)
    vb = v.reshape(B, nb, WINDOW, ATT_KV_HEADS, ATT_HEAD_DIM)

    def with_prev(t):
        prev = jnp.pad(t, ((0, 0), (1, 0), (0, 0), (0, 0), (0, 0)))[:, :-1]
        return jnp.concatenate([prev, t], axis=2)

    kband = with_prev(kb)
    vband = with_prev(vb)
    a_idx = jnp.arange(WINDOW)[:, None]
    c_idx = jnp.arange(2 * WINDOW)[None, :]
    band = (c_idx > a_idx) & (c_idx <= a_idx + WINDOW)
    sink = sinks.astype(jnp.float32).reshape(ATT_KV_HEADS, G)[None, :, :, None, None]
    scale = ATT_HEAD_DIM ** -0.5

    def one_block(args):
        qj, kj, vj, j = args
        s = jnp.einsum('bqhgd,bkhd->bhgqk', qj, kj).astype(jnp.float32) * scale
        valid = band & ((j * WINDOW + c_idx - WINDOW) >= 0)
        s = jnp.where(valid, s, -jnp.inf)
        m = jnp.maximum(jnp.max(s, axis=-1, keepdims=True), sink)
        p = jnp.exp(s - m)
        denom = jnp.sum(p, axis=-1, keepdims=True) + jnp.exp(sink - m)
        return jnp.einsum('bhgqk,bkhd->bqhgd', (p / denom).astype(vj.dtype), vj)

    xs = (jnp.moveaxis(qb, 1, 0), jnp.moveaxis(kband, 1, 0), jnp.moveaxis(vband, 1, 0),
          jnp.arange(nb, dtype=jnp.int32))
    out = lax.map(one_block, xs)
    return jnp.moveaxis(out, 0, 1).reshape(B, S, ATT_Q_W)

def mlstm_chunkwise(q, k, v, i_pre, f_pre):
    B, S, H = q.shape[0], q.shape[1], q.shape[2]
    L = ML_CHUNK
    nc = S // L
    f32 = jnp.float32
    qc = q.astype(f32).reshape(B, nc, L, H, ML_QK_DIM).transpose(1, 0, 3, 2, 4)
    kc = (k.astype(f32) * (ML_QK_DIM ** -0.5)).reshape(B, nc, L, H, ML_QK_DIM).transpose(1, 0, 3, 2, 4)
    vc = v.astype(f32).reshape(B, nc, L, H, ML_V_DIM).transpose(1, 0, 3, 2, 4)
    ic = i_pre.reshape(B, nc, L, H).transpose(1, 0, 3, 2)
    lfc = jax.nn.log_sigmoid(f_pre).reshape(B, nc, L, H).transpose(1, 0, 3, 2)
    causal = jnp.tril(jnp.ones((L, L), dtype=bool))

    def step(carry, xs):
        C, n, m = carry
        qj, kj, vj, ij, lfj = xs
        b = jnp.cumsum(lfj, axis=-1)
        dmat = jnp.where(causal, b[..., :, None] - b[..., None, :] + ij[..., None, :], -jnp.inf)
        inter = b + m[..., None]
        m_t = jnp.maximum(inter, jnp.max(dmat, axis=-1))
        w_intra = jnp.exp(dmat - m_t[..., None])
        w_inter = jnp.exp(inter - m_t)
        qk = jnp.einsum('bhtd,bhsd->bhts', qj, kj) * w_intra
        num = jnp.einsum('bhts,bhsv->bhtv', qk, vj) + w_inter[..., None] * jnp.einsum('bhvd,bhtd->bhtv', C, qj)
        den = jnp.sum(qk, axis=-1) + w_inter * jnp.einsum('bhd,bhtd->bht', n, qj)
        h = num / jnp.maximum(jnp.abs(den), jnp.exp(-m_t))[..., None]
        b_last = b[..., -1]
        g = b_last[..., None] - b + ij
        m_new = jnp.maximum(b_last + m, jnp.max(g, axis=-1))
        w_s = jnp.exp(g - m_new[..., None])
        decay = jnp.exp(b_last + m - m_new)
        C_new = decay[..., None, None] * C + jnp.einsum('bhs,bhsv,bhsd->bhvd', w_s, vj, kj)
        n_new = decay[..., None] * n + jnp.einsum('bhs,bhsd->bhd', w_s, kj)
        return (C_new, n_new, m_new), h

    init = (jnp.zeros((B, H, ML_V_DIM, ML_QK_DIM), f32), jnp.zeros((B, H, ML_QK_DIM), f32),
            jnp.zeros((B, H), f32))
    _, h = lax.scan(step, init, (qc, kc, vc, ic, lfc))
    return h.transpose(1, 0, 3, 2, 4).reshape(B, S, H, ML_V_DIM).astype(q.dtype)

def peer_ffn(x, w_query, sub_keys, expert_down, expert_up):
    B, S, D = x.shape
    xt = x.reshape((B * S) // PEER_TOKEN_BLOCK, PEER_TOKEN_BLOCK, D)
    K = PEER_TOPK

    def one_block(xb):
        t = xb.shape[0]
        q = (xb @ w_query).reshape(t, PEER_HEADS, 2, PEER_KEY_DIM // 2)
        s = jnp.einsum('thpd,hpkd->thpk', q, sub_keys).astype(jnp.float32)
        top_s, top_i = lax.top_k(s, K)
        cand_s = (top_s[:, :, 0, :, None] + top_s[:, :, 1, None, :]).reshape(t, PEER_HEADS, K * K)
        cand_i = (top_i[:, :, 0, :, None] * N_KEYS + top_i[:, :, 1, None, :]).reshape(t, PEER_HEADS, K * K)
        best_s, best_pos = lax.top_k(cand_s, K)
        idx = jnp.take_along_axis(cand_i, best_pos, axis=-1)
        gate = jax.nn.softmax(best_s, axis=-1)
        u = expert_down[idx]
        act = jax.nn.gelu(jnp.einsum('td,thkd->thk', xb, u).astype(jnp.float32), approximate=False)
        vv = expert_up[idx]
        return jnp.einsum('thk,thkd->td', (gate * act).astype(xb.dtype), vv)

    return lax.map(one_block, xt).reshape(B, S, D)

def split_columns(proj):
    offs = np.cumsum(np.array(IN_SPLITS))[:-1].tolist()
    return jnp.split(proj, offs, axis=-1)

def first_inputs(seed: int = 0) -> dict:
    key = jax.random.key(seed)
    ks = jax.random.split(key, 20)
    f32 = jnp.float32
    nrm = lambda k, shape, s: jax.random.normal(k, shape, f32) * s
    x = jax.random.normal(ks[0], (BATCH, SEQ, D_MODEL), f32)
    offset = jax.random.randint(ks[1], (BATCH, 1), 0, 1024, dtype=jnp.int32)
    positions = offset + jnp.arange(SEQ, dtype=jnp.int32)[None, :]
    return {
        "x": x,
        "positions": positions,
        "norm1_gain": 1.0 + nrm(ks[2], (DEPTH, D_MODEL), 0.02),
        "w_in": nrm(ks[3], (DEPTH, D_MODEL, IN_WIDTH), D_MODEL ** -0.5),
        "ml_i_bias": nrm(ks[4], (DEPTH, ML_HEADS), 0.1),
        "ml_f_bias": jnp.linspace(3.0, 6.0, ML_HEADS, dtype=f32)[None, :] + nrm(ks[5], (DEPTH, ML_HEADS), 0.1),
        "q_norm_gain": 1.0 + nrm(ks[6], (DEPTH, ATT_HEAD_DIM), 0.02),
        "k_norm_gain": 1.0 + nrm(ks[7], (DEPTH, ATT_HEAD_DIM), 0.02),
        "attn_sinks": nrm(ks[8], (DEPTH, ATT_HEADS), 0.5),
        "ml_out_norm_gain": 1.0 + nrm(ks[9], (DEPTH, ML_V_W), 0.02),
        "w_branch_attn": nrm(ks[10], (DEPTH, ATT_Q_W, D_MODEL), ATT_Q_W ** -0.5),
        "w_branch_mlstm": nrm(ks[11], (DEPTH, ML_V_W, D_MODEL), ML_V_W ** -0.5),
        "w_out": nrm(ks[12], (DEPTH, D_MODEL, D_MODEL), D_MODEL ** -0.5),
        "norm2_gain": 1.0 + nrm(ks[13], (DEPTH, D_MODEL), 0.02),
        "peer_w_query": nrm(ks[14], (DEPTH, D_MODEL, PEER_HEADS * PEER_KEY_DIM), D_MODEL ** -0.5),
        "peer_sub_keys": nrm(ks[15], (DEPTH, PEER_HEADS, 2, N_KEYS, PEER_KEY_DIM // 2), (PEER_KEY_DIM // 2) ** -0.5),
        "peer_down": nrm(ks[16], (DEPTH, N_EXPERTS, D_MODEL), D_MODEL ** -0.5),
        "peer_up": nrm(ks[17], (DEPTH, N_EXPERTS, D_MODEL), PEER_HEADS ** -0.5),
    }

def first_block(x, positions, norm1_gain, w_in, ml_i_bias, ml_f_bias, q_norm_gain, k_norm_gain,
              attn_sinks, ml_out_norm_gain, w_branch_attn, w_branch_mlstm, w_out, norm2_gain,
              peer_w_query, peer_sub_keys, peer_down, peer_up):
    B, S, _ = x.shape
    for l in range(DEPTH):
        h = rmsnorm(x, norm1_gain[l])
        (aq, ak, av, mq, mk, mv, mi, mf, mo, gate_a, gate_m) = split_columns(h @ w_in[l])
        aq = partial_rope(rmsnorm(aq.reshape(B, S, ATT_HEADS, ATT_HEAD_DIM), q_norm_gain[l]), positions)
        ak = partial_rope(rmsnorm(ak.reshape(B, S, ATT_KV_HEADS, ATT_HEAD_DIM), k_norm_gain[l]), positions)
        av = av.reshape(B, S, ATT_KV_HEADS, ATT_HEAD_DIM)
        att = sliding_window_attention(aq, ak, av, attn_sinks[l])
        att_b = att @ w_branch_attn[l]
        i_pre = mi.astype(jnp.float32) + ml_i_bias[l].astype(jnp.float32)
        f_pre = mf.astype(jnp.float32) + ml_f_bias[l].astype(jnp.float32)
        i_pre = GATE_CAP * jnp.tanh(i_pre / GATE_CAP)
        f_pre = GATE_CAP * jnp.tanh(f_pre / GATE_CAP)
        hm = mlstm_chunkwise(mq.reshape(B, S, ML_HEADS, ML_QK_DIM), mk.reshape(B, S, ML_HEADS, ML_QK_DIM),
                             mv.reshape(B, S, ML_HEADS, ML_V_DIM), i_pre, f_pre)
        hm = rmsnorm(hm, ml_out_norm_gain[l].reshape(ML_HEADS, ML_V_DIM)).reshape(B, S, ML_V_W)
        hm = hm * jax.nn.sigmoid(mo)
        ml_b = hm @ w_branch_mlstm[l]
        mixed = jax.nn.sigmoid(gate_a) * att_b + jax.nn.sigmoid(gate_m) * ml_b
        x = x + mixed @ w_out[l]
        x = x + peer_ffn(rmsnorm(x, norm2_gain[l]), peer_w_query[l], peer_sub_keys[l], peer_down[l], peer_up[l])
    return x


SB_HEADS = 8
SB_HEAD_DIM = 64
SB_WIDTH = SB_HEADS * SB_HEAD_DIM
Q_BLOCK = 128
HG_HEADS = 4
HG_KEY_DIM = 128
HG_VAL_DIM = 128
HG_KEY_WIDTH = HG_HEADS * HG_KEY_DIM
HG_WIDTH = HG_HEADS * HG_VAL_DIM
HG_CHUNK = 64
MIX_WIDTH = SB_WIDTH + HG_WIDTH
FFN_HIDDEN = -(-8 * D_MODEL // (3 * 256)) * 256
IN_SIZES = (SB_WIDTH, SB_WIDTH, SB_WIDTH, HG_KEY_WIDTH, HG_KEY_WIDTH,
            HG_WIDTH, HG_WIDTH, D_MODEL, D_MODEL)
IN_WIDTH_2 = sum(IN_SIZES)


def rms_norm(x, g):
    xf = x.astype(jnp.float32)
    y = xf * lax.rsqrt(jnp.mean(xf * xf, axis=-1, keepdims=True) + EPS)
    return (y * g.astype(jnp.float32)).astype(x.dtype)

def split_cols(t, sizes):
    idx, acc = [], 0
    for s in sizes[:-1]:
        acc += s
        idx.append(acc)
    return jnp.split(t, idx, axis=-1)

def stick_breaking_attention(q, k, v):
    seq = q.shape[2]
    scale = SB_HEAD_DIM ** -0.5
    outs = []
    for blk in range(seq // Q_BLOCK):
        t0 = blk * Q_BLOCK
        end = t0 + Q_BLOCK
        qb, kb, vb = q[:, :, t0:end], k[:, :, :end], v[:, :, :end]
        z = jnp.einsum('bhtd,bhsd->bhts', qb, kb).astype(jnp.float32) * scale
        t_idx = t0 + jnp.arange(Q_BLOCK)[:, None]
        s_idx = jnp.arange(end)[None, :]
        causal = s_idx < t_idx
        sp = jnp.where(causal, jax.nn.softplus(z), 0.0)
        rest = lax.cumsum(sp, axis=3, reverse=True) - sp
        w = jnp.where(causal, jnp.exp(jax.nn.log_sigmoid(z) - rest), 0.0)
        outs.append(jnp.einsum('bhts,bhsd->bhtd', w.astype(vb.dtype), vb))
    return jnp.concatenate(outs, axis=2)

def hgrn2_mixer(q_in, f_in, i_in, g_in, lb, norm_g):
    B, S, _ = q_in.shape
    n_chunks = S // HG_CHUNK
    f = lb + (1.0 - lb) * jax.nn.sigmoid(f_in.astype(jnp.float32))
    log_f = jnp.log(f)
    key = 1.0 - f
    q = jax.nn.silu(q_in.astype(jnp.float32))
    val = i_in.astype(jnp.float32)

    def to_chunks(t):
        return t.reshape(B, n_chunks, HG_CHUNK, HG_HEADS, -1).transpose(1, 0, 3, 2, 4)

    mask = jnp.tril(jnp.ones((HG_CHUNK, HG_CHUNK), dtype=bool))[:, :, None]

    def step(state, xs):
        qc, kc, vc, gc = xs
        b = jnp.cumsum(gc, axis=2)
        diff = b[:, :, :, None, :] - b[:, :, None, :, :]
        decay = jnp.exp(jnp.where(mask, diff, -jnp.inf))
        attn = jnp.einsum('bhtk,bhsk,bhtsk->bhts', qc, kc, decay)
        o_intra = jnp.einsum('bhts,bhsv->bhtv', attn, vc)
        o_inter = jnp.einsum('bhtk,bhkv->bhtv', qc * jnp.exp(b), state)
        b_last = b[:, :, -1:, :]
        new_state = jnp.exp(b_last[:, :, 0, :])[..., None] * state + \
            jnp.einsum('bhsk,bhsv->bhkv', kc * jnp.exp(b_last - b), vc)
        return new_state, o_intra + o_inter

    s0 = jnp.zeros((B, HG_HEADS, HG_KEY_DIM, HG_VAL_DIM), jnp.float32)
    _, o = lax.scan(step, s0, (to_chunks(q), to_chunks(key), to_chunks(val), to_chunks(log_f)))
    o = o.transpose(1, 0, 3, 2, 4).reshape(B, S, HG_HEADS, HG_VAL_DIM)
    o = rms_norm(o, norm_g)
    gate = jax.nn.silu(g_in.astype(jnp.float32)).reshape(B, S, HG_HEADS, HG_VAL_DIM)
    return (o * gate).reshape(B, S, HG_WIDTH).astype(q_in.dtype)

def hybrid_layer(x, norm1_g, w_in, q_norm_g, k_norm_g, lb, hg_norm_g, w_branch, w_out,
                 norm2_g, w_gate, w_up, w_down):
    B, S, _ = x.shape
    xn = rms_norm(x, norm1_g)
    proj = xn @ w_in
    q_sb, k_sb, v_sb, q_hg, f_hg, i_hg, g_hg, gate_sb, gate_hg = split_cols(proj, IN_SIZES)

    def heads(t):
        return t.reshape(B, S, SB_HEADS, SB_HEAD_DIM).transpose(0, 2, 1, 3)

    q = rms_norm(heads(q_sb), q_norm_g)
    k = rms_norm(heads(k_sb), k_norm_g)
    o_sb = stick_breaking_attention(q, k, heads(v_sb))
    o_sb = o_sb.transpose(0, 2, 1, 3).reshape(B, S, SB_WIDTH)

    o_hg = hgrn2_mixer(q_hg, f_hg, i_hg, g_hg, lb, hg_norm_g)

    y_sb = o_sb @ w_branch[:SB_WIDTH]
    y_hg = o_hg @ w_branch[SB_WIDTH:]
    mixed = jax.nn.sigmoid(gate_sb) * y_sb + jax.nn.sigmoid(gate_hg) * y_hg
    h = x + mixed @ w_out

    hn = rms_norm(h, norm2_g)
    ffn = (jax.nn.silu(hn @ w_gate) * (hn @ w_up)) @ w_down
    return h + ffn

def second_inputs(seed: int = 0) -> dict:
    key = jax.random.key(seed)
    ks = jax.random.split(key, 13)
    n = jax.random.normal
    f32 = jnp.float32
    return {
        "x": n(ks[0], (BATCH, SEQ, D_MODEL), f32),
        "norm1_g": 1.0 + 0.02 * n(ks[1], (DEPTH, D_MODEL), f32),
        "w_in": n(ks[2], (DEPTH, D_MODEL, IN_WIDTH_2), f32) * D_MODEL ** -0.5,
        "q_norm_g": 1.0 + 0.02 * n(ks[3], (DEPTH, SB_HEAD_DIM), f32),
        "k_norm_g": 1.0 + 0.02 * n(ks[4], (DEPTH, SB_HEAD_DIM), f32),
        "lb_table": 0.5 * n(ks[5], (DEPTH + 1, HG_KEY_WIDTH), f32),
        "hg_norm_g": 1.0 + 0.02 * n(ks[6], (DEPTH, HG_VAL_DIM), f32),
        "w_branch": n(ks[7], (DEPTH, MIX_WIDTH, D_MODEL), f32) * SB_WIDTH ** -0.5,
        "w_out": n(ks[8], (DEPTH, D_MODEL, D_MODEL), f32) * D_MODEL ** -0.5,
        "norm2_g": 1.0 + 0.02 * n(ks[9], (DEPTH, D_MODEL), f32),
        "w_ffn_gate": n(ks[10], (DEPTH, D_MODEL, FFN_HIDDEN), f32) * D_MODEL ** -0.5,
        "w_ffn_up": n(ks[11], (DEPTH, D_MODEL, FFN_HIDDEN), f32) * D_MODEL ** -0.5,
        "w_ffn_down": n(ks[12], (DEPTH, FFN_HIDDEN, D_MODEL), f32) * FFN_HIDDEN ** -0.5,
    }

def second_block(x, norm1_g, w_in, q_norm_g, k_norm_g, lb_table, hg_norm_g, w_branch, w_out,
              norm2_g, w_ffn_gate, w_ffn_up, w_ffn_down):
    lower_bounds = jnp.cumsum(jax.nn.softmax(lb_table.astype(jnp.float32), axis=0), axis=0)
    h = x
    for layer in range(DEPTH):
        h = hybrid_layer(h, norm1_g[layer], w_in[layer], q_norm_g[layer], k_norm_g[layer],
                         lower_bounds[layer], hg_norm_g[layer], w_branch[layer], w_out[layer],
                         norm2_g[layer], w_ffn_gate[layer], w_ffn_up[layer], w_ffn_down[layer])
    return h


def setup_inputs(seed=0):
    out = dict(first_inputs(seed))
    for name, value in second_inputs(seed + 1).items():
        if name != "x":
            out[name + "_2"] = value
    return out


def reference(
    x, positions, norm1_gain, w_in, ml_i_bias, ml_f_bias, q_norm_gain, k_norm_gain, attn_sinks,
    ml_out_norm_gain, w_branch_attn, w_branch_mlstm, w_out, norm2_gain, peer_w_query,
    peer_sub_keys, peer_down, peer_up, norm1_g_2, w_in_2, q_norm_g_2, k_norm_g_2, lb_table_2,
    hg_norm_g_2, w_branch_2, w_out_2, norm2_g_2, w_ffn_gate_2, w_ffn_up_2, w_ffn_down_2,
):
    x = first_block(
        x, positions, norm1_gain, w_in, ml_i_bias, ml_f_bias, q_norm_gain, k_norm_gain,
        attn_sinks, ml_out_norm_gain, w_branch_attn, w_branch_mlstm, w_out, norm2_gain,
        peer_w_query, peer_sub_keys, peer_down, peer_up,
    )
    return second_block(
        x, norm1_g_2, w_in_2, q_norm_g_2, k_norm_g_2, lb_table_2, hg_norm_g_2, w_branch_2,
        w_out_2, norm2_g_2, w_ffn_gate_2, w_ffn_up_2, w_ffn_down_2,
    )


_drawn_inputs = setup_inputs


def setup_inputs(seed=0):
    import zlib

    import numpy as np

    out = dict(_drawn_inputs(seed))
    spreads = {}
    factors = {'ml_i_bias': 8.0,
     'q_norm_gain': 6.15,
     'k_norm_gain': 6.124,
     'attn_sinks': 28.399,
     'ml_out_norm_gain': 3.222,
     'norm1_g_2': 4.511,
     'q_norm_g_2': 25.824,
     'k_norm_g_2': 27.954,
     'lb_table_2': 3.214,
     'hg_norm_g_2': 8.0,
     'norm2_g_2': 13.508}
    for name, (base, spread) in spreads.items():
        noise = np.random.default_rng([zlib.crc32(name.encode()), seed]).standard_normal(out[name].shape)
        drawn = base * np.exp(spread * noise) if base else spread * noise
        out[name] = __import__('jax').numpy.asarray(drawn.astype(out[name].dtype))
    for name, factor in factors.items():
        out[name] = (out[name] * factor).astype(out[name].dtype)
    return out
```

```python
from contextlib import ExitStack

import numpy as np
import concourse.bass as bass
from concourse import mybir

F32 = mybir.dt.float32
U32 = mybir.dt.uint32
I32 = mybir.dt.int32
ALU = mybir.AluOpType
ACT = mybir.ActivationFunctionType
AX = mybir.AxisListType.X

P = 128
S = 256
NB = S // P
D = 1024
KT = D // P
EPS = 1e-6
NEG = -1e30

AH, AKV, AD = 16, 2, 64
ROPE = AD // 4
RH = ROPE // 2
ROPE_THETA = 500000.0
MH, MQ, MV = 8, 64, 128
CAP = 15.0
PH, NKEY, TOPK = 8, 128, 16
AQ0 = 0
AK0 = AQ0 + AH * AD
AV0 = AK0 + AKV * AD
MQ0 = AV0 + AKV * AD
MK0 = MQ0 + MH * MQ
MV0 = MK0 + MH * MQ
MI0 = MV0 + MH * MV
MF0 = MI0 + MH
MO0 = MF0 + MH
GA0 = MO0 + MH * MV
GM0 = GA0 + D
W1N = GM0 + D

SH, SD = 8, 64
HH, HK, HV = 4, 128, 128
HC = 16
NHC = S // HC
SBW = SH * SD
HGW = HH * HV
FF = -(-8 * D // (3 * 256)) * 256
W2N = 3 * SBW + 2 * HH * HK + 2 * HGW + 2 * D

CW = 512
DSLOTS = 8
SLOTS = 4

TWO_PI_PARTS = (6.28125, 0.0019352436065673828, 6.357301884918343e-08)
MAGIC = 12582912.0
PI_IN = 3.1415925


def inv_freq():
    return (np.float32(ROPE_THETA) ** (-np.arange(0, ROPE, 2, dtype=np.float32) / np.float32(ROPE))).astype(np.float32)


def build(nc, a, out):
    ctx = ExitStack()
    with ctx:
        def sb(name, shape, dt=F32):
            return ctx.enter_context(nc.sbuf_tensor(name, shape, dt))

        made = {}

        def sem(name):
            if name not in made:
                made[name] = ctx.enter_context(nc.semaphore(name))
            return made[name]

        NSMALL = 10
        ring = sb("ring", [P, SLOTS, KT, CW])
        xres = sb("xres", [P, NB, D])
        xn = sb("xn", [P, NB, D])
        hT = sb("hT", [P, KT, S])
        arena = sb("arena", [P, 23808])
        ps = ctx.enter_context(nc.psum_tensor("ps", [P, 8, 512], F32))

        class Area:
            def __init__(self, at=0):
                self.at = at

            def take(self, *shape, dt=F32):
                n = int(np.prod(shape))
                v = arena[:, self.at:self.at + n]
                self.at += n
                assert self.at <= 23808, self.at
                if dt != F32:
                    v = v.bitcast(dt)
                if len(shape) > 1:
                    names = "abcdef"[:len(shape)]
                    v = v.rearrange(f"p ({' '.join(names)}) -> p {' '.join(names)}",
                                    **{k: s for k, s in zip(names[1:], shape[1:])})
                return v

        ident = sb("ident", [P, P])
        ones = sb("ones", [P, P])
        mask_band = sb("mask_band", [P, NB, P])
        mask_inc = sb("mask_inc", [P, P])
        sel = sb("sel", [P, MH, P])
        gcol = sb("gcol", [P, 4, KT])
        mlgain = sb("mlgain", [P, KT])
        qkgain = sb("qkgain", [P, 2, AD])
        sinks = sb("sinks", [P, AH])
        ifbias = sb("ifbias", [P, 2, MH])
        pos_i = sb("pos_i", [P, NB], I32)
        freq = sb("freq", [P, RH])
        ss = sb("ss", [P, NB])
        ms = sb("ms", [P, NB])
        sd = sb("sd", [P, NB])
        rr = sb("rr", [P, NB])

        one = Area()
        p1 = one.take(NB, AH * AD + 2 * AKV * AD + 2 * MH)
        sga = one.take(KT, S)
        sgm = one.take(KT, S)
        mo = one.take(NB, MH * MV)
        mva = one.take(NB, MH, MV + 1)
        mqT = one.take(MH // 2, S)
        mkT = one.take(MH // 2, S)
        qT = one.take(KT, S)
        kT = one.take(AKV, S)
        attT = one.take(KT, S)
        wl = one.take(MH, 3, P)
        cw = one.take(2, 3 * P)
        at_sm = one.at
        sm = one.take(4, S)
        pt = one.take(NB, 4, P)
        sq = Area(at_sm).take((AH + AKV) * AD)
        hmT = Area(0)
        hmT.at = 0
        hraw = Area(0).take(NB, MH, MV + 1)
        off_q = NB * 1296 + 2 * KT * S + NB * D + NB * MH * (MV + 1)
        hmT = Area(off_q).take(KT, S)
        hs = Area(off_q + 2048).take(NB, MH, MV)
        mixT = Area(off_q + 2048).take(KT, S)
        hsq = Area(off_q + 2048 + 2048 + 512 + 2048).take(NB, MH, MV)
        tmpT = hsq.rearrange("p a b c -> p (a b c)").rearrange("p (a b) -> p a b", b=S)

        two = Area()
        h2 = two.take(NB, D)
        sk = two.take(PH, NKEY)
        qpT = two.take(PH, S)
        scr = [two.take(PH, 2, NKEY), qpT.rearrange("p h (c k) -> p h c k", c=2)]
        hot = two.take(PH, TOPK, TOPK)
        picked = two.take(PH, TOPK, TOPK)
        n2row = hot.rearrange("p a b c -> p (a b c)")[:, 0:D]
        tv = two.take(PH, 2, TOPK)
        ti = two.take(PH, 2, TOPK, dt=U32)
        tif = two.take(PH, 2, TOPK)
        bv = two.take(PH, TOPK)
        bp = two.take(PH, TOPK, dt=U32)
        bij = two.take(2, PH * TOPK, dt=U32)
        bijf = two.take(2, PH * TOPK)
        exf = two.take(3, PH * TOPK)
        gate = two.take(NB, PH * TOPK)
        idx = two.take(NB, PH * TOPK, dt=U32)
        rows_d = two.take(DSLOTS, D)
        rows_u = ring[:].rearrange("p s t (c n) -> p (s t c) n", n=CW).rearrange("p (k two) n -> p k (two n)", two=2)[:, 0:TOPK, :]
        iota16 = sb("iota16", [P, TOPK])
        idx_st = sb("idx_st", [P, 2, TOPK], U32)
        dots = sb("dots", [P, 2, TOPK])
        gelu = sb("gelu", [P, 2, TOPK])
        wgt = sb("wgt", [P, 2, TOPK])
        diag = sb("diag", [P, 4, P])
        gsum = sb("gsum", [P, 2, PH])

        thr = Area()
        p2 = thr.take(NB, 3 * SBW)
        qkT2 = thr.take(8, S)
        zm = thr.take(4, 3 * P)
        sp_ = thr.take(4, 3 * P)
        wT = thr.take(4, 3 * P)
        end_sb = thr.at
        hv = thr.take(NB, HGW)
        hq = thr.take(HH, S)
        hf = thr.take(HH, S)
        hg = thr.take(HH, S)
        sg2 = thr.take(2 * KT, S)
        osbT = thr.take(SBW // P, S)
        ohgT = thr.take(HGW // P, S)
        far = thr.at
        hgp = Area(0)
        key = hgp.take(HH, S)
        bb = hgp.take(HH, S)
        qe = hgp.take(HH, S)
        keT = hgp.take(HH, S)
        ket = hgp.take(NB, HH, P)
        vpar = hgp.take(2, NB, HGW)
        AT = hgp.take(HH, NB, P)
        state = hgp.take(3, HH, P)
        assert hgp.at <= end_sb
        xbuf = xn[:].rearrange("p b (h t) -> p b h t", h=HH)
        osq = key.rearrange("p h (b t) -> p h b t", b=NB)
        orr = bb.rearrange("p h (b t) -> p h b t", b=NB)
        mixT2 = Area(0).take(KT, S)
        tmp2 = Area(2048).take(2, S)
        ffa = Area(far)
        silu = Area(3072).take(2, 2, S)
        hid = Area(3072 + 1024).take(4, 2, S)
        mask_str = sb("mask_str", [P, P])
        tri = sb("tri", [P, P])
        every16 = sb("every16", [P, P + HC])
        m16 = sb("m16", [P, P])
        restart = sb("restart", [P, HH * S])
        par = sb("par", [P, 2])
        sbgain = sb("sbgain", [P, 2])
        hgain = sb("hgain", [P, 1])
        lbt = sb("lbt", [P, 2, HH])
        lbs = sb("lbs", [P, 5, HH])
        dec = sb("dec", [P, HH, NHC])
        hst2 = sb("hst2", [P, 3, 2 * SH])

        kd = Area(at_sm + 1152).take(NB, 2 * AKV * AD)
        ang = sb("ang", [P, 4, NB, RH])
        cs = sb("cs", [P, 2, NB, RH])
        posf = sb("posf", [P, NB])
        hst = sb("hst", [P, 3, AH + AKV])
        rt = Area(at_sm - 768 - 3072).take(4, AH + AKV, RH)
        am = sb("am", [P, 6, 4])
        gt = sb("gt", [P, 4, NB, MH])
        aT = sb("aT", [P, NB, MH])
        em = sb("em", [P, NB, MH])
        rows = sb("rows", [MH, 6, S])
        den = sb("den", [P, 4, NB, MH])

        block = ctx.enter_context(nc.Block())

        def wview(w):
            return w.rearrange("(t p) n -> p t n", p=P)

        w1 = wview(a["w_in"])
        chunks = []

        used = []
        multiplied = {}

        def add(name, done, *parts):
            multiplied[done] = multiplied.get(done, 0) + 2
            used.append((done, multiplied[done]))
            chunks.append((name, parts))

        for c in range(2):
            add("aq", "p1_done", (w1[:, :, AQ0 + c * CW:AQ0 + (c + 1) * CW], 0))
        add("kv", "p1_done", (w1[:, :, AK0:MQ0], 0), (w1[:, :, MI0:MO0], MQ0 - AK0))
        add("mq", "p1_done", (w1[:, :, MQ0:MQ0 + CW], 0))
        add("mk", "p1_done", (w1[:, :, MK0:MK0 + CW], 0))
        for c in range(2):
            add("mv", "p1_done", (w1[:, :, MV0 + c * CW:MV0 + (c + 1) * CW], 0))
        for c in range(2):
            add("mo", "p1_done", (w1[:, :, MO0 + c * CW:MO0 + (c + 1) * CW], 0))
        for c in range(4):
            add("gates", "p1_done", (w1[:, :, GA0 + c * CW:GA0 + (c + 1) * CW], 0))
        NW1 = len(chunks)
        for nm in ("w_branch_attn", "w_branch_mlstm", "w_out"):
            v = wview(a[nm])
            for c in range(2):
                add(nm, "out_done" if nm == "w_out" else "br_done", (v[:, :, c * CW:(c + 1) * CW], 0))
        v = wview(a["peer_w_query"])
        for c in range(2):
            add("query", "q_done", (v[:, :, c * CW:(c + 1) * CW], 0))
        NPEER = len(chunks)
        w2 = wview(a["w_in_2"])
        for c, nm in enumerate(("sb", "sb", "sb", "hq", "hf", "hv", "hg", "g2", "g2", "g2", "g2")):
            add(nm, "p2_done", (w2[:, :, c * CW:(c + 1) * CW], 0))
        N2 = len(chunks)
        v = wview(a["w_branch_2"])
        for c in range(2):
            add("branch_2", "br2_done", (v[:, :, c * CW:(c + 1) * CW], 0))
            multiplied["br2_done"] += 2
            used[-1] = ("br2_done", multiplied["br2_done"])
        v = wview(a["w_out_2"])
        for c in range(2):
            add("out_2", "out2_done", (v[:, :, c * CW:(c + 1) * CW], 0))
        fg, fu = wview(a["w_ffn_gate_2"]), wview(a["w_ffn_up_2"])
        fd = wview(a["w_ffn_down_2"])
        NFF = FF // S
        for c in range(NFF):
            add("gate_up", "gu_done", (fg[:, :, c * S:(c + 1) * S], 0), (fu[:, :, c * S:(c + 1) * S], S))
            if c % 2 or c == NFF - 1:
                c0 = c - c % 2
                add("down", "down_done", (fd[:, 2 * c0:2 * (c + 1), :], None))
                multiplied["down_done"] -= 1
                used[-1] = ("down_done", multiplied["down_done"])
        loads = []
        per_slot = [0] * SLOTS
        for n, (nm, parts) in enumerate(chunks):
            per_slot[n % SLOTS] += 16 * len(parts)
            loads.append(per_slot[n % SLOTS])

        @block.sync
        def _(sp):
            sp.dma_start(xres[:], a["x"].rearrange("(b p) n -> p b n", p=P)).then_inc(sem("x_loaded"), 16)
            for n, (nm, parts) in enumerate(chunks):
                if n >= SLOTS:
                    sp.wait_ge(sem(used[n - SLOTS][0]), used[n - SLOTS][1])
                if n == NPEER:
                    sp.wait_ge(sem("row_free"), TOPK * (1 + NB * PH))
                if n == NPEER - 2:
                    sp.wait_ge(sem("x2_ready"), 4)
                    sp.dma_start(sk, a["sub_keys"]).then_inc(sem("sk_loaded"), 16)
                    sp.dma_start(n2row, a["n2row"]).then_inc(sem("sk_loaded"), 16)
                for v, at in parts:
                    if at is None:
                        rows4 = ring[:, n % SLOTS, :, :].rearrange("p (t c) n -> p t (c n)", c=2)
                        sp.dma_start(rows4[:, 0:v.shape[1], :], v).then_inc(sem(f"w_loaded{n % SLOTS}"), 16)
                        continue
                    sp.dma_start(ring[:, n % SLOTS, :, at:at + v.shape[2]], v).then_inc(sem(f"w_loaded{n % SLOTS}"), 16)
            sp.wait_ge(sem("x5_ready"), 4)
            sp.dma_start(out.rearrange("(b p) n -> p b n", p=P), xres[:]).then_inc(sem("stored"), 16)
            sp.wait_ge(sem("stored"), 16)

        @block.gpsimd
        def _(pool):
            step = [0]

            def link(ins):
                step[0] += 1
                ins.then_inc(sem("pool_step"), 1)
                pool.wait_ge(sem("pool_step"), step[0])

            for n, (t, v) in enumerate((("gcol", gcol[:]), ("mlgain", mlgain[:]), ("qkgain", qkgain[:]), ("sinks", sinks[:]),
                         ("ifbias", ifbias[:]), ("pos", pos_i[:]), ("freq", freq[:]), ("sbgain", sbgain[:]), ("hgain", hgain[:]), ("lbt", lbt[:]))):
                pool.dma_start(v, a[t]).then_inc(sem("small_loaded"), 16)
            link(pool.memset(ident[:], 0.0))
            pool.affine_select(out=ident[:], in_=ident[:], compare_op=ALU.not_equal, fill=1.0, base=0,
                               pattern=[[-1, P]], channel_multiplier=1).then_inc(sem("ident_ready"), 1)
            pool.memset(ones[:], 1.0)
            pool.memset(mask_band[:], 0.0)
            pool.memset(mask_inc[:], 0.0)
            link(pool.memset(sel[:], 0.0))
            pool.affine_select(out=mask_band[:, 0, :], in_=mask_band[:, 0, :], compare_op=ALU.is_gt, fill=NEG, base=0,
                               pattern=[[1, P]], channel_multiplier=-1)
            pool.affine_select(out=mask_band[:, 1, :], in_=mask_band[:, 1, :], compare_op=ALU.is_ge, fill=NEG, base=0,
                               pattern=[[-1, P]], channel_multiplier=1)
            pool.affine_select(out=mask_inc[:], in_=mask_inc[:], compare_op=ALU.is_ge, fill=NEG, base=0,
                               pattern=[[1, P]], channel_multiplier=-1)
            pool.affine_select(out=sel[:], in_=sel[:], compare_op=ALU.not_equal, fill=1.0, base=0,
                               pattern=[[-1, MH], [0, P]], channel_multiplier=1)
            pool.memset(mva[:, :, :, MV:MV + 1], 1.0).then_inc(sem("masks_ready"), 1)
            pool.iota(iota16[:], [[1, TOPK]], base=0, channel_multiplier=0, allow_small_or_imprecise_dtypes=True)
            pool.memset(mask_str[:], 0.0)
            pool.memset(tri[:], 1.0)
            pool.memset(every16[:], 0.0)
            pool.memset(m16[:], 1.0)
            pool.memset(restart[:], 1.0)
            link(pool.memset(par[:], 0.0))
            pool.affine_select(out=mask_str[:], in_=mask_str[:], compare_op=ALU.is_gt, fill=NEG, base=0,
                               pattern=[[1, P]], channel_multiplier=-1)
            pool.affine_select(out=tri[:], in_=tri[:], compare_op=ALU.is_ge, fill=0.0, base=0,
                               pattern=[[-1, P]], channel_multiplier=1)
            pool.memset(every16[:].rearrange("p (a b) -> p a b", b=HC)[:, :, 0:1], 1.0)
            pool.memset(restart[:].rearrange("p (a b) -> p a b", b=HC)[:, :, 0:1], 0.0)
            m3 = m16[:].rearrange("p (a b) -> p a b", b=HC)
            link(pool.affine_select(out=m3, in_=m3, compare_op=ALU.is_ge, fill=0.0, base=0,
                                    pattern=[[-HC, P // HC], [0, HC]], channel_multiplier=1))
            link(pool.affine_select(out=m3, in_=m3, compare_op=ALU.is_ge, fill=0.0, base=HC - 1,
                                    pattern=[[HC, P // HC], [0, HC]], channel_multiplier=-1))
            link(pool.tensor_copy(par[:], m3[:, 0:2, 0]))
            for c in range(1, P // HC // 2):
                link(pool.tensor_tensor(par[:], par[:], m3[:, 2 * c:2 * c + 2, 0], ALU.add))
            pool.affine_select(out=m16[:], in_=m16[:], compare_op=ALU.is_ge, fill=0.0, base=0,
                               pattern=[[1, P]], channel_multiplier=-1).then_inc(sem("masks2_ready"), 1)

            for b in range(NB):
                pool.wait_ge(sem("routed"), b + 1)
                with pool.Fori(0, PH // 2) as it:
                    for o in range(2):
                        g = it * 2 + (b * PH + o)
                        pool.wait_ge(sem("row_free"), g * TOPK + 1)
                        pool.tensor_copy(idx_st[:, o, :], idx[:, b, bass.ds(it * (2 * TOPK) + o * TOPK, TOPK)]).then_inc(sem("idx_staged"), 1)
                        pool.wait_ge(sem("idx_staged"), g + 1)
                        for k in range(TOPK):
                            pool.wait_ge(sem("drow_free"), g * TOPK + (k + 1))
                            pool.sem_inc(sem("slots_granted"), 1)
                            pool.indirect_dma_start(rows_d[:, k % DSLOTS, :], None, a["peer_down"],
                                                    bass.IndirectOffsetOnAxis(ap=idx_st[:, o, k:k + 1], axis=0)).then_inc(sem(f"drow{k % DSLOTS}"), 16)
                        for k in range(TOPK):
                            pool.wait_ge(sem("row_free"), g * TOPK + (k + 1))
                            pool.sem_inc(sem("slots_granted"), 1)
                            pool.indirect_dma_start(rows_u[:, k, :], None, a["peer_up"],
                                                    bass.IndirectOffsetOnAxis(ap=idx_st[:, o, k:k + 1], axis=0)).then_inc(sem(f"urow{k}"), 16)

        def norm_act(act, k, ready, count):
            act.wait_ge(sem(ready), count)
            for b in range(NB):
                act.activation(xn[:, b, :], xres[:, b, :], ACT.Square, accum_out=ss[:, b:b + 1]).then_inc(sem("sumsq"), 1)
            act.wait_ge(sem("meansq"), k + 1)
            act.activation(sd[:], ms[:], ACT.Sqrt).then_inc(sem("root"), 1)
            for t in range(KT):
                act.wait_ge(sem("turned"), KT // 2 * k + t // 2 + 1)
                act.activation(hT[:, t, :], ps[:, t // 2, (t % 2) * S:(t % 2 + 1) * S], ACT.Copy,
                               scale=gcol[:, k, t:t + 1]).then_inc(sem("hT_ready"), 1)

        def norm_dve(dve, link, k):
            dve.wait_ge(sem("sumsq"), NB * (k + 1))
            dve.tensor_scalar(ms[:], ss[:], 1.0 / D, EPS, ALU.mult, ALU.add).then_inc(sem("meansq"), 1)
            dve.wait_ge(sem("root"), k + 1)
            link(dve.reciprocal(rr[:], sd[:]))
            for b in range(NB):
                dve.tensor_scalar(xn[:, b, :], xres[:, b, :], rr[:, b:b + 1], None, ALU.mult).then_inc(sem("xn_ready"), 1)

        def norm_pe(pe, k):
            for b in range(NB):
                pe.wait_ge(sem("xn_ready"), NB * k + b + 1)
                for t in range(KT):
                    ins = pe.transpose(ps[:, t // 2, (t % 2) * S + b * P:(t % 2) * S + (b + 1) * P],
                                       xn[:, b, t * P:(t + 1) * P], ident[:])
                    if b == NB - 1 and t % 2:
                        ins.then_inc(sem("turned"), 1)

        @block.tensor
        def _(pe):
            n_half = [0]
            n_chunk = [0]

            def begin_half(evac, first):
                h = n_half[0]
                if h - first >= 4:
                    pe.wait_ge(sem(evac), h - first - 3)
                n_half[0] += 1
                return ps[:, h % 4, :]

            def chunk_tok(src, cols, evac, done, first):
                n = n_chunk[0]
                pe.wait_ge(sem(f"w_loaded{n % SLOTS}"), loads[n])
                for b in range(NB):
                    bank = begin_half(evac, first)
                    for t in range(KT):
                        ins = pe.matmul(bank[:, 0:cols], src[:, t, b * P:(b + 1) * P], ring[:, n % SLOTS, t, 0:cols],
                                        start=(t == 0), stop=(t == KT - 1))
                    ins.then_inc(sem(done), 1)
                n_chunk[0] += 1

            def chunk_T(src, evac, done, first):
                n = n_chunk[0]
                pe.wait_ge(sem(f"w_loaded{n % SLOTS}"), loads[n])
                for g in range(2):
                    bank = begin_half(evac, first)
                    for j in range(2):
                        for t in range(KT):
                            ins = pe.matmul(bank[:, j * S:(j + 1) * S],
                                            ring[:, n % SLOTS, t, (2 * g + j) * P:(2 * g + j + 1) * P], src[:, t, :],
                                            start=(t == 0), stop=(t == KT - 1))
                    ins.then_inc(sem(done), 1)
                n_chunk[0] += 1

            pe.wait_ge(sem("ident_ready"), 1)
            norm_pe(pe, 0)
            pe.wait_ge(sem("hT_ready"), KT)
            for n in range(NW1):
                nm = chunks[n][0]
                if nm in ("aq", "kv", "mv", "mo"):
                    chunk_tok(hT, 272 if nm == "kv" else CW, "p1_evac", "p1_done", 0)
                else:
                    chunk_T(hT, "p1_evac", "p1_done", 0)

            for b in range(NB):
                pe.wait_ge(sem("qk_rotated"), b + 1)
                if b == 0:
                    pe.wait_ge(sem("p1_evac"), 2 * NW1)
                for j in range(10):
                    src = p1[:, b, j * P:(j + 1) * P] if j < 8 else kd[:, b, (j - 8) * P:(j - 7) * P]
                    ins = pe.transpose(ps[:, j // 2, (j % 2) * S + b * P:(j % 2) * S + (b + 1) * P], src, ident[:])
            ins.then_inc(sem("qk_turned"), 1)
            pe.wait_ge(sem("qkT_ready"), 1)
            g = 0
            pe.wait_ge(sem("masks_ready"), 1)
            for b in range(NB):
                nk = P * (b + 1)
                for q in range(4):
                    if g >= 1:
                        pe.wait_ge(sem("scores_read"), g)
                    for i in range(4):
                        h = 4 * q + i
                        half = (h % 2) * AD
                        pe_out = ps[:, i % 2, (i // 2) * S:(i // 2) * S + nk]
                        ins = pe.matmul(pe_out, qT[half:half + AD, h // 2, b * P:(b + 1) * P],
                                        kT[half:half + AD, h // (AH // AKV), 0:nk], start=True, stop=True)
                    ins.then_inc(sem("scores"), 1)
                    pe.wait_ge(sem("probs"), g + 1)
                    for kb in range(b + 1):
                        for i in range(4):
                            ins = pe.transpose(ps[:, 4 + kb, i * P:(i + 1) * P], sm[:, i, kb * P:(kb + 1) * P], ident[:])
                    ins.then_inc(sem("probs_turned"), 1)
                    pe.wait_ge(sem("probsT"), g + 1)
                    if g >= 1:
                        pe.wait_ge(sem("att_evac"), g)
                    kv = q // 2
                    for kb in range(b + 1):
                        v = p1[:, kb, AV0 + kv * AD:AV0 + (kv + 1) * AD]
                        for i in range(2):
                            ins = pe.matmul(ps[i * AD:(i + 1) * AD, 6 + i, 0:S],
                                            v, pt[:, kb, i::2, :], start=(kb == 0), stop=(kb == b))
                    ins.then_inc(sem("att_done"), 1)
                    g += 1

            pe.wait_ge(sem("gates_tok"), 1)
            pe.wait_ge(sem("att_evac"), 8)
            for k in range(2):
                for b in range(NB):
                    ins = pe.matmul(ps[0:MH, 0, k * S + b * P:k * S + (b + 1) * P], gt[:, k, b, :], ident[:],
                                    start=True, stop=True)
            ins.then_inc(sem("gates_turned"), 1)
            pe.wait_ge(sem("rows_ready"), 1)
            for b in range(NB):
                for k, r in enumerate((3, 5)):
                    ins = pe.matmul(ps[:, 4, (2 * k + b) * MH:(2 * k + b + 1) * MH], rows[:, r, b * P:(b + 1) * P],
                                    ident[0:MH, 0:MH], start=True, stop=True)
            for h in range(MH):
                ins = pe.matmul(ps[:, h // 2, (h % 2) * S:(h % 2 + 1) * S], sel[0:MH, h, :], rows[:, 4, :], start=True, stop=True)
            ins.then_inc(sem("m_spread"), 1)
            for h in range(MH + 1):
                if h < MH:
                    half = (h % 2) * MQ
                    if h >= 2:
                        pe.wait_ge(sem("cw_ready"), h - 1)
                    else:
                        pe.wait_ge(sem("spread_read"), 1)
                    bank = ps[:, 4 + h % 2, :]
                    pe.matmul(bank[:, 0:S], mkT[half:half + MQ, h // 2, 0:P], mqT[half:half + MQ, h // 2, :], start=True, stop=True)
                    pe.matmul(bank[:, S:S + P], mkT[half:half + MQ, h // 2, P:S], mqT[half:half + MQ, h // 2, P:S],
                              start=True, stop=True).then_inc(sem("ml_qk"), 1)
                if h >= 1:
                    g = h - 1
                    pe.wait_ge(sem("cw_ready"), g + 1)
                    if g >= 2:
                        pe.wait_ge(sem("num_evac"), g - 1)
                    bank = ps[:, 6 + g % 2, :]
                    w = MV + 1
                    pe.matmul(bank[:, 0:w], cw[:, g % 2, 0:P], mva[:, 0, g, :], start=True, stop=True)
                    pe.matmul(bank[:, w:2 * w], cw[:, g % 2, P:2 * P], mva[:, 0, g, :], start=True, stop=False)
                    pe.matmul(bank[:, w:2 * w], cw[:, g % 2, 2 * P:3 * P], mva[:, 1, g, :], start=False,
                              stop=True).then_inc(sem("num_done"), 1)
            pe.wait_ge(sem("hm_tok"), 1)
            for t in range(KT):
                for b in range(NB):
                    ins = pe.transpose(ps[:, t // 2, (t % 2) * S + b * P:(t % 2) * S + (b + 1) * P], hs[:, b, t, :], ident[:])
                if t % 2:
                    ins.then_inc(sem("hm_turned"), 1)

            pe.wait_ge(sem("hmT_ready"), KT)
            f = n_half[0]
            assert f % 4 == 2
            n_half[0] += 2
            f = n_half[0]
            for c in range(2):
                chunk_T(attT, "br_evac", "br_done", f)
            for c in range(2):
                chunk_T(hmT, "br_evac", "br_done", f)
            pe.wait_ge(sem("br_evac"), 8)
            f = n_half[0]
            for c in range(2):
                chunk_tok(mixT, CW, "x2_ready", "out_done", f)

            pe.wait_ge(sem("x2_ready"), 4)
            norm_pe(pe, 1)
            pe.wait_ge(sem("hT_ready"), 2 * KT)
            assert n_half[0] % 4 == 0
            f = n_half[0]
            for c in range(2):
                chunk_T(hT, "q_evac", "q_done", f)
            pe.wait_ge(sem("sk_loaded"), 32)
            pe.wait_ge(sem("q_evac"), 4)
            for b in range(NB):
                for h in range(PH):
                    for p in range(2):
                        r = slice(p * (P // 2), (p + 1) * (P // 2))
                        ins = pe.matmul(ps[:, 4 - 4 * b + 2 * (h // 4) + p, (h % 4) * NKEY:(h % 4 + 1) * NKEY],
                                        qpT[r, h, b * P:(b + 1) * P], sk[r, h, :], start=True, stop=True)
                ins.then_inc(sem("key_scores"), 1)
            for b in range(NB):
                pe.wait_ge(sem("scr_ready"), NB)
                acc = ps[:, 6 - 2 * b:8 - 2 * b, :]
                for c in range(2):
                    ins = pe.matmul(acc[:, c, :], ident[:], xres[:, b, c * CW:(c + 1) * CW], start=True, stop=True)
                if b == 0:
                    ins.then_inc(sem("row_free"), TOPK)
                with pe.Fori(0, PH // 2) as it:
                    for o in range(2):
                        g = it * 2 + (b * PH + o)
                        for k in range(TOPK):
                            pe.wait_ge(sem("diag_ready"), g * TOPK + (k + 1))
                            pe.wait_ge(sem(f"urow{k}"), g * 16 + 16)
                            for c in range(2):
                                ins = pe.matmul(acc[:, c, :], diag[:, k % 4, :], rows_u[:, k, c * CW:(c + 1) * CW],
                                                start=False, stop=True, skip_group_check=True)
                            ins.then_inc(sem("row_free"), 1)

            pe.wait_ge(sem("x3_ready"), NB)
            norm_pe(pe, 2)
            pe.wait_ge(sem("hT_ready"), 3 * KT)
            f = n_half[0]
            assert f % 4 == 0
            for n in range(NPEER, N2):
                if chunks[n][0] in ("sb", "hv"):
                    chunk_tok(hT, CW, "p2_evac", "p2_done", f)
                else:
                    chunk_T(hT, "p2_evac", "p2_done", f)
            pe.wait_ge(sem("sb_normed"), 1)
            pe.wait_ge(sem("p2_evac"), 2 * (N2 - NPEER))
            for j in range(8):
                for b in range(NB):
                    ins = pe.transpose(ps[:, j // 2, (j % 2) * S + b * P:(j % 2) * S + (b + 1) * P],
                                       p2[:, b, j * P:(j + 1) * P], ident[:])
            ins.then_inc(sem("sb_turned"), 1)
            pe.wait_ge(sem("sbT_ready"), 1)
            pe.wait_ge(sem("masks2_ready"), 1)
            for q in range(2):
                if q:
                    pe.wait_ge(sem("osb_evac"), q)
                for i in range(4):
                    h = 4 * q + i
                    r = slice((h % 2) * SD, (h % 2 + 1) * SD)
                    pe.matmul(ps[:, 4 + i, 0:S], qkT2[r, 4 + h // 2, 0:P], qkT2[r, h // 2, :], start=True, stop=True)
                    ins = pe.matmul(ps[:, 4 + i, S:S + P], qkT2[r, 4 + h // 2, P:S], qkT2[r, h // 2, P:S], start=True, stop=True)
                ins.then_inc(sem("z_done"), 1)
                pe.wait_ge(sem("sp_ready"), q + 1)
                for i in range(4):
                    pe.matmul(ps[:, i, 0:3 * P], tri[:], sp_[:, i, :], start=True, stop=False)
                    ins = pe.matmul(ps[:, i, P:S], ones[:], sp_[:, i, S:3 * P], start=False, stop=True)
                ins.then_inc(sem("rest_done"), 1)
                pe.wait_ge(sem("w_ready"), q + 1)
                for i in range(4):
                    h = 4 * q + i
                    o = ps[(h % 2) * SD:(h % 2 + 1) * SD, 4 + i // 2, 0:S]
                    v0 = 2 * SBW + h * SD
                    pe.matmul(o, p2[:, 0, v0:v0 + SD], wT[:, i, 0:S], start=True, stop=False)
                    ins = pe.matmul(o[:, P:S], p2[:, 1, v0:v0 + SD], wT[:, i, S:3 * P], start=False, stop=True)
                ins.then_inc(sem("osb_done"), 1)
            for j in range(HC):
                pe.wait_ge(sem("pairs_ready"), j + 1)
                if j == 0:
                    pe.wait_ge(sem("osb_evac"), 2)
                for c in range(2):
                    ins = pe.matmul(ps[:, c, :], every16[:, HC - j:HC - j + P], xbuf[:, j % 2, 2 * c:2 * c + 2, :],
                                    start=(j == 0), stop=(j == HC - 1), skip_group_check=True)
                ins.then_inc(sem("pairs_summed"), 1)
            pe.wait_ge(sem("keT_ready"), 1)
            for b in range(NB):
                for h in range(HH):
                    ins = pe.transpose(ps[:, 6 + b, h * P:(h + 1) * P], keT[:, h, b * P:(b + 1) * P], ident[:])
            ins.then_inc(sem("ke_turned"), 1)
            pe.wait_ge(sem("AT_ready"), 1)
            for b in range(NB):
                for h in range(HH):
                    pe.matmul(ps[:, 4 + b, h * P:(h + 1) * P], hv[:, b, h * P:(h + 1) * P], AT[:, h, b, :],
                              start=(h == 0), stop=True, skip_group_check=True)
            pe.wait_ge(sem("ket_ready"), 1)
            pe.wait_ge(sem("vpar_ready"), 1)
            for c in range(NHC):
                b, r0 = c // (P // HC), (c % (P // HC)) * HC
                rb = slice(r0 // 32 * 32, r0 // 32 * 32 + 32)
                if c < NHC - 1:
                    if c >= 2:
                        pe.wait_ge(sem("state_ready"), c - 1)
                    for h in range(HH):
                        ins = pe.matmul(ps[:, 2 + c % 2, h * P:(h + 1) * P], ket[rb, b, h, :], vpar[rb, c % 2, b, h * P:(h + 1) * P],
                                        start=True, stop=True)
                    ins.then_inc(sem("inc_done"), 1)
                if c >= 1:
                    pe.wait_ge(sem("state_ready"), c)
                    for h in range(HH):
                        ins = pe.matmul(ps[:, 4 + b, h * P + r0:h * P + r0 + HC], state[:, c % 3, h, :], qe[:, h, b * P + r0:b * P + r0 + HC],
                                        start=False, stop=True, skip_group_check=True)
                    ins.then_inc(sem("read_done"), 1)
            pe.wait_ge(sem("osq_ready"), 2)
            for b in range(NB):
                ins = pe.matmul(ps[:, 6 + b, :], ones[:], osq[:, :, b, :], start=True, stop=True)
            ins.then_inc(sem("osq_summed"), 1)
            pe.wait_ge(sem("ohg_ready"), 1)
            assert n_half[0] % 4 == 2
            n_half[0] += 2
            f = n_half[0]
            for c in range(2):
                n = n_chunk[0]
                pe.wait_ge(sem(f"w_loaded{n % SLOTS}"), loads[n])
                for j in range(4):
                    bank = begin_half("br2_evac", f)
                    for e, src in enumerate((osbT, ohgT)):
                        for t in range(4):
                            ins = pe.matmul(bank[:, e * S:(e + 1) * S], ring[:, n % SLOTS, 4 * e + t, j * P:(j + 1) * P], src[:, t, :],
                                            start=(t == 0), stop=(t == 3))
                    ins.then_inc(sem("br2_done"), 1)
                n_chunk[0] += 1
            pe.wait_ge(sem("br2_evac"), 8)
            f = n_half[0]
            for c in range(2):
                chunk_tok(mixT2, CW, "x4_ready", "out2_done", f)
            pe.wait_ge(sem("x4_ready"), 4)
            norm_pe(pe, 3)
            pe.wait_ge(sem("hT_ready"), 4 * KT)
            f = n_half[0]
            pend = []
            nd = 0

            def down(cs, nslot):
                for m, c in enumerate(cs):
                    pe.wait_ge(sem("hid_ready"), c + 1)
                    for j in range(2):
                        w = ring[:, nslot, :, :].rearrange("p (t c) n -> p t (c n)", c=2)[:, 2 * m + j, :]
                        for b in range(NB):
                            for e in range(2):
                                ins = pe.matmul(ps[:, 4 + 2 * b + e, :], hid[:, c % 4, j, b * P:(b + 1) * P], w[:, e * CW:(e + 1) * CW],
                                                start=(c == 0 and j == 0), stop=(c == NFF - 1 and j == 1), skip_group_check=True)
                ins.then_inc(sem("down_done"), 1)

            waiting = None
            for n in range(n_chunk[0], len(chunks)):
                if chunks[n][0] == "gate_up":
                    c = (n_half[0] - f) // 2
                    if c >= 2:
                        pe.wait_ge(sem("hid_ready"), c - 1)
                    chunk_T(hT, "none", "gu_done", n_half[0])
                else:
                    if n == len(chunks) - 1:
                        pass
                    pend.append((c, n))
                    pe.wait_ge(sem(f"w_loaded{n % SLOTS}"), loads[n])
                    down([c - 1, c] if c % 2 else [c], n % SLOTS)
                    n_chunk[0] += 1

        @block.scalar
        def _(act):
            step = [0]

            def link(ins):
                step[0] += 1
                ins.then_inc(sem("act_step"), 1)
                act.wait_ge(sem("act_step"), step[0])

            act.wait_ge(sem("small_loaded"), NSMALL * 16)
            norm_act(act, 0, "x_loaded", 16)
            act.wait_ge(sem("masks_ready"), 1)
            h = 0
            seen = {}
            for n in range(NW1):
                nm = chunks[n][0]
                c = seen.get(nm, 0)
                seen[nm] = c + 1
                for g in range(2):
                    act.wait_ge(sem("p1_done"), h + 1)
                    bank = ps[:, h % 4, :]
                    if nm == "aq":
                        ins = act.activation(p1[:, g, c * CW:(c + 1) * CW], bank, ACT.Copy)
                    elif nm == "kv":
                        ins = act.activation(p1[:, g, AK0:AK0 + 272], bank[:, 0:272], ACT.Copy)
                    elif nm in ("mq", "mk"):
                        dst = mqT if nm == "mq" else mkT
                        ins = act.activation(dst[:, 2 * g:2 * g + 2, :], bank.rearrange("p (a b) -> p a b", a=2), ACT.Copy)
                    elif nm == "mv":
                        ins = act.activation(mva[:, g, 4 * c:4 * c + 4, 0:MV], bank.rearrange("p (a b) -> p a b", a=4), ACT.Copy)
                    elif nm == "mo":
                        ins = act.activation(mo[:, g, c * CW:(c + 1) * CW], bank, ACT.Sigmoid)
                    else:
                        dst = sga if c < 2 else sgm
                        t = 4 * (c % 2) + 2 * g
                        ins = act.activation(dst[:, t:t + 2, :], bank.rearrange("p (a b) -> p a b", a=2), ACT.Sigmoid)
                    ins.then_inc(sem("p1_evac"), 1)
                    h += 1
            act.wait_ge(sem("angles"), 1)
            act.activation(cs[:], ang[:, 2:4, :, :], ACT.Sin).then_inc(sem("sines"), 1)
            for b in range(NB):
                act.wait_ge(sem("qk_ms"), b + 1)
                act.activation(hst[:, 1, :], hst[:, 0, :], ACT.Sqrt).then_inc(sem("qk_root"), 1)
            act.wait_ge(sem("qk_turned"), 1)
            for j in range(4):
                act.activation(qT[:, 2 * j:2 * j + 2, :], ps[:, j, :].rearrange("p (a b) -> p a b", a=2), ACT.Copy)
            act.activation(kT, ps[:, 4, :].rearrange("p (a b) -> p a b", a=2), ACT.Copy).then_inc(sem("qkT_ready"), 1)
            g = 0
            for b in range(NB):
                nk = P * (b + 1)
                for q in range(4):
                    act.wait_ge(sem("row_max"), g + 1)
                    for i in range(4):
                        act.activation(sm[:, i, 0:nk], sm[:, i, 0:nk], ACT.Exp, bias=am[:, 1, i:i + 1],
                                       accum_out=am[:, 2, i:i + 1])
                    act.activation(am[:, 4, :], am[:, 3, :], ACT.Exp).then_inc(sem("exps"), 1)
                    act.wait_ge(sem("probs_turned"), g + 1)
                    for kb in range(b + 1):
                        ins = act.activation(pt[:, kb, :, :], ps[:, 4 + kb, :].rearrange("p (a b) -> p a b", a=4), ACT.Copy)
                    ins.then_inc(sem("probsT"), 1)
                    act.wait_ge(sem("att_done"), g + 1)
                    for i in range(2):
                        ins = act.activation(attT[i * AD:(i + 1) * AD, 2 * q:2 * q + 2, b * P:(b + 1) * P],
                                             ps[i * AD:(i + 1) * AD, 6 + i, 0:S].rearrange("p (a b) -> p a b", a=2), ACT.Copy)
                    ins.then_inc(sem("att_evac"), 1)
                    g += 1
            act.wait_ge(sem("gates_raw"), 1)
            act.activation(gt[:, 2:4, :, :], gt[:, 0:2, :, :], ACT.Tanh, scale=1.0 / CAP).then_inc(sem("gates_tanh"), 1)
            act.wait_ge(sem("gates_cap"), 1)
            link(act.activation(gt[:, 2, :, :], gt[:, 1, :, :], ACT.Exp, scale=-1.0))
            act.activation(gt[:, 3, :, :], gt[:, 2, :, :], ACT.Ln, bias=1.0).then_inc(sem("gates_soft"), 1)
            act.wait_ge(sem("gates_turned"), 1)
            act.activation(rows[:, 0:2, :], ps[0:MH, 0, :].rearrange("p (a b) -> p a b", a=2), ACT.Copy).then_inc(sem("rows_gates"), 1)
            act.wait_ge(sem("m_rows"), 1)
            act.activation(rows[:, 5, :], rows[:, 5, :], ACT.Exp, scale=-1.0).then_inc(sem("rows_ready"), 1)
            act.wait_ge(sem("m_spread"), 1)
            act.activation(aT[:], ps[:, 4, 0:NB * MH].rearrange("p (a b) -> p a b", a=NB), ACT.Copy)
            act.activation(em[:], ps[:, 4, NB * MH:2 * NB * MH].rearrange("p (a b) -> p a b", a=NB),
                           ACT.Copy).then_inc(sem("spread_read"), 1)
            act.wait_ge(sem("spread_read"), 1)
            act.wait_ge(sem("wl_masked"), 1)
            for h in range(MH):
                act.activation(wl[:, h, 0, :], wl[:, h, 0, :], ACT.Exp, bias=aT[:, 0, h:h + 1])
                act.activation(wl[:, h, 1, :], ps[:, h // 2, (h % 2) * S + P:(h % 2 + 1) * S], ACT.Exp, bias=aT[:, 0, h:h + 1])
                ins = act.activation(wl[:, h, 2, :], wl[:, h, 2, :], ACT.Exp, bias=aT[:, 1, h:h + 1])
                ins.then_inc(sem("wl_ready"), 1)
            for h in range(MH):
                act.wait_ge(sem("num_done"), h + 1)
                act.activation(hraw[:, :, h, :], ps[:, 6 + h % 2, 0:2 * (MV + 1)].rearrange("p (a b) -> p a b", a=2),
                               ACT.Copy).then_inc(sem("num_evac"), 1)
            act.wait_ge(sem("hm_ms"), 1)
            act.activation(den[:, 2, :, :], den[:, 1, :, :], ACT.Sqrt).then_inc(sem("hm_root"), 1)
            for t in range(KT):
                act.wait_ge(sem("hm_turned"), t // 2 + 1)
                act.activation(hmT[:, t, :], ps[:, t // 2, (t % 2) * S:(t % 2 + 1) * S], ACT.Copy,
                               scale=mlgain[:, t:t + 1]).then_inc(sem("hmT_ready"), 1)

            norm_act(act, 1, "x2_ready", 4)
            h0 = 2 * NW1 + 2 + 8 + 4
            for c in range(2):
                for g in range(2):
                    act.wait_ge(sem("q_done"), 2 * c + g + 1)
                    act.activation(qpT[:, 4 * c + 2 * g:4 * c + 2 * g + 2, :], ps[:, (h0 + 2 * c + g) % 4, :].rearrange("p (a b) -> p a b", a=2),
                                   ACT.Copy).then_inc(sem("q_evac"), 1)
            act.wait_ge(sem("key_scores"), NB)
            for b in range(NB):
                for g in range(2):
                    for p in range(2):
                        ins = act.activation(scr[b][:, 4 * g:4 * g + 4, p, :], ps[:, 4 - 4 * b + 2 * g + p, :].rearrange("p (a b) -> p a b", a=4), ACT.Copy)
                ins.then_inc(sem("scr_ready"), 1)
            for b in range(NB):
                act.wait_ge(sem("best_shifted"), b + 1)
                act.activation(exf[:, 0, :], exf[:, 2, :], ACT.Exp).then_inc(sem("best_exp"), 1)
                with act.Fori(0, PH // 2) as it:
                    for o in range(2):
                        g = it * 2 + (b * PH + o)
                        act.wait_ge(sem("drow_free"), g * TOPK + (DSLOTS + TOPK))
                        act.activation(gelu[:, o, :], dots[:, o, :], ACT.Gelu).then_inc(sem("gelu_done"), 1)
                        act.wait_ge(sem("wgt_ready"), g + 1)
                        for k in range(TOPK):
                            act.wait_ge(sem("row_free"), g * TOPK + (TOPK + k - 3))
                            act.activation(diag[:, k % 4, :], ident[:], ACT.Copy, scale=wgt[:, o, k:k + 1]).then_inc(sem("diag_ready"), 1)
                act.wait_ge(sem("row_free"), TOPK + (b + 1) * PH * TOPK)
                act.activation(xres[:, b, :], ps[:, 6 - 2 * b:8 - 2 * b, :].rearrange("p a b -> p (a b)"), ACT.Copy).then_inc(sem("x3_ready"), 1)
            norm_act(act, 2, "x3_ready", NB)
            h = 0
            h0 += 4
            for n in range(NPEER, N2):
                nm = chunks[n][0]
                c = n - NPEER
                for g in range(2):
                    act.wait_ge(sem("p2_done"), h + 1)
                    bank = ps[:, (h0 + h) % 4, :]
                    bank2 = bank.rearrange("p (a b) -> p a b", a=2)
                    if nm == "sb":
                        ins = act.activation(p2[:, g, c * CW:(c + 1) * CW], bank, ACT.Copy)
                    elif nm == "hv":
                        ins = act.activation(hv[:, g, :], bank, ACT.Copy)
                    elif nm == "g2":
                        t = 4 * (c - 7) + 2 * g
                        ins = act.activation(sg2[:, t:t + 2, :], bank2, ACT.Sigmoid)
                    else:
                        dst = {"hq": hq, "hf": hf, "hg": hg}[nm]
                        ins = act.activation(dst[:, 2 * g:2 * g + 2, :], bank2, ACT.Sigmoid if nm == "hf" else ACT.Silu)
                    ins.then_inc(sem("p2_evac"), 1)
                    h += 1
            act.wait_ge(sem("sb_ms"), 1)
            for b in range(NB):
                act.wait_ge(sem("sb_ms"), b + 1)
                act.activation(hst2[:, 1, :], hst2[:, 0, :], ACT.Sqrt).then_inc(sem("sb_root"), 1)
            act.wait_ge(sem("sb_turned"), 1)
            for j in range(4):
                ins = act.activation(qkT2[:, 2 * j:2 * j + 2, :], ps[:, j, :].rearrange("p (a b) -> p a b", a=2), ACT.Copy,
                                     scale=sbgain[:, j // 2:j // 2 + 1])
            ins.then_inc(sem("sbT_ready"), 1)
            for q in range(2):
                act.wait_ge(sem("zm_ready"), q + 1)
                link(act.activation(sp_, zm, ACT.Abs))
                link(act.activation(sp_, sp_, ACT.Exp, scale=-1.0))
                act.activation(sp_, sp_, ACT.Ln, bias=1.0).then_inc(sem("sp_ln"), 1)
                act.wait_ge(sem("logw_ready"), q + 1)
                act.activation(wT, zm, ACT.Exp).then_inc(sem("w_ready"), 1)
                act.wait_ge(sem("osb_done"), q + 1)
                ins = act.activation(osbT[:, 2 * q:2 * q + 2, :], ps[:, 4:6, 0:S], ACT.Copy)
                ins.then_inc(sem("osb_evac"), 1)
            act.wait_ge(sem("lb_shifted"), 1)
            act.activation(lbs[:, 1:3, :], lbs[:, 1:3, :], ACT.Exp).then_inc(sem("lb_exp"), 1)
            act.wait_ge(sem("f_ready"), 1)
            act.activation(hf, hf, ACT.Ln).then_inc(sem("logf_ready"), 1)
            act.wait_ge(sem("bb_ready"), 1)
            act.activation(qe, bb, ACT.Exp)
            act.activation(dec[:].rearrange("p h c -> p (h c)"), bb.rearrange("p h (c r) -> p (h c) r", r=HC)[:, :, HC - 1], ACT.Exp).then_inc(sem("eb_ready"), 1)
            act.wait_ge(sem("left_ready"), 1)
            act.activation(keT, keT, ACT.Exp).then_inc(sem("eleft_ready"), 1)
            x4 = [xbuf[:, i, :, :].rearrange("p h (c r) -> p (h c) r", r=HC) for i in range(2)]
            for j in range(HC):
                act.wait_ge(sem("diff_ready"), j + 1)
                act.activation(x4[j % 2][:, :, j:HC], x4[j % 2][:, :, j:HC], ACT.Exp).then_inc(sem("diff_exp"), 1)
            act.wait_ge(sem("ke_turned"), 1)
            for b in range(NB):
                ins = act.activation(ket[:, b, :, :], ps[:, 6 + b, :].rearrange("p (a b) -> p a b", a=HH), ACT.Copy)
            ins.then_inc(sem("ket_ready"), 1)
            act.wait_ge(sem("read_done"), NHC - 1)
            for b in range(NB):
                act.activation(osq[:, :, b, :], ps[:, 4 + b, :].rearrange("p (a b) -> p a b", a=HH), ACT.Square).then_inc(sem("osq_ready"), 1)
            act.wait_ge(sem("oms_ready"), 2)
            act.activation(orr, orr, ACT.Sqrt).then_inc(sem("oroot"), 1)
            norm_act(act, 3, "x4_ready", 4)
            h0 = h0 + 22 + 2 + 8 + 4
            for c in range(NFF):
                act.wait_ge(sem("gu_done"), 2 * c + 1)
                if c >= 2:
                    act.wait_ge(sem("hid_ready"), c - 1)
                act.activation(silu[:, c % 2, :, :], ps[:, (h0 + 2 * c) % 4, :].rearrange("p (a b) -> p a b", a=2), ACT.Silu).then_inc(sem("silu_ready"), 1)

        @block.vector
        def _(dve):
            step = [0]

            def link(ins):
                step[0] += 1
                ins.then_inc(sem("dve_step"), 1)
                dve.wait_ge(sem("dve_step"), step[0])

            norm_dve(dve, link, 0)
            dve.wait_ge(sem("small_loaded"), NSMALL * 16)
            link(dve.tensor_copy(posf[:], pos_i[:]))
            for b in range(NB):
                link(dve.tensor_scalar(ang[:, 0, b, :], freq[:], posf[:, b:b + 1], None, ALU.mult))
            flat = [ang[:, k, :, :].rearrange("p a b -> p (a b)") for k in range(4)]
            link(dve.tensor_scalar(flat[1], flat[0], 1.0 / (2 * np.pi), MAGIC, ALU.mult, ALU.add))
            link(dve.tensor_scalar(flat[1], flat[1], MAGIC, None, ALU.subtract))
            for part in TWO_PI_PARTS:
                link(dve.scalar_tensor_tensor(out=flat[0], in0=flat[1], scalar=-part, in1=flat[0], op0=ALU.mult, op1=ALU.add))
            link(dve.tensor_scalar(flat[1], flat[0], np.pi / 2, None, ALU.add))
            link(dve.tensor_scalar(flat[2], flat[1], np.pi, -2 * np.pi, ALU.is_gt, ALU.mult))
            link(dve.tensor_tensor(flat[1], flat[1], flat[2], ALU.add))
            link(dve.tensor_scalar(flat[2], flat[1], PI_IN, -PI_IN, ALU.min, ALU.max))
            dve.tensor_scalar(flat[3], flat[0], PI_IN, -PI_IN, ALU.min, ALU.max).then_inc(sem("angles"), 1)
            dve.wait_ge(sem("p1_evac"), 6)
            NH = AH + AKV
            for b in range(NB):
                qk = p1[:, b, 0:NH * AD]
                qk3 = qk.rearrange("p (h d) -> p h d", d=AD)
                sq3 = sq.rearrange("p (h d) -> p h d", d=AD)
                link(dve.tensor_tensor(sq, qk, qk, ALU.mult))
                link(dve.tensor_reduce(hst[:, 0, :], sq3, AX, ALU.add))
                dve.tensor_scalar(hst[:, 0, :], hst[:, 0, :], 1.0 / AD, EPS, ALU.mult, ALU.add).then_inc(sem("qk_ms"), 1)
                dve.wait_ge(sem("qk_root"), b + 1)
                link(dve.reciprocal(hst[:, 2, :], hst[:, 1, :]))
                link(dve.tensor_tensor(qk3, qk3, hst[:, 2, :].unsqueeze(2).broadcast_to([P, NH, AD]), ALU.mult))
                dve.tensor_tensor(qk3[:, 0:AH, :], qk3[:, 0:AH, :], qkgain[:, 0:1, :].broadcast_to([P, AH, AD]), ALU.mult)
                link(dve.tensor_tensor(qk3[:, AH:NH, :], qk3[:, AH:NH, :], qkgain[:, 1:2, :].broadcast_to([P, AKV, AD]), ALU.mult))
                if b == 0:
                    dve.wait_ge(sem("sines"), 1)
                x1, x2 = qk3[:, :, 0:RH], qk3[:, :, RH:ROPE]
                co = cs[:, 0, b:b + 1, :].broadcast_to([P, NH, RH])
                si = cs[:, 1, b:b + 1, :].broadcast_to([P, NH, RH])
                dve.tensor_tensor(rt[:, 0, :, :], x1, co, ALU.mult)
                dve.tensor_tensor(rt[:, 1, :, :], x2, si, ALU.mult)
                dve.tensor_tensor(rt[:, 2, :, :], x2, co, ALU.mult)
                link(dve.tensor_tensor(rt[:, 3, :, :], x1, si, ALU.mult))
                dve.tensor_tensor(x1, rt[:, 0, :, :], rt[:, 1, :, :], ALU.subtract)
                link(dve.tensor_tensor(x2, rt[:, 2, :, :], rt[:, 3, :, :], ALU.add))
                kk = p1[:, b, AK0:AV0].rearrange("p (h d) -> p h d", d=AD)
                kdv = kd[:, b, :].rearrange("p (h two d) -> p h two d", two=2, d=AD)
                dve.tensor_copy(kdv[:, :, 0, :], kk)
                dve.tensor_copy(kdv[:, :, 1, :], kk).then_inc(sem("qk_rotated"), 1)
            g = 0
            for b in range(NB):
                nk = P * (b + 1)
                m3 = mask_band[:, 1 - b:2, :].rearrange("p a b -> p (a b)").unsqueeze(1)
                for q in range(4):
                    dve.wait_ge(sem("scores"), g + 1)
                    if g >= 1:
                        dve.wait_ge(sem("probs_turned"), g)
                    for i in range(2):
                        ins = dve.scalar_tensor_tensor(out=sm[:, i::2, 0:nk],
                                                 in0=ps[:, i, :].rearrange("p (a b) -> p a b", a=2)[:, :, 0:nk], scalar=AD ** -0.5,
                                                 in1=m3.broadcast_to([P, 2, nk]), op0=ALU.mult, op1=ALU.add)
                    ins.then_inc(sem("scores_read"), 1)
                    dve.wait_ge(sem("scores_read"), g + 1)
                    link(dve.tensor_reduce(am[:, 0, :], sm[:, :, 0:nk], AX, ALU.max))
                    snk = sinks[:, 4 * q:4 * q + 4]
                    link(dve.tensor_tensor(am[:, 0, :], am[:, 0, :], snk, ALU.max))
                    dve.tensor_scalar(am[:, 1, :], am[:, 0, :], -1.0, None, ALU.mult)
                    dve.tensor_tensor(am[:, 3, :], snk, am[:, 0, :], ALU.subtract).then_inc(sem("row_max"), 1)
                    dve.wait_ge(sem("exps"), g + 1)
                    link(dve.tensor_tensor(am[:, 5, :], am[:, 2, :], am[:, 4, :], ALU.add))
                    link(dve.reciprocal(am[:, 0, :], am[:, 5, :]))
                    dve.tensor_tensor(sm[:, :, 0:nk], sm[:, :, 0:nk], am[:, 0, :].unsqueeze(2).broadcast_to([P, 4, nk]),
                                      ALU.mult).then_inc(sem("probs"), 1)
                    g += 1
            mif = p1[:, :, AV0 + AKV * AD:AV0 + AKV * AD + 2 * MH]
            for k in range(2):
                ins = dve.tensor_tensor(gt[:, k, :, :], mif[:, :, k * MH:(k + 1) * MH], ifbias[:, k:k + 1, :].broadcast_to([P, NB, MH]), ALU.add)
            ins.then_inc(sem("gates_raw"), 1)
            dve.wait_ge(sem("gates_tanh"), 1)
            dve.tensor_scalar(gt[:, 0:2, :, :], gt[:, 2:4, :, :], CAP, None, ALU.mult).then_inc(sem("gates_cap"), 1)
            dve.wait_ge(sem("gates_soft"), 1)
            dve.tensor_scalar(gt[:, 1, :, :], gt[:, 3, :, :], -1.0, None, ALU.mult).then_inc(sem("gates_tok"), 1)
            dve.wait_ge(sem("rows_gates"), 1)
            link(dve.tensor_tensor_scan(rows[:, 2, :], ones[0:MH, 0:1].broadcast_to([MH, S]), rows[:, 1, :], 0.0, ALU.mult, ALU.add))
            link(dve.tensor_tensor(rows[:, 3, :], rows[:, 0, :], rows[:, 2, :], ALU.subtract))
            link(dve.tensor_tensor_scan(rows[:, 4, :], rows[:, 3, :], rows[:, 3, :], 0.0, ALU.max, ALU.max))
            link(dve.tensor_tensor(rows[:, 5, :], rows[:, 2, :], rows[:, 4, :], ALU.add))
            dve.tensor_scalar(rows[:, 4, :], rows[:, 4, :], -1.0, None, ALU.mult).then_inc(sem("m_rows"), 1)
            dve.wait_ge(sem("m_spread"), 1)
            mi3 = mask_inc[:].unsqueeze(1)
            for j in range(4):
                bank = ps[:, j, :].rearrange("p (h b c) -> p h b c", h=2, b=2)
                dve.tensor_tensor(wl[:, 2 * j:2 * j + 2, 0, :], bank[:, :, 0, :], mi3.broadcast_to([P, 2, P]), ALU.add)
                ins = dve.tensor_tensor(wl[:, 2 * j:2 * j + 2, 2, :], bank[:, :, 1, :], mi3.broadcast_to([P, 2, P]), ALU.add)
            ins.then_inc(sem("wl_masked"), 1)
            for h in range(MH):
                dve.wait_ge(sem("wl_ready"), h + 1)
                dve.wait_ge(sem("ml_qk"), h + 1)
                if h >= 2:
                    dve.wait_ge(sem("num_done"), h - 1)
                dve.scalar_tensor_tensor(out=cw[:, h % 2, :], in0=ps[:, 4 + h % 2, 0:3 * P], scalar=MQ ** -0.5,
                                         in1=wl[:, h, :, :].rearrange("p a b -> p (a b)"), op0=ALU.mult,
                                         op1=ALU.mult).then_inc(sem("cw_ready"), 1)
            dve.wait_ge(sem("num_evac"), MH)
            dn = hraw[:, :, :, MV]
            link(dve.scalar_tensor_tensor(out=den[:, 0, :, :], in0=dn, scalar=-1.0, in1=dn, op0=ALU.mult, op1=ALU.max))
            link(dve.tensor_tensor(den[:, 0, :, :], den[:, 0, :, :], em[:], ALU.max))
            link(dve.reciprocal(den[:, 1, :, :], den[:, 0, :, :]))
            for b in range(NB):
                link(dve.tensor_tensor(hs[:, b, :, :], hraw[:, b, :, 0:MV], den[:, 1, b, :].unsqueeze(2).broadcast_to([P, MH, MV]), ALU.mult))
            link(dve.tensor_tensor(hsq, hs, hs, ALU.mult))
            link(dve.tensor_reduce(den[:, 0, :, :], hsq, AX, ALU.add))
            dve.tensor_scalar(den[:, 1, :, :], den[:, 0, :, :], 1.0 / MV, EPS, ALU.mult, ALU.add).then_inc(sem("hm_ms"), 1)
            dve.wait_ge(sem("hm_root"), 1)
            link(dve.reciprocal(den[:, 0, :, :], den[:, 2, :, :]))
            for b in range(NB):
                link(dve.tensor_tensor(hs[:, b, :, :], hs[:, b, :, :], den[:, 0, b, :].unsqueeze(2).broadcast_to([P, MH, MV]), ALU.mult))
            dve.tensor_tensor(hs, hs, mo.rearrange("p b (h v) -> p b h v", h=MH), ALU.mult).then_inc(sem("hm_tok"), 1)
            f = 2 * NW1 + 2
            for k in range(4):
                dve.wait_ge(sem("br_done"), k + 1)
                dve.tensor_tensor(mixT[:, 2 * k:2 * k + 2, :], ps[:, (f + k) % 4, :].rearrange("p (a b) -> p a b", a=2),
                                  sga[:, 2 * k:2 * k + 2, :], ALU.mult).then_inc(sem("br_evac"), 1)
            for k in range(4):
                dve.wait_ge(sem("br_done"), 4 + k + 1)
                link(dve.tensor_tensor(tmpT[:, 2 * k:2 * k + 2, :], ps[:, (f + k) % 4, :].rearrange("p (a b) -> p a b", a=2),
                                       sgm[:, 2 * k:2 * k + 2, :], ALU.mult))
                dve.tensor_tensor(mixT[:, 2 * k:2 * k + 2, :], mixT[:, 2 * k:2 * k + 2, :], tmpT[:, 2 * k:2 * k + 2, :],
                                  ALU.add).then_inc(sem("br_evac"), 1)
            f = f + 8
            for c in range(2):
                for b in range(NB):
                    dve.wait_ge(sem("out_done"), 2 * c + b + 1)
                    dve.tensor_tensor(xres[:, b, c * CW:(c + 1) * CW], xres[:, b, c * CW:(c + 1) * CW],
                                      ps[:, (f + 2 * c + b) % 4, :], ALU.add).then_inc(sem("x2_ready"), 1)

            norm_dve(dve, link, 1)
            dve.wait_ge(sem("sk_loaded"), 32)
            dve.wait_ge(sem("xn_ready"), 2 * NB)
            for b in range(NB):
                ins = dve.tensor_tensor(h2[:, b, :], xn[:, b, :], n2row, ALU.mult)
            link(ins)

            def top16(values, vals, where, rows):
                for half in range(2):
                    e = slice(8 * half, 8 * half + 8)
                    for r in range(rows):
                        ins = dve.max(vals[r][:, e], values[r])
                    link(ins)
                    for r in range(rows):
                        ins = dve.max_index(where[r][:, e], vals[r][:, e], values[r])
                    link(ins)
                    if half == 0:
                        for r in range(rows):
                            ins = dve.match_replace(values[r], vals[r][:, e], values[r], -3.0e38)
                        link(ins)

            def route(b):
                dve.wait_ge(sem("scr_ready"), NB)
                dve.wait_ge(sem("masks2_ready"), 1)
                hp = [(h, p) for h in range(PH) for p in range(2)]
                top16([scr[b][:, h, p, :] for h, p in hp], [tv[:, h, p, :] for h, p in hp], [ti[:, h, p, :] for h, p in hp], len(hp))
                flat = "p a b c -> p (a b c)"
                link(dve.tensor_copy(tif.rearrange(flat), ti.rearrange(flat)))
                cand = scr[b].rearrange("p h q k -> p h (q k)")
                c4 = cand.rearrange("p h (i j) -> p h i j", i=TOPK)
                link(dve.tensor_tensor(c4, tv[:, :, 0, :].unsqueeze(3).broadcast_to([P, PH, TOPK, TOPK]),
                                       tv[:, :, 1, :].unsqueeze(2).broadcast_to([P, PH, TOPK, TOPK]), ALU.add))
                top16([cand[:, h, :] for h in range(PH)], [bv[:, h, :] for h in range(PH)], [bp[:, h, :] for h in range(PH)], PH)
                bpf = bp.rearrange("p a b -> p (a b)")
                dve.tensor_scalar(bij[:, 0, :], bpf, 4, None, ALU.logical_shift_right)
                link(dve.tensor_scalar(bij[:, 1, :], bpf, TOPK - 1, None, ALU.bitwise_and))
                link(dve.tensor_copy(bijf.rearrange("p a b -> p (a b)"), bij.rearrange("p a b -> p (a b)")))
                for p in range(2):
                    hot3 = hot.rearrange("p h k i -> p (h k) i")
                    link(dve.tensor_tensor(hot3, bijf[:, p, :].unsqueeze(2).broadcast_to([P, PH * TOPK, TOPK]),
                                           iota16[:].unsqueeze(1).broadcast_to([P, PH * TOPK, TOPK]), ALU.is_equal))
                    link(dve.tensor_tensor(picked, hot, tif[:, :, p, :].unsqueeze(2).broadcast_to([P, PH, TOPK, TOPK]), ALU.mult))
                    link(dve.tensor_reduce(exf[:, p, :], picked.rearrange("p h k i -> p (h k) i"), AX, ALU.add))
                link(dve.scalar_tensor_tensor(out=exf[:, 2, :], in0=exf[:, 0, :], scalar=float(NKEY), in1=exf[:, 1, :], op0=ALU.mult, op1=ALU.add))
                link(dve.tensor_copy(idx[:, b, :], exf[:, 2, :]))
                e3 = exf.rearrange("p a (h k) -> p a h k", h=PH)
                dve.tensor_tensor(e3[:, 2, :, :], bv, bv[:, :, 0:1].broadcast_to([P, PH, TOPK]), ALU.subtract).then_inc(sem("best_shifted"), 1)
                dve.wait_ge(sem("best_exp"), b + 1)
                link(dve.tensor_reduce(gsum[:, 0, :], e3[:, 0, :, :], AX, ALU.add))
                link(dve.reciprocal(gsum[:, 1, :], gsum[:, 0, :]))
                dve.tensor_tensor(gate[:, b, :].rearrange("p (h k) -> p h k", h=PH), e3[:, 0, :, :],
                                  gsum[:, 1, :].unsqueeze(2).broadcast_to([P, PH, TOPK]), ALU.mult).then_inc(sem("routed"), 1)
                dve.wait_ge(sem("routed"), b + 1)

            for b in range(NB):
                route(b)
                if b == 0:
                    dve.memset(dots[:], 0.0).then_inc(sem("drow_free"), DSLOTS)
                    dve.wait_ge(sem("drow_free"), DSLOTS)
                with dve.Fori(0, PH // 2) as it:
                    for o in range(2):
                        g = it * 2 + (b * PH + o)
                        for k in range(TOPK):
                            dve.wait_ge(sem(f"drow{k % DSLOTS}"), g * 32 + (16 + 16 * (k // DSLOTS)))
                            row = rows_d[:, k % DSLOTS, :]
                            dve.tensor_tensor_reduce(row, row, h2[:, b, :], 1.0, 0.0, ALU.mult, ALU.add,
                                                     dots[:, o, k:k + 1]).then_inc(sem("drow_free"), 1)
                        dve.wait_ge(sem("gelu_done"), g + 1)
                        dve.tensor_tensor(wgt[:, o, :], gelu[:, o, :], gate[:, b, bass.ds(it * (2 * TOPK) + o * TOPK, TOPK)],
                                          ALU.mult).then_inc(sem("wgt_ready"), 1)

            norm_dve(dve, link, 2)
            link(dve.tensor_tensor(lbs[:, 0, :], lbt[:, 0, :], lbt[:, 1, :], ALU.max))
            dve.tensor_tensor(lbs[:, 1:3, :], lbt[:], lbs[:, 0:1, :].broadcast_to([P, 2, HH]), ALU.subtract).then_inc(sem("lb_shifted"), 1)
            dve.wait_ge(sem("p2_evac"), 6)
            for b in range(NB):
                qk = p2[:, b, 0:2 * SBW]
                qk3 = qk.rearrange("p (h d) -> p h d", d=SD)
                sqs = zm.rearrange("p a b -> p (a b)")[:, 0:2 * SBW]
                link(dve.tensor_tensor(sqs, qk, qk, ALU.mult))
                link(dve.tensor_reduce(hst2[:, 0, :], sqs.rearrange("p (h d) -> p h d", d=SD), AX, ALU.add))
                dve.tensor_scalar(hst2[:, 0, :], hst2[:, 0, :], 1.0 / SD, EPS, ALU.mult, ALU.add).then_inc(sem("sb_ms"), 1)
                dve.wait_ge(sem("sb_root"), b + 1)
                link(dve.reciprocal(hst2[:, 2, :], hst2[:, 1, :]))
                ins = dve.tensor_tensor(qk3, qk3, hst2[:, 2, :].unsqueeze(2).broadcast_to([P, 2 * SH, SD]), ALU.mult)
                if b == 0:
                    link(ins)
                else:
                    ins.then_inc(sem("sb_normed"), 1)
            ms3 = mask_str[:].unsqueeze(1).broadcast_to([P, 4, P])
            for q in range(2):
                dve.wait_ge(sem("z_done"), q + 1)
                if q:
                    dve.wait_ge(sem("w_ready"), q)
                sc = SD ** -0.5
                for c0 in (0, S):
                    dve.scalar_tensor_tensor(out=zm[:, :, c0:c0 + P], in0=ps[:, 4:8, c0:c0 + P], scalar=sc, in1=ms3, op0=ALU.mult, op1=ALU.add)
                dve.tensor_scalar(zm[:, :, P:S], ps[:, 4:8, P:S], sc, None, ALU.mult).then_inc(sem("zm_ready"), 1)
                dve.wait_ge(sem("sp_ln"), q + 1)
                fz = "p a b -> p (a b)"
                dve.scalar_tensor_tensor(out=sp_.rearrange(fz), in0=zm.rearrange(fz), scalar=0.0, in1=sp_.rearrange(fz), op0=ALU.max, op1=ALU.add).then_inc(sem("sp_ready"), 1)
                dve.wait_ge(sem("rest_done"), q + 1)
                dve.tensor_tensor(zm, zm, ps[:, 0:4, 0:3 * P], ALU.subtract).then_inc(sem("logw_ready"), 1)
            dve.wait_ge(sem("lb_exp"), 1)
            link(dve.tensor_tensor(lbs[:, 3, :], lbs[:, 1, :], lbs[:, 2, :], ALU.add))
            link(dve.reciprocal(lbs[:, 4, :], lbs[:, 3, :]))
            link(dve.tensor_tensor(lbs[:, 0, :], lbs[:, 1, :], lbs[:, 4, :], ALU.mult))
            link(dve.tensor_scalar(lbs[:, 3, :], lbs[:, 0, :], -1.0, 1.0, ALU.mult, ALU.add))
            dve.wait_ge(sem("osb_done"), 2)
            for h in range(HH):
                ins = dve.tensor_scalar(hf[:, h, :], hf[:, h, :], lbs[:, 3, h:h + 1], lbs[:, 0, h:h + 1], ALU.mult, ALU.add)
            link(ins)
            fl = "p a b -> p (a b)"
            dve.tensor_scalar(key.rearrange(fl), hf.rearrange(fl), -1.0, 1.0, ALU.mult, ALU.add).then_inc(sem("f_ready"), 1)
            for o in range(2):
                ins = dve.tensor_scalar(vpar[:, o, :, :].rearrange(fl), hv.rearrange(fl), par[:, o:o + 1], None, ALU.mult)
            ins.then_inc(sem("vpar_ready"), 1)
            dve.memset(xn[:], 0.0)
            dve.wait_ge(sem("logf_ready"), 1)
            dve.tensor_tensor_scan(bb.rearrange(fl), restart[:], hf.rearrange(fl), 0.0, ALU.mult, ALU.add).then_inc(sem("bb_ready"), 1)
            dve.wait_ge(sem("bb_ready"), 1)
            b4 = bb.rearrange("p h (c r) -> p (h c) r", r=HC)
            k4 = keT.rearrange("p h (c r) -> p (h c) r", r=HC)
            key4 = key.rearrange("p h (c r) -> p (h c) r", r=HC)
            q4 = hq.rearrange("p h (c r) -> p (h c) r", r=HC)
            dve.tensor_tensor(k4, b4[:, :, HC - 1:HC].broadcast_to([P, HH * NHC, HC]), b4, ALU.subtract).then_inc(sem("left_ready"), 1)
            dve.wait_ge(sem("eb_ready"), 1)
            dve.tensor_tensor(qe, qe, hq, ALU.mult)
            dve.wait_ge(sem("eleft_ready"), 1)
            dve.tensor_tensor(keT, keT, key, ALU.mult).then_inc(sem("keT_ready"), 1)
            x4 = [xbuf[:, i, :, :].rearrange("p h (c r) -> p (h c) r", r=HC) for i in range(2)]

            def diff(j):
                if j >= 2:
                    dve.wait_ge(sem("pairs_summed"), j - 1)
                dve.tensor_tensor(x4[j % 2][:, :, j:HC], b4[:, :, j:HC], b4[:, :, j:j + 1].broadcast_to([P, HH * NHC, HC - j]),
                                  ALU.subtract).then_inc(sem("diff_ready"), 1)

            diff(0)
            for j in range(HC):
                if j + 1 < HC:
                    diff(j + 1)
                x = x4[j % 2][:, :, j:HC]
                dve.wait_ge(sem("diff_exp"), j + 1)
                link(dve.tensor_tensor(x, x, q4[:, :, j:HC], ALU.mult))
                dve.tensor_tensor(x, x, key4[:, :, j:j + 1].broadcast_to([P, HH * NHC, HC - j]), ALU.mult).then_inc(sem("pairs_ready"), 1)
            dve.wait_ge(sem("pairs_summed"), HC)
            for c in range(2):
                ins = dve.tensor_tensor(AT[:, 2 * c:2 * c + 2, :, :].rearrange("p h b t -> p (h b) t"), ps[:, c, :].rearrange("p (a b) -> p a b", b=P),
                                        m16[:].unsqueeze(1).broadcast_to([P, 4, P]), ALU.mult)
            ins.then_inc(sem("AT_ready"), 1)
            for c in range(NHC - 1):
                dve.wait_ge(sem("inc_done"), c + 1)
                if c >= 3:
                    dve.wait_ge(sem("read_done"), c - 2)
                for h in range(HH):
                    new = state[:, (c + 1) % 3, h, :]
                    inc = ps[:, 2 + c % 2, h * P:(h + 1) * P]
                    if c == 0:
                        ins = dve.tensor_copy(new, inc)
                    else:
                        ins = dve.scalar_tensor_tensor(out=new, in0=state[:, c % 3, h, :], scalar=dec[:, h, c:c + 1], in1=inc, op0=ALU.mult, op1=ALU.add)
                ins.then_inc(sem("state_ready"), 1)
                dve.wait_ge(sem("state_ready"), c + 1)
            dve.wait_ge(sem("osq_summed"), 1)
            for b in range(NB):
                dve.tensor_scalar(orr[:, :, b, :], ps[:, 6 + b, :].rearrange("p (a b) -> p a b", a=HH), 1.0 / HV, EPS, ALU.mult, ALU.add).then_inc(sem("oms_ready"), 1)
            dve.wait_ge(sem("oroot"), 1)
            link(dve.reciprocal(orr, orr))
            for b in range(NB):
                ins = dve.scalar_tensor_tensor(out=ohgT[:, :, b * P:(b + 1) * P], in0=ps[:, 4 + b, :].rearrange("p (a b) -> p a b", a=HH), scalar=hgain[:, 0:1],
                                               in1=orr[:, :, b, :], op0=ALU.mult, op1=ALU.mult)
            link(ins)
            dve.tensor_tensor(ohgT, ohgT, hg, ALU.mult).then_inc(sem("ohg_ready"), 1)
            f = f + 4 + 4 + 22 + 2
            for k in range(8):
                dve.wait_ge(sem("br2_done"), k + 1)
                bank = ps[:, (f + k) % 4, :]
                dve.tensor_tensor(mixT2[:, k, :], bank[:, 0:S], sg2[:, k, :], ALU.mult)
                link(dve.tensor_tensor(tmp2[:, 0, :], bank[:, S:2 * S], sg2[:, KT + k, :], ALU.mult))
                dve.tensor_tensor(mixT2[:, k, :], mixT2[:, k, :], tmp2[:, 0, :], ALU.add).then_inc(sem("br2_evac"), 1)
                dve.wait_ge(sem("br2_evac"), k + 1)
            f += 8
            for c in range(2):
                for b in range(NB):
                    dve.wait_ge(sem("out2_done"), 2 * c + b + 1)
                    dve.tensor_tensor(xres[:, b, c * CW:(c + 1) * CW], xres[:, b, c * CW:(c + 1) * CW],
                                      ps[:, (f + 2 * c + b) % 4, :], ALU.add).then_inc(sem("x4_ready"), 1)
            norm_dve(dve, link, 3)
            f += 4
            for c in range(NFF):
                dve.wait_ge(sem("gu_done"), 2 * c + 2)
                dve.wait_ge(sem("silu_ready"), c + 1)
                if c >= 4:
                    dve.wait_ge(sem("down_done"), (c - 4) // 2 + 1)
                dve.tensor_tensor(hid[:, c % 4, :, :], silu[:, c % 2, :, :], ps[:, (f + 2 * c + 1) % 4, :].rearrange("p (a b) -> p a b", a=2),
                                  ALU.mult).then_inc(sem("hid_ready"), 1)
            dve.wait_ge(sem("down_done"), (NFF + 1) // 2)
            for b in range(NB):
                for c in range(2):
                    dve.tensor_tensor(xres[:, b, c * CW:(c + 1) * CW], xres[:, b, c * CW:(c + 1) * CW],
                                      ps[:, 4 + 2 * b + c, :], ALU.add).then_inc(sem("x5_ready"), 1)


def lay_out(inp):
    c = np.ascontiguousarray
    f = lambda k: np.asarray(inp[k])
    col = lambda v: v.reshape(KT, P).T
    rep = lambda v: np.broadcast_to(v, (P,) + v.shape)
    return {
        "x": c(f("x")[0]),
        "w_in": c(f("w_in")[0]),
        "w_branch_attn": c(f("w_branch_attn")[0]),
        "w_branch_mlstm": c(f("w_branch_mlstm")[0]),
        "w_out": c(f("w_out")[0]),
        "gcol": c(np.stack([col(f(k)[0]) for k in ("norm1_gain", "norm2_gain", "norm1_g_2", "norm2_g_2")], 1)),
        "mlgain": c(col(f("ml_out_norm_gain")[0])),
        "qkgain": c(rep(np.stack([f("q_norm_gain")[0], f("k_norm_gain")[0]]))),
        "sinks": c(rep(f("attn_sinks")[0])),
        "ifbias": c(rep(np.stack([f("ml_i_bias")[0], f("ml_f_bias")[0]]))),
        "pos": c(f("positions").reshape(NB, P).T.astype(np.int32)),
        "freq": c(rep(inv_freq())),
        "peer_w_query": c(f("peer_w_query")[0]),
        "sub_keys": c(f("peer_sub_keys")[0].transpose(1, 3, 0, 2).reshape(P, PH, NKEY)),
        "n2row": c(rep(f("norm2_gain")[0])),
        "peer_down": c(f("peer_down")[0]),
        "peer_up": c(f("peer_up")[0]),
        "w_in_2": c(f("w_in_2")[0]),
        "w_branch_2": c(f("w_branch_2")[0]),
        "w_out_2": c(f("w_out_2")[0]),
        "w_ffn_gate_2": c(f("w_ffn_gate_2")[0]),
        "w_ffn_up_2": c(f("w_ffn_up_2")[0]),
        "w_ffn_down_2": c(f("w_ffn_down_2")[0]),
        "sbgain": c(np.stack([np.tile(f(k)[0], 2) for k in ("q_norm_g_2", "k_norm_g_2")], 1)),
        "hgain": c(f("hg_norm_g_2")[0].reshape(P, 1)),
        "lbt": c(f("lb_table_2").reshape(2, HH, HK).transpose(2, 0, 1)),
    }


def kernel(**inputs):
    import concourse.bacc as bacc
    from concourse.bass_utils import run_bass_kernel_spmd

    nc = bacc.Bacc("TRN2", target_bir_lowering=False, num_devices=1)
    arrays = lay_out(inputs)
    aps = {k: nc.dram_tensor(k + "_in", v.shape, mybir.dt.from_np(v.dtype), kind="ExternalInput").ap() for k, v in arrays.items()}
    out = nc.dram_tensor("out", (S, D), F32, kind="ExternalOutput").ap()
    build(nc, aps, out)
    r = run_bass_kernel_spmd(nc, [{k + "_in": v for k, v in arrays.items()}], core_ids=[0])
    return r.results[0]["out"].reshape(1, S, D)
```

```python
from contextlib import ExitStack

import numpy as np
import concourse.bass as bass
from concourse import mybir

F32 = mybir.dt.float32
R32 = mybir.dt.float32r
U32 = mybir.dt.uint32
I32 = mybir.dt.int32
ALU = mybir.AluOpType
ACT = mybir.ActivationFunctionType
AX = mybir.AxisListType.X

P = 128
S = 256
NB = S // P
D = 1024
KT = D // P
EPS = 1e-6
NEG = -1e30

AH, AKV, AD = 16, 2, 64
ROPE = AD // 4
RH = ROPE // 2
ROPE_THETA = 500000.0
MH, MQ, MV = 8, 64, 128
CAP = 15.0
PH, NKEY, TOPK = 8, 128, 16
PR = 2
NR = PH // PR
AQ0 = 0
AK0 = AQ0 + AH * AD
AV0 = AK0 + AKV * AD
MQ0 = AV0 + AKV * AD
MK0 = MQ0 + MH * MQ
MV0 = MK0 + MH * MQ
MI0 = MV0 + MH * MV
MF0 = MI0 + MH
MO0 = MF0 + MH
GA0 = MO0 + MH * MV
GM0 = GA0 + D
W1N = GM0 + D

SH, SD = 8, 64
HH, HK, HV = 4, 128, 128
HC = 16
NHC = S // HC
SBW = SH * SD
HGW = HH * HV
FF = -(-8 * D // (3 * 256)) * 256
W2N = 3 * SBW + 2 * HH * HK + 2 * HGW + 2 * D

CW = 512
DSLOTS = 8
HC2 = CW // 2
SLOTS = 2
KU = KT // 2

TWO_PI_PARTS = (6.28125, 0.0019352436065673828, 6.357301884918343e-08)
MAGIC = 12582912.0
PI_IN = 3.1415925


def inv_freq():
    return (np.float32(ROPE_THETA) ** (-np.arange(0, ROPE, 2, dtype=np.float32) / np.float32(ROPE))).astype(np.float32)


def build(nc, a, out):
    ctx = ExitStack()
    with ctx:
        def sb(name, shape, dt=F32):
            return ctx.enter_context(nc.sbuf_tensor(name, shape, dt))

        made = {}

        def sem(name):
            if name not in made:
                made[name] = ctx.enter_context(nc.semaphore(name))
            return made[name]

        NSMALL = 10
        with ExitStack() as shared:
            rows_u = shared.enter_context(nc.sbuf_tensor("rows_u", [P, TOPK, D], F32))
        ring = sb("ring", [P, SLOTS, KT, CW])
        w_hi = sb("w_hi", [P, 2, KT, HC2], R32)
        w_lo = sb("w_lo", [P, 2, KT, HC2], R32)
        xres = sb("xres", [P, NB, D])
        with ExitStack() as shared:
            xn = shared.enter_context(nc.sbuf_tensor("xn", [P, NB, D], F32))
        hT_lo = sb("hT_lo", [P, KT, S], R32)
        hT_hi = sb("hT_hi", [P, KT, S], R32)
        arena = sb("arena", [P, 23808])
        ps = ctx.enter_context(nc.psum_tensor("ps", [P, 8, 512], F32))

        class Area:
            def __init__(self, at=0):
                self.at = at

            def take(self, *shape, dt=F32):
                n = int(np.prod(shape))
                v = arena[:, self.at:self.at + n]
                self.at += n
                assert self.at <= 23808, self.at
                if dt != F32:
                    v = v.bitcast(dt)
                if len(shape) > 1:
                    names = "abcdef"[:len(shape)]
                    v = v.rearrange(f"p ({' '.join(names)}) -> p {' '.join(names)}",
                                    **{k: s for k, s in zip(names[1:], shape[1:])})
                return v

        ident = sb("ident", [P, P])
        ones = sb("ones", [P, P])
        mask_band = sb("mask_band", [P, NB, P])
        mask_inc = sb("mask_inc", [P, P])
        sel = sb("sel", [P, MH, P])
        gcol = sb("gcol", [P, 4, KT])
        mlgain = sb("mlgain", [P, KT])
        qkgain = sb("qkgain", [P, 2, AD])
        sinks = sb("sinks", [P, AH])
        ifbias = sb("ifbias", [P, 2, MH])
        pos_i = sb("pos_i", [P, NB], I32)
        freq = sb("freq", [P, RH])
        ss = sb("ss", [P, NB])
        ms = sb("ms", [P, NB])
        sd = sb("sd", [P, NB])
        rr = sb("rr", [P, NB])

        one = Area()
        p1 = one.take(NB, AH * AD + 2 * AKV * AD + 2 * MH)
        sga = one.take(KT, S)
        sgm = one.take(KT, S)
        mo = one.take(NB, MH * MV)
        mva = one.take(NB, MH, MV + 1)
        mqT = one.take(MH // 2, S)
        mkT = one.take(MH // 2, S)
        qT = one.take(KT, S)
        kT = one.take(AKV, S)
        attT = one.take(KT, S)
        wl = one.take(MH, 3, P)
        cw = one.take(2, 3 * P)
        at_sm = one.at
        sm = one.take(2, 4, S)
        pt = Area(at_sm - 768 - 3072 + 1024).take(NB, 4, P)
        sq = Area(at_sm).take((AH + AKV) * AD)
        hraw = Area(0).take(NB, MH, MV + 1)
        off_q = NB * 1296 + 2 * KT * S + NB * D + NB * MH * (MV + 1)
        hmT = Area(off_q).take(KT, S)
        hs = Area(at_sm).take(NB, MH, MV)
        mixT = Area(off_q + 2048).take(KT, S)
        hsq = Area(off_q + 2048 + 2048 + 512 + 2048).take(NB, MH, MV)
        tmpT = hsq.rearrange("p a b c -> p (a b c)").rearrange("p (a b) -> p a b", b=S)
        LB = 3

        two = Area()
        h2 = two.take(NB, D)
        sk = two.take(PH, NKEY)
        qpT = two.take(PH, S)
        scr = [two.take(PH, 2, NKEY), qpT.rearrange("p h (c k) -> p h c k", c=2)]
        hot = two.take(PR, TOPK, TOPK)
        picked = two.take(PR, TOPK, TOPK)
        n2row = Area(two.at - D).take(D)
        tv = two.take(PR, 2, TOPK)
        ti = two.take(PR, 2, TOPK, dt=U32)
        tif = two.take(PR, 2, TOPK)
        bv = two.take(PR, TOPK)
        bp = two.take(PR, TOPK, dt=U32)
        bij = two.take(2, PR * TOPK, dt=U32)
        bijf = two.take(2, PR * TOPK)
        exf = two.take(3, PR * TOPK)
        gates = two.take(NB * PH * TOPK)
        idx = two.take(NB, PH * TOPK, dt=U32)
        rows_d = two.take(DSLOTS, D)
        iota16 = sb("iota16", [P, TOPK])
        idx_st = sb("idx_st", [P, 2, TOPK], U32)
        dots = sb("dots", [P, 2, TOPK])
        gelu = sb("gelu", [P, 2, TOPK])
        wgt = sb("wgt", [P, 2, TOPK])
        diag = sb("diag", [P, 4, P])
        gsum = sb("gsum", [P, 2, PR])

        thr = Area()
        p2 = thr.take(NB, 3 * SBW)
        qkT2 = thr.take(8, S)
        zm = thr.take(2, 2, 3 * P)
        sp_ = thr.take(2, 2, 3 * P)
        wT = thr.take(2, 2, 3 * P)
        end_sb = thr.at
        hv = thr.take(NB, HGW)
        hq = thr.take(HH, S)
        hf = thr.take(HH, S)
        hg = thr.take(HH, S)
        sg2 = thr.take(2 * KT, S)
        osbT = thr.take(SBW // P, S)
        ohgT = thr.take(HGW // P, S)
        far = thr.at
        hgp = Area(0)
        key = hgp.take(HH, S)
        bb = hgp.take(HH, S)
        qe = hgp.take(HH, S)
        keT = hgp.take(HH, S)
        ket = hgp.take(NB, HH, P)
        vpar = hgp.take(2, NB, HGW)
        AT = hgp.take(HH, NB, P)
        state = hgp.take(3, HH, P)
        assert hgp.at <= end_sb
        xbuf = Area(far).take(2, HH, S)
        osq = key.rearrange("p h (b t) -> p h b t", b=NB)
        orr = bb.rearrange("p h (b t) -> p h b t", b=NB)
        mixT2 = Area(0).take(KT, S)
        tmp2 = Area(2048).take(2, S)
        silu = Area(3072).take(2, 2, S)
        hid = Area(3072 + 1024).take(4, 2, S)
        mask_str = sb("mask_str", [P, P])
        tri = sb("tri", [P, P])
        every16 = sb("every16", [P, P + HC])
        m16 = sb("m16", [P, P])
        restart = sb("restart", [P, HH * S])
        par = sb("par", [P, 2])
        sbgain = sb("sbgain", [P, 2])
        hgain = sb("hgain", [P, 1])
        lbt = sb("lbt", [P, 2, HH])
        lbs = sb("lbs", [P, 5, HH])
        dec = sb("dec", [P, HH, NHC])
        hst2 = sb("hst2", [P, 3, 2 * SH])

        kd = Area(at_sm + 1152).take(NB, 2 * AKV * AD)
        ang = sb("ang", [P, 4, NB, RH])
        cs = sb("cs", [P, 2, NB, RH])
        posf = sb("posf", [P, NB])
        hst = sb("hst", [P, 3, AH + AKV])
        rt = Area(at_sm - 768 - 3072).take(4, AH + AKV, RH)
        am = sb("am", [P, 2, 6, 4])
        gt = sb("gt", [P, 4, NB, MH])
        aT = sb("aT", [P, NB, MH])
        em = sb("em", [P, NB, MH])
        rows = sb("rows", [MH, 6, S])
        den = sb("den", [P, 4, NB, MH])

        block = ctx.enter_context(nc.Block())

        def wview(w):
            return w.rearrange("(t p) n -> p t n", p=P)

        w1 = wview(a["w_in"])
        chunks = []

        done_count = {}
        used = []
        halves = []

        def add(name, view, done, n=2):
            done_count[done] = done_count.get(done, 0) + n
            used.append((done, done_count[done]))
            chunks.append((name, (view,)))

        def add_split(name, *views):
            for g in range(2):
                halves.append((len(chunks), g))
            used.append(None)
            chunks.append((name, views))

        def add_columns(name, w, c0):
            add_split(name, *[w[:, :, c0 + g * HC2:c0 + (g + 1) * HC2] for g in range(2)])

        for c in range(2):
            add_columns("aq", w1, AQ0 + c * CW)
        add_split("kv", w1[:, :, AK0:MQ0], w1[:, :, MI0:MO0])
        for nm, c0, c1 in (("mq", MQ0, MK0), ("mk", MK0, MV0), ("mv", MV0, MI0), ("mo", MO0, GA0), ("gates", GA0, W1N)):
            for c in range(c0, c1, CW):
                add_columns(nm, w1, c)
        NW1 = len(chunks)
        for nm in ("w_branch_attn", "w_branch_mlstm", "w_out"):
            v = wview(a[nm])
            for c in range(2):
                add(nm, v[:, :, c * CW:(c + 1) * CW], "out_done" if nm == "w_out" else "br_done")
        v = wview(a["peer_w_query"])
        NQUERY = len(chunks)
        for c in range(2):
            add_columns("query", v, c * CW)
        NPEER = len(chunks)
        w2 = wview(a["w_in_2"])
        for c, nm in enumerate(("sb", "sb", "sb", "hq", "hf", "hv", "hg", "g2", "g2", "g2", "g2")):
            add_columns(nm, w2, c * CW)
        N2 = len(chunks)
        v = wview(a["w_branch_2"])
        for c in range(2):
            add("branch_2", v[:, :, c * CW:(c + 1) * CW], "br2_done", 4)
        v = wview(a["w_out_2"])
        for c in range(2):
            add("out_2", v[:, :, c * CW:(c + 1) * CW], "out2_done")
        NFFN = len(chunks)
        fg, fu = wview(a["w_ffn_gate_2"]), wview(a["w_ffn_up_2"])
        fd = wview(a["w_ffn_down_2"])
        NFF = FF // S
        for c in range(NFF):
            add_split("gate_up", fg[:, :, c * S:(c + 1) * S], fu[:, :, c * S:(c + 1) * S])
            if c % 2 or c == NFF - 1:
                c0 = c - c % 2
                add("down", fd[:, 2 * c0:2 * (c + 1), :], "down_done", 1)
        ffn_chunk = [n for n in range(NFFN, len(chunks)) if chunks[n][0] == "gate_up"]
        unit = {half: 2 * u for u, half in enumerate(halves)}
        ffn_unit = [unit[n, 0] for n in ffn_chunk]
        loads = {}
        per_slot = {}
        for n, (nm, views) in enumerate(chunks):
            for g in range(len(views)):
                per_slot[n % SLOTS, g] = per_slot.get((n % SLOTS, g), 0) + 16
                loads[n, g] = per_slot[n % SLOTS, g]

        def slot_sem(n, g):
            return sem(f"w_loaded{n % SLOTS}{'ab'[g]}")

        def raw_half(n, g):
            half = ring[:, n % SLOTS, :, :].rearrange("p t c -> p (t c)")[:, g * KT * HC2:(g + 1) * KT * HC2]
            return half.rearrange("p (t c) -> p t c", c=HC2)

        def split_units(n, g):
            cols = chunks[n][1][g].shape[2]
            return [(unit[n, g] + v, slice(v * KU, (v + 1) * KU), cols) for v in range(2)]

        def upper_parts(act, n, g):
            act.wait_ge(slot_sem(n, g), loads[n, g])
            for u, t, cols in split_units(n, g):
                if u >= 4:
                    act.wait_ge(sem("unit_used"), u - 3)
                act.activation(w_hi[:, u // 2 % 2, t, 0:cols], raw_half(n, g)[:, t, 0:cols], ACT.Copy).then_inc(sem("hi_ready"), 1)

        def lower_parts(pool, n, g):
            for u, t, cols in split_units(n, g):
                pool.wait_ge(sem("hi_ready"), u + 1)
                pool.tensor_tensor(w_lo[:, u // 2 % 2, t, 0:cols], raw_half(n, g)[:, t, 0:cols], w_hi[:, u // 2 % 2, t, 0:cols].bitcast(F32),
                                   ALU.subtract).then_inc(sem("lo_ready"), 1)

        def next_half(n, g, last):
            return [(n + 1, g)] if n + 1 < last else []

        def steps_after(halves, steps, skip, per=1):
            order, left = [], list(steps)
            for i, half in enumerate(halves):
                order.append(("half",) + half)
                if i >= skip:
                    order += left[:per]
                    left = left[per:]
            return order + left

        def halves_of(first, last):
            return [(n, g) for n in range(first, last) for g in range(2)]

        GROUPS = NB * 4
        att_steps = [("turn_qk", 0), ("turn_qk", 1)]
        for g in range(GROUPS + 2):
            att_steps.append(("attend", g))
        att_steps += [("gate_rows", 0), ("spread", 0)] + [("memory", h) for h in range(MH + 1)]
        plan1 = steps_after(halves_of(0, NW1 + 2), att_steps, 6)

        BATCHES = SH // 2
        hg_steps = [("turn_sb", 0)] + [("stick", q) for q in range(BATCHES + 2)]
        hg_steps += [("pairs", j) for j in range(0, HC, 2)] + [("turn_ke", 0)] + [("state", c) for c in range(0, NHC, 2)]
        plan2 = steps_after(halves_of(NPEER, N2), hg_steps, 6)

        @block.sync
        def _(sp):
            sp.dma_start(xres[:], a["x"].rearrange("(b p) n -> p b n", p=P)).then_inc(sem("x_loaded"), 16)
            for n, (nm, views) in enumerate(chunks):
                if n == NPEER:
                    sp.wait_ge(sem("x2_ready"), 4)
                    sp.dma_start(sk, a["sub_keys"]).then_inc(sem("sk_loaded"), 16)
                    sp.dma_start(n2row, a["n2row"]).then_inc(sem("sk_loaded"), 16)
                    sp.wait_ge(sem("row_free"), TOPK * (1 + NB * PH))
                for g, v in enumerate(views):
                    m = n - SLOTS
                    if m >= 0 and used[m] is not None:
                        if g == 0:
                            sp.wait_ge(sem(used[m][0]), used[m][1])
                    elif m >= 0:
                        for half in (range(g, g + 1) if len(views) == 2 else range(2)):
                            sp.wait_ge(sem("lo_ready"), unit[m, half] + 2)
                    if len(views) == 2:
                        to = raw_half(n, g)[:, :, 0:v.shape[2]]
                    elif nm == "down":
                        to = ring[:, n % SLOTS, :, :].rearrange("p (t c) n -> p t (c n)", c=2)[:, 0:v.shape[1], :]
                    else:
                        to = ring[:, n % SLOTS, :, :]
                    sp.dma_start(to, v).then_inc(slot_sem(n, g), 16)
            sp.wait_ge(sem("x5_ready"), 4)
            sp.dma_start(out.rearrange("(b p) n -> p b n", p=P), xres[:]).then_inc(sem("stored"), 16)
            sp.wait_ge(sem("stored"), 16)

        @block.gpsimd
        def _(pool):
            step = [0]

            def link(ins):
                step[0] += 1
                ins.then_inc(sem("pool_step"), 1)
                pool.wait_ge(sem("pool_step"), step[0])

            link(pool.memset(ident[:], 0.0))
            pool.affine_select(out=ident[:], in_=ident[:], compare_op=ALU.not_equal, fill=1.0, base=0,
                               pattern=[[-1, P]], channel_multiplier=1).then_inc(sem("ident_ready"), 1)
            pool.memset(ones[:], 1.0)
            pool.memset(mask_band[:], 0.0)
            pool.memset(mask_inc[:], 0.0)
            link(pool.memset(sel[:], 0.0))
            pool.affine_select(out=mask_band[:, 0, :], in_=mask_band[:, 0, :], compare_op=ALU.is_gt, fill=NEG, base=0,
                               pattern=[[1, P]], channel_multiplier=-1)
            pool.affine_select(out=mask_band[:, 1, :], in_=mask_band[:, 1, :], compare_op=ALU.is_ge, fill=NEG, base=0,
                               pattern=[[-1, P]], channel_multiplier=1)
            pool.affine_select(out=mask_inc[:], in_=mask_inc[:], compare_op=ALU.is_ge, fill=NEG, base=0,
                               pattern=[[1, P]], channel_multiplier=-1)
            pool.affine_select(out=sel[:], in_=sel[:], compare_op=ALU.not_equal, fill=1.0, base=0,
                               pattern=[[-1, MH], [0, P]], channel_multiplier=1)
            pool.memset(mva[:, :, :, MV:MV + 1], 1.0).then_inc(sem("masks_ready"), 1)
            for n, g in halves_of(0, NW1):
                lower_parts(pool, n, g)
            pool.iota(iota16[:], [[1, TOPK]], base=0, channel_multiplier=0, allow_small_or_imprecise_dtypes=True)
            pool.memset(mask_str[:], 0.0)
            pool.memset(tri[:], 1.0)
            pool.memset(every16[:], 0.0)
            pool.memset(m16[:], 1.0)
            pool.memset(restart[:], 1.0)
            link(pool.memset(par[:], 0.0))
            pool.affine_select(out=mask_str[:], in_=mask_str[:], compare_op=ALU.is_gt, fill=NEG, base=0,
                               pattern=[[1, P]], channel_multiplier=-1)
            pool.affine_select(out=tri[:], in_=tri[:], compare_op=ALU.is_ge, fill=0.0, base=0,
                               pattern=[[-1, P]], channel_multiplier=1)
            pool.memset(every16[:].rearrange("p (a b) -> p a b", b=HC)[:, :, 0:1], 1.0)
            pool.memset(restart[:].rearrange("p (a b) -> p a b", b=HC)[:, :, 0:1], 0.0)
            m3 = m16[:].rearrange("p (a b) -> p a b", b=HC)
            link(pool.affine_select(out=m3, in_=m3, compare_op=ALU.is_ge, fill=0.0, base=0,
                                    pattern=[[-HC, P // HC], [0, HC]], channel_multiplier=1))
            link(pool.affine_select(out=m3, in_=m3, compare_op=ALU.is_ge, fill=0.0, base=HC - 1,
                                    pattern=[[HC, P // HC], [0, HC]], channel_multiplier=-1))
            link(pool.tensor_copy(par[:], m3[:, 0:2, 0]))
            for c in range(1, P // HC // 2):
                link(pool.tensor_tensor(par[:], par[:], m3[:, 2 * c:2 * c + 2, 0], ALU.add))
            pool.affine_select(out=m16[:], in_=m16[:], compare_op=ALU.is_ge, fill=0.0, base=0,
                               pattern=[[1, P]], channel_multiplier=-1).then_inc(sem("masks2_ready"), 1)

            for n, g in halves_of(NQUERY, NPEER):
                lower_parts(pool, n, g)

            for b in range(NB):
                with pool.Fori(0, NR) as it:
                    pool.wait_ge(sem("routed"), it + (b * NR + 1))
                    for o in range(2):
                        g = it * 2 + (b * PH + o)
                        pool.wait_ge(sem("row_free"), g * TOPK + 1)
                        pool.tensor_copy(idx_st[:, o, :], idx[:, b, bass.ds(it * (2 * TOPK) + o * TOPK, TOPK)]).then_inc(sem("idx_staged"), 1)
                        pool.wait_ge(sem("idx_staged"), g + 1)
                        for k in range(TOPK):
                            pool.wait_ge(sem("drow_free"), g * TOPK + (k + 1))
                            pool.sem_inc(sem("slots_granted"), 1)
                            pool.indirect_dma_start(rows_d[:, k % DSLOTS, :], None, a["peer_down"],
                                                    bass.IndirectOffsetOnAxis(ap=idx_st[:, o, k:k + 1], axis=0)).then_inc(sem(f"drow{k % DSLOTS}"), 16)
                        for k in range(TOPK):
                            pool.wait_ge(sem("row_free"), g * TOPK + (k + 1))
                            pool.sem_inc(sem("slots_granted"), 1)
                            pool.indirect_dma_start(rows_u[:, k, :], None, a["peer_up"],
                                                    bass.IndirectOffsetOnAxis(ap=idx_st[:, o, k:k + 1], axis=0)).then_inc(sem(f"urow{k}"), 16)
            for n, g in halves_of(NPEER, N2) + [(n, g) for n, g in halves if n >= NFFN]:
                lower_parts(pool, n, g)

        def norm_act(act, k, ready, count, first):
            act.wait_ge(sem(ready), count)
            for b in range(NB):
                act.activation(xn[:, b, :], xres[:, b, :], ACT.Square, accum_out=ss[:, b:b + 1]).then_inc(sem("sumsq"), 1)
            act.wait_ge(sem("meansq"), k + 1)
            act.activation(sd[:], ms[:], ACT.Sqrt).then_inc(sem("root"), 1)
            for g in range(2):
                upper_parts(act, first, g)
            for t in range(KT):
                act.wait_ge(sem("turned"), KT // 2 * k + t // 2 + 1)
                act.activation(hT_hi[:, t, :], ps[:, t // 2, (t % 2) * S:(t % 2 + 1) * S], ACT.Copy,
                               scale=gcol[:, k, t:t + 1]).then_inc(sem("hT_hi_ready"), 1)

        def norm_dve(dve, link, k):
            dve.wait_ge(sem("sumsq"), NB * (k + 1))
            dve.tensor_scalar(ms[:], ss[:], 1.0 / D, EPS, ALU.mult, ALU.add).then_inc(sem("meansq"), 1)
            dve.wait_ge(sem("root"), k + 1)
            link(dve.reciprocal(rr[:], sd[:]))
            for b in range(NB):
                dve.tensor_scalar(xn[:, b, :], xres[:, b, :], rr[:, b:b + 1], None, ALU.mult).then_inc(sem("xn_ready"), 1)
            if k == 1:
                dve.wait_ge(sem("sk_loaded"), 32)
                dve.wait_ge(sem("xn_ready"), 2 * NB)
                for b in range(NB):
                    ins = dve.tensor_tensor(h2[:, b, :], xn[:, b, :], n2row, ALU.mult)
                link(ins)
            dve.wait_ge(sem("turned"), KT // 2 * (k + 1))
            for t in range(KT):
                dve.wait_ge(sem("hT_hi_ready"), KT * k + t // 2 * 2 + 2)
                dve.scalar_tensor_tensor(out=hT_lo[:, t, :], in0=ps[:, t // 2, (t % 2) * S:(t % 2 + 1) * S], scalar=gcol[:, k, t:t + 1],
                                         in1=hT_hi[:, t, :].bitcast(F32), op0=ALU.mult, op1=ALU.subtract).then_inc(sem("hT_ready"), 1)

        def norm_pe(pe, k):
            for b in range(NB):
                pe.wait_ge(sem("xn_ready"), NB * k + b + 1)
                for t in range(KT):
                    ins = pe.transpose(ps[:, t // 2, (t % 2) * S + b * P:(t % 2) * S + (b + 1) * P],
                                       xn[:, b, t * P:(t + 1) * P], ident[:])
                    if b == NB - 1 and t % 2:
                        ins.then_inc(sem("turned"), 1)

        @block.tensor
        def _(pe):
            n_half = [0]
            n_chunk = [0]

            def begin_half(evac, first):
                h = n_half[0]
                if h - first >= LB:
                    pe.wait_ge(sem(evac), h - first - LB + 1)
                n_half[0] += 1
                return ps[:, (h - first) % LB, :]

            def split_half(n, g, tok, bank):
                for u, ts, cols in split_units(n, g):
                    pe.wait_ge(sem("lo_ready"), u + 1)
                    hi, lo = w_hi[:, u // 2 % 2], w_lo[:, u // 2 % 2]
                    for t in range(ts.start, ts.stop):
                        for j in range(2):
                            js = slice(j * P, (j + 1) * P)
                            if tok:
                                to = bank[:, j * cols:(j + 1) * cols]
                                parts = ((hT_hi[:, t, js], hi[:, t, 0:cols]), (hT_hi[:, t, js], lo[:, t, 0:cols]), (hT_lo[:, t, js], hi[:, t, 0:cols]))
                            else:
                                to = bank[:, j * S:(j + 1) * S]
                                parts = ((hi[:, t, js], hT_hi[:, t, :]), (hi[:, t, js], hT_lo[:, t, :]), (lo[:, t, js], hT_hi[:, t, :]))
                            for e, (still, moving) in enumerate(parts):
                                ins = pe.matmul(to, still, moving, start=(t == 0 and j == 0 and e == 0), stop=(t == KT - 1 and e == 2),
                                                skip_group_check=True)
                    ins.then_inc(sem("unit_used"), 1)
                n_chunk[0] = n + g

            def half_tok(n, b, src, cols, evac, done, first):
                if b == 0:
                    pe.wait_ge(slot_sem(n, 0), loads[n, 0])
                bank = begin_half(evac, first)
                for t in range(KT):
                    ins = pe.matmul(bank[:, 0:cols], src[:, t, b * P:(b + 1) * P], ring[:, n % SLOTS, t, 0:cols],
                                    start=(t == 0), stop=(t == KT - 1))
                ins.then_inc(sem(done), 1)
                n_chunk[0] = n + b

            def half_T(n, g, src, evac, done, first):
                if g == 0:
                    pe.wait_ge(slot_sem(n, 0), loads[n, 0])
                bank = begin_half(evac, first)
                for j in range(2):
                    for t in range(KT):
                        ins = pe.matmul(bank[:, j * S:(j + 1) * S],
                                        ring[:, n % SLOTS, t, (2 * g + j) * P:(2 * g + j + 1) * P], src[:, t, :],
                                        start=(t == 0), stop=(t == KT - 1))
                ins.then_inc(sem(done), 1)
                n_chunk[0] = n + g

            def chunk_tok(src, cols, evac, done, first):
                n = n_chunk[0]
                for b in range(NB):
                    half_tok(n, b, src, cols, evac, done, first)

            def chunk_T(src, evac, done, first):
                n = n_chunk[0]
                for g in range(2):
                    half_T(n, g, src, evac, done, first)

            pe.wait_ge(sem("ident_ready"), 1)
            norm_pe(pe, 0)
            pe.wait_ge(sem("hT_ready"), KT)

            def turn_qk(b):
                pe.wait_ge(sem("qk_rotated"), b + 1)
                if b:
                    pe.wait_ge(sem("qkT_ready"), b)
                for j in range(10):
                    src = p1[:, b, j * P:(j + 1) * P] if j < 8 else kd[:, b, (j - 8) * P:(j - 7) * P]
                    ins = pe.transpose(ps[:, 4 + j // 4, (j % 4) * P:(j % 4 + 1) * P], src, ident[:])
                ins.then_inc(sem("qk_turned"), 1)

            def attend(k):
                if 1 <= k <= GROUPS:
                    b = (k - 1) // 4
                    pe.wait_ge(sem("probs"), k)
                    if k >= 2:
                        pe.wait_ge(sem("probsT"), k - 1)
                    for kb in range(b + 1):
                        for i in range(4):
                            ins = pe.transpose(ps[:, 6 + kb, i * P:(i + 1) * P], sm[:, (k - 1) % 2, i, kb * P:(kb + 1) * P], ident[:])
                    ins.then_inc(sem("probs_turned"), 1)
                if k < GROUPS:
                    b, q = k // 4, k % 4
                    if k == 0:
                        pe.wait_ge(sem("qkT_ready"), NB)
                        pe.wait_ge(sem("masks_ready"), 1)
                    else:
                        pe.wait_ge(sem("scores_read"), k)
                    for i in range(4):
                        h = 4 * q + i
                        r = slice((h % 2) * AD, (h % 2 + 1) * AD)
                        ins = pe.matmul(ps[:, 4 + i % 2, (i // 2) * S:(i // 2) * S + P * (b + 1)], qT[r, h // 2, b * P:(b + 1) * P],
                                        kT[r, h // (AH // AKV), 0:P * (b + 1)], start=True, stop=True)
                    ins.then_inc(sem("scores"), 1)
                if k >= 2:
                    b, q = (k - 2) // 4, (k - 2) % 4
                    pe.wait_ge(sem("probsT"), k - 1)
                    if k >= 3:
                        pe.wait_ge(sem("att_evac"), k - 2)
                    for i in range(2):
                        for kb in range(b + 1):
                            v = p1[:, kb, AV0 + q // 2 * AD:AV0 + (q // 2 + 1) * AD]
                            ins = pe.matmul(ps[i * AD:(i + 1) * AD, 3, 0:S], v, pt[:, kb, i::2, :], start=(kb == 0), stop=(kb == b))
                    ins.then_inc(sem("att_done"), 1)

            def gate_rows(_):
                pe.wait_ge(sem("gates_tok"), 1)
                pe.wait_ge(sem("att_evac"), GROUPS)
                for k in range(2):
                    for b in range(NB):
                        ins = pe.matmul(ps[0:MH, 3, k * S + b * P:k * S + (b + 1) * P], gt[:, k, b, :], ident[:],
                                        start=True, stop=True)
                ins.then_inc(sem("gates_turned"), 1)

            def spread(_):
                pe.wait_ge(sem("rows_ready"), 1)
                for b in range(NB):
                    for k, r in enumerate((3, 5)):
                        ins = pe.matmul(ps[:, 3, (2 * k + b) * MH:(2 * k + b + 1) * MH], rows[:, r, b * P:(b + 1) * P],
                                        ident[0:MH, 0:MH], start=True, stop=True)
                for h in range(MH):
                    ins = pe.matmul(ps[:, 4 + h // 2, (h % 2) * S:(h % 2 + 1) * S], sel[0:MH, h, :], rows[:, 4, :], start=True, stop=True)
                ins.then_inc(sem("m_spread"), 1)

            def memory(h):
                if h >= 1:
                    g = h - 1
                    pe.wait_ge(sem("cw_ready"), g + 1)
                    if g >= 2:
                        pe.wait_ge(sem("num_evac"), g - 1)
                    bank = ps[:, 6 + g % 2, :]
                    w = MV + 1
                    pe.matmul(bank[:, 0:w], cw[:, g % 2, 0:P], mva[:, 0, g, :], start=True, stop=True)
                    pe.matmul(bank[:, w:2 * w], cw[:, g % 2, P:2 * P], mva[:, 0, g, :], start=True, stop=False)
                    pe.matmul(bank[:, w:2 * w], cw[:, g % 2, 2 * P:3 * P], mva[:, 1, g, :], start=False,
                              stop=True).then_inc(sem("num_done"), 1)
                if h < MH:
                    r = slice((h % 2) * MQ, (h % 2 + 1) * MQ)
                    if h >= 2:
                        pe.wait_ge(sem("cw_ready"), h - 1)
                    else:
                        pe.wait_ge(sem("wl_ready"), MH)
                    bank = ps[:, 4 + h % 2, :]
                    pe.matmul(bank[:, 0:S], mkT[r, h // 2, 0:P], mqT[r, h // 2, :], start=True, stop=True)
                    pe.matmul(bank[:, S:S + P], mkT[r, h // 2, P:S], mqT[r, h // 2, P:S],
                              start=True, stop=True).then_inc(sem("ml_qk"), 1)

            do = {"turn_qk": turn_qk, "attend": attend, "gate_rows": gate_rows, "spread": spread, "memory": memory}
            for what, n, *g in plan1:
                if what != "half":
                    do[what](n)
                elif n >= NW1:
                    if n == NW1 and g[0] == 0:
                        pe.wait_ge(sem("att_evac"), GROUPS)
                        pe.wait_ge(sem("p1_evac"), 2 * NW1)
                    half_T(n, g[0], attT, "br_evac", "br_done", 2 * NW1)
                else:
                    split_half(n, g[0], chunks[n][0] in ("aq", "kv", "mv", "mo"), begin_half("p1_evac", 0))
            pe.wait_ge(sem("hm_tok"), 1)
            for t in range(KT):
                for b in range(NB):
                    ins = pe.transpose(ps[:, 4 + t // 2, (t % 2) * S + b * P:(t % 2) * S + (b + 1) * P], hs[:, b, t, :], ident[:])
                if t % 2:
                    ins.then_inc(sem("hm_turned"), 1)
            pe.wait_ge(sem("hmT_ready"), KT)
            for c in range(2):
                chunk_T(hmT, "br_evac", "br_done", 2 * NW1)
            pe.wait_ge(sem("br_evac"), 8)
            f = n_half[0]
            for c in range(2):
                chunk_tok(mixT, CW, "x2_ready", "out_done", f)

            pe.wait_ge(sem("x2_ready"), 4)
            norm_pe(pe, 1)
            pe.wait_ge(sem("hT_ready"), 2 * KT)
            f = n_half[0]
            for c in range(2):
                for g in range(2):
                    split_half(NQUERY + c, g, False, begin_half("q_evac", f))
            pe.wait_ge(sem("sk_loaded"), 32)
            pe.wait_ge(sem("q_evac"), 4)
            for b in range(NB):
                for h in range(PH):
                    for p in range(2):
                        r = slice(p * (P // 2), (p + 1) * (P // 2))
                        ins = pe.matmul(ps[:, 4 - 4 * b + 2 * (h // 4) + p, (h % 4) * NKEY:(h % 4 + 1) * NKEY],
                                        qpT[r, h, b * P:(b + 1) * P], sk[r, h, :], start=True, stop=True)
                ins.then_inc(sem("key_scores"), 1)
            for b in range(NB):
                pe.wait_ge(sem("scr_ready"), 2 * NB)
                acc = ps[:, 6 - 2 * b:8 - 2 * b, :]
                for c in range(2):
                    ins = pe.matmul(acc[:, c, :], ident[:], xres[:, b, c * CW:(c + 1) * CW], start=True, stop=True)
                if b == 0:
                    ins.then_inc(sem("row_free"), TOPK)
                with pe.Fori(0, PH // 2) as it:
                    for o in range(2):
                        g = it * 2 + (b * PH + o)
                        for k in range(TOPK):
                            pe.wait_ge(sem("diag_ready"), g * TOPK + (k + 1))
                            pe.wait_ge(sem(f"urow{k}"), g * 16 + 16)
                            for c in range(2):
                                ins = pe.matmul(acc[:, c, :], diag[:, k % 4, :], rows_u[:, k, c * CW:(c + 1) * CW],
                                                start=False, stop=True, skip_group_check=True)
                            ins.then_inc(sem("row_free"), 1)

            pe.wait_ge(sem("x3_ready"), NB)
            norm_pe(pe, 2)
            pe.wait_ge(sem("hT_ready"), 3 * KT)

            def turn_sb(_):
                pe.wait_ge(sem("sb_normed"), 1)
                pe.wait_ge(sem("masks2_ready"), 1)
                for j in range(8):
                    for b in range(NB):
                        ins = pe.transpose(ps[:, 4 + j // 2, (j % 2) * S + b * P:(j % 2) * S + (b + 1) * P],
                                           p2[:, b, j * P:(j + 1) * P], ident[:])
                ins.then_inc(sem("sb_turned"), 1)

            def stick(k):
                if 1 <= k <= BATCHES:
                    q = (k - 1) % 2
                    pe.wait_ge(sem("sp_ready"), k)
                    if k >= 2:
                        pe.wait_ge(sem("logw_ready"), k - 1)
                    for i in range(2):
                        pe.matmul(ps[:, 6 + i, 0:3 * P], tri[:], sp_[:, q, i, :], start=True, stop=False)
                        ins = pe.matmul(ps[:, 6 + i, P:S], ones[:], sp_[:, q, i, S:3 * P], start=False, stop=True)
                    ins.then_inc(sem("rest_done"), 1)
                if k < BATCHES:
                    if k == 0:
                        pe.wait_ge(sem("sbT_ready"), 1)
                    else:
                        pe.wait_ge(sem("zm_ready"), k)
                    for i in range(2):
                        h = 2 * k + i
                        r = slice(i * SD, (i + 1) * SD)
                        pe.matmul(ps[:, 4 + i, 0:S], qkT2[r, 4 + h // 2, 0:P], qkT2[r, h // 2, :], start=True, stop=True)
                        ins = pe.matmul(ps[:, 4 + i, S:S + P], qkT2[r, 4 + h // 2, P:S], qkT2[r, h // 2, P:S], start=True, stop=True)
                    ins.then_inc(sem("z_done"), 1)
                if k >= 2:
                    pe.wait_ge(sem("w_ready"), k - 1)
                    if k >= 3:
                        pe.wait_ge(sem("osb_evac"), k - 2)
                    for i in range(2):
                        o = ps[i * SD:(i + 1) * SD, 3, 0:S]
                        v0 = 2 * SBW + (2 * (k - 2) + i) * SD
                        pe.matmul(o, p2[:, 0, v0:v0 + SD], wT[:, k % 2, i, 0:S], start=True, stop=False)
                        ins = pe.matmul(o[:, P:S], p2[:, 1, v0:v0 + SD], wT[:, k % 2, i, S:3 * P], start=False, stop=True)
                    ins.then_inc(sem("osb_done"), 1)

            def pairs(j0):
                for j in range(j0, j0 + 2):
                    pe.wait_ge(sem("pairs_ready"), j + 1)
                    for c in range(2):
                        ins = pe.matmul(ps[:, 4 + c, :], every16[:, HC - j:HC - j + P], xbuf[:, j % 2, 2 * c:2 * c + 2, :],
                                        start=(j == 0), stop=(j == HC - 1), skip_group_check=True)
                    ins.then_inc(sem("pairs_summed"), 1)

            def turn_ke(_):
                pe.wait_ge(sem("keT_ready"), 1)
                for b in range(NB):
                    for h in range(HH):
                        ins = pe.transpose(ps[:, 6 + b, h * P:(h + 1) * P], keT[:, h, b * P:(b + 1) * P], ident[:])
                ins.then_inc(sem("ke_turned"), 1)
                pe.wait_ge(sem("AT_ready"), 1)
                for b in range(NB):
                    for h in range(HH):
                        pe.matmul(ps[:, 4 + b, h * P:(h + 1) * P], hv[:, b, h * P:(h + 1) * P], AT[:, h, b, :],
                                  start=(h == 0), stop=True, skip_group_check=True)

            def state_pe(c0):
                for c in range(c0, c0 + 2):
                    b, r0 = c // (P // HC), (c % (P // HC)) * HC
                    rb = slice(r0 // 32 * 32, r0 // 32 * 32 + 32)
                    if c == 0:
                        pe.wait_ge(sem("ket_ready"), 1)
                        pe.wait_ge(sem("vpar_ready"), 1)
                    if c < NHC - 1:
                        if c >= 2:
                            pe.wait_ge(sem("state_ready"), c - 1)
                        for h in range(HH):
                            ins = pe.matmul(ps[:, 6 + c % 2, h * P:(h + 1) * P], ket[rb, b, h, :], vpar[rb, c % 2, b, h * P:(h + 1) * P],
                                            start=True, stop=True)
                        ins.then_inc(sem("inc_done"), 1)
                    if c >= 1:
                        pe.wait_ge(sem("state_ready"), c)
                        for h in range(HH):
                            ins = pe.matmul(ps[:, 4 + b, h * P + r0:h * P + r0 + HC], state[:, c % 3, h, :], qe[:, h, b * P + r0:b * P + r0 + HC],
                                            start=False, stop=True, skip_group_check=True)
                        ins.then_inc(sem("read_done"), 1)

            f = n_half[0]
            do = {"turn_sb": turn_sb, "stick": stick, "pairs": pairs, "turn_ke": turn_ke, "state": state_pe}
            for what, n, *g in plan2:
                if what != "half":
                    do[what](n)
                else:
                    split_half(n, g[0], chunks[n][0] in ("sb", "hv"), begin_half("p2_evac", f))
            pe.wait_ge(sem("osq_ready"), 2)
            for b in range(NB):
                ins = pe.matmul(ps[:, 6 + b, :], ones[:], osq[:, :, b, :], start=True, stop=True)
            ins.then_inc(sem("osq_summed"), 1)
            pe.wait_ge(sem("ohg_ready"), 1)
            pe.wait_ge(sem("p2_evac"), 2 * (N2 - NPEER))
            f = n_half[0]
            for c in range(2):
                n = n_chunk[0]
                pe.wait_ge(slot_sem(n, 0), loads[n, 0])
                for j in range(4):
                    bank = begin_half("br2_evac", f)
                    for e, src in enumerate((osbT, ohgT)):
                        for t in range(4):
                            ins = pe.matmul(bank[:, e * S:(e + 1) * S], ring[:, n % SLOTS, 4 * e + t, j * P:(j + 1) * P], src[:, t, :],
                                            start=(t == 0), stop=(t == 3))
                    ins.then_inc(sem("br2_done"), 1)
                n_chunk[0] += 1
            pe.wait_ge(sem("br2_evac"), 8)
            f = n_half[0]
            for c in range(2):
                chunk_tok(mixT2, CW, "x4_ready", "out2_done", f)
            pe.wait_ge(sem("x4_ready"), 4)
            norm_pe(pe, 3)
            pe.wait_ge(sem("hT_ready"), 4 * KT)
            f = n_half[0]

            def down(cs, nslot):
                for m, c in enumerate(cs):
                    pe.wait_ge(sem("hid_ready"), c + 1)
                    for j in range(2):
                        w = ring[:, nslot, :, :].rearrange("p (t c) n -> p t (c n)", c=2)[:, 2 * m + j, :]
                        for b in range(NB):
                            for e in range(2):
                                ins = pe.matmul(ps[:, 4 + 2 * b + e, :], hid[:, c % 4, j, b * P:(b + 1) * P], w[:, e * CW:(e + 1) * CW],
                                                start=(c == 0 and j == 0), stop=(c == NFF - 1 and j == 1), skip_group_check=True)
                ins.then_inc(sem("down_done"), 1)

            waiting = None
            for n in range(n_chunk[0], len(chunks)):
                if chunks[n][0] == "gate_up":
                    c = (n_half[0] - f) // 2
                    if c >= 2:
                        pe.wait_ge(sem("hid_ready"), c - 1)
                    for g in range(2):
                        split_half(n, g, False, ps[:, (2 * c + g) % 4, :])
                        n_half[0] += 1
                else:
                    pe.wait_ge(slot_sem(n, 0), loads[n, 0])
                    down([c - 1, c] if c % 2 else [c], n % SLOTS)
                    n_chunk[0] += 1

        @block.scalar
        def _(act):
            step = [0]

            def link(ins):
                step[0] += 1
                ins.then_inc(sem("act_step"), 1)
                act.wait_ge(sem("act_step"), step[0])

            for n, (t, v) in enumerate((("gcol", gcol[:]), ("mlgain", mlgain[:]), ("qkgain", qkgain[:]), ("sinks", sinks[:]),
                         ("ifbias", ifbias[:]), ("pos", pos_i[:]), ("freq", freq[:]), ("sbgain", sbgain[:]), ("hgain", hgain[:]), ("lbt", lbt[:]))):
                act.dma_start(v, a[t]).then_inc(sem("small_loaded"), 16)
            act.wait_ge(sem("small_loaded"), NSMALL * 16)
            norm_act(act, 0, "x_loaded", 16, 0)
            act.wait_ge(sem("masks_ready"), 1)
            seen = [chunks[n][0] for n in range(N2)]

            def leave1(n, g):
                h = 2 * n + g
                nm = chunks[n][0]
                c = seen[:n].count(nm)
                act.wait_ge(sem("unit_used"), unit[n, g] + 2)
                bank = ps[:, h % LB, :]
                col = c * CW + g * HC2
                by_block = bank.rearrange("p (b c) -> p b c", b=NB)
                if nm == "aq":
                    ins = act.activation(p1[:, :, col:col + HC2], by_block, ACT.Copy)
                elif nm == "kv" and g == 0:
                    ins = act.activation(p1[:, :, AK0:MQ0], by_block, ACT.Copy)
                elif nm == "kv":
                    ins = act.activation(p1[:, :, MQ0:MQ0 + 2 * MH], bank[:, 0:NB * 2 * MH].rearrange("p (b c) -> p b c", b=NB), ACT.Copy)
                elif nm in ("mq", "mk"):
                    dst = mqT if nm == "mq" else mkT
                    ins = act.activation(dst[:, 2 * g:2 * g + 2, :], bank.rearrange("p (a b) -> p a b", a=2), ACT.Copy)
                elif nm == "mv":
                    ins = act.activation(mva[:, :, 4 * c + 2 * g:4 * c + 2 * g + 2, 0:MV], bank.rearrange("p (b h v) -> p b h v", b=NB, v=MV), ACT.Copy)
                elif nm == "mo":
                    ins = act.activation(mo[:, :, col:col + HC2], by_block, ACT.Sigmoid)
                else:
                    dst = sga if c < 2 else sgm
                    t = 4 * (c % 2) + 2 * g
                    ins = act.activation(dst[:, t:t + 2, :], bank.rearrange("p (a b) -> p a b", a=2), ACT.Sigmoid)
                ins.then_inc(sem("p1_evac"), 1)

            def turn_qk(b):
                if b == 0:
                    act.wait_ge(sem("angles"), 1)
                    act.activation(cs[:], ang[:, 2:4, :, :], ACT.Sin).then_inc(sem("sines"), 1)
                    for k in range(NB):
                        act.wait_ge(sem("qk_ms"), k + 1)
                        act.activation(hst[:, 1, :], hst[:, 0, :], ACT.Sqrt).then_inc(sem("qk_root"), 1)
                act.wait_ge(sem("qk_turned"), b + 1)
                for j in range(2):
                    act.activation(qT[:, 4 * j:4 * j + 4, b * P:(b + 1) * P], ps[:, 4 + j, :].rearrange("p (a b) -> p a b", a=4), ACT.Copy)
                act.activation(kT[:, :, b * P:(b + 1) * P], ps[:, 6, 0:S].rearrange("p (a b) -> p a b", a=2), ACT.Copy).then_inc(sem("qkT_ready"), 1)

            def attend(k):
                if k < GROUPS:
                    nk = P * (k // 4 + 1)
                    act.wait_ge(sem("row_max"), k + 1)
                    for i in range(4):
                        x = sm[:, k % 2, i, 0:nk]
                        act.activation(x, x, ACT.Exp, bias=am[:, k % 2, 1, i:i + 1], accum_out=am[:, k % 2, 2, i:i + 1])
                    act.activation(am[:, k % 2, 4, :], am[:, k % 2, 3, :], ACT.Exp).then_inc(sem("exps"), 1)
                if k >= 2:
                    b, q = (k - 2) // 4, (k - 2) % 4
                    act.wait_ge(sem("att_done"), k - 1)
                    for i in range(2):
                        ins = act.activation(attT[i * AD:(i + 1) * AD, 2 * q:2 * q + 2, b * P:(b + 1) * P],
                                             ps[i * AD:(i + 1) * AD, 3, 0:S].rearrange("p (a b) -> p a b", a=2), ACT.Copy)
                    ins.then_inc(sem("att_evac"), 1)
                if 1 <= k <= GROUPS:
                    act.wait_ge(sem("probs_turned"), k)
                    for kb in range((k - 1) // 4 + 1):
                        ins = act.activation(pt[:, kb, :, :], ps[:, 6 + kb, :].rearrange("p (a b) -> p a b", a=4), ACT.Copy)
                    ins.then_inc(sem("probsT"), 1)

            def gate_rows(_):
                act.wait_ge(sem("gates_raw"), 1)
                act.activation(gt[:, 2:4, :, :], gt[:, 0:2, :, :], ACT.Tanh, scale=1.0 / CAP).then_inc(sem("gates_tanh"), 1)
                act.wait_ge(sem("gates_cap"), 1)
                link(act.activation(gt[:, 2, :, :], gt[:, 1, :, :], ACT.Exp, scale=-1.0))
                act.activation(gt[:, 3, :, :], gt[:, 2, :, :], ACT.Ln, bias=1.0).then_inc(sem("gates_soft"), 1)
                act.wait_ge(sem("gates_turned"), 1)
                act.activation(rows[:, 0:2, :], ps[0:MH, 3, :].rearrange("p (a b) -> p a b", a=2), ACT.Copy).then_inc(sem("rows_gates"), 1)
                act.wait_ge(sem("m_rows"), 1)
                act.activation(rows[:, 5, :], rows[:, 5, :], ACT.Exp, scale=-1.0).then_inc(sem("rows_ready"), 1)

            def spread(_):
                act.wait_ge(sem("m_spread"), 1)
                act.activation(aT[:], ps[:, 3, 0:NB * MH].rearrange("p (a b) -> p a b", a=NB), ACT.Copy)
                link(act.activation(em[:], ps[:, 3, NB * MH:2 * NB * MH].rearrange("p (a b) -> p a b", a=NB), ACT.Copy))
                act.wait_ge(sem("wl_masked"), 1)
                for h in range(MH):
                    act.activation(wl[:, h, 0, :], wl[:, h, 0, :], ACT.Exp, bias=aT[:, 0, h:h + 1])
                    act.activation(wl[:, h, 1, :], ps[:, 4 + h // 2, (h % 2) * S + P:(h % 2 + 1) * S], ACT.Exp, bias=aT[:, 0, h:h + 1])
                    act.activation(wl[:, h, 2, :], wl[:, h, 2, :], ACT.Exp, bias=aT[:, 1, h:h + 1]).then_inc(sem("wl_ready"), 1)

            def memory(h):
                if h >= 1:
                    act.wait_ge(sem("num_done"), h)
                    act.activation(hraw[:, :, h - 1, :], ps[:, 6 + (h - 1) % 2, 0:2 * (MV + 1)].rearrange("p (a b) -> p a b", a=2),
                                   ACT.Copy).then_inc(sem("num_evac"), 1)

            do = {"turn_qk": turn_qk, "attend": attend, "gate_rows": gate_rows, "spread": spread, "memory": memory}
            for what, n, *g in plan1:
                if what != "half":
                    do[what](n)
                elif n < NW1:
                    leave1(n, g[0])
                    for half in next_half(n, g[0], NW1):
                        upper_parts(act, *half)
            act.wait_ge(sem("hm_ms"), 1)
            act.activation(den[:, 2, :, :], den[:, 1, :, :], ACT.Sqrt).then_inc(sem("hm_root"), 1)
            for t in range(KT):
                act.wait_ge(sem("hm_turned"), t // 2 + 1)
                act.activation(hmT[:, t, :], ps[:, 4 + t // 2, (t % 2) * S:(t % 2 + 1) * S], ACT.Copy,
                               scale=mlgain[:, t:t + 1]).then_inc(sem("hmT_ready"), 1)

            norm_act(act, 1, "x2_ready", 4, NQUERY)
            for c in range(2):
                for g in range(2):
                    act.wait_ge(sem("unit_used"), unit[NQUERY + c, g] + 2)
                    act.activation(qpT[:, 4 * c + 2 * g:4 * c + 2 * g + 2, :], ps[:, (2 * c + g) % LB, :].rearrange("p (a b) -> p a b", a=2),
                                   ACT.Copy).then_inc(sem("q_evac"), 1)
                    for half in next_half(NQUERY + c, g, NPEER):
                        upper_parts(act, *half)
            act.wait_ge(sem("key_scores"), NB)
            for b in range(NB):
                for g in range(2):
                    for p in range(2):
                        ins = act.activation(scr[b][:, 4 * g:4 * g + 4, p, :], ps[:, 4 - 4 * b + 2 * g + p, :].rearrange("p (a b) -> p a b", a=4), ACT.Copy)
                    ins.then_inc(sem("scr_ready"), 1)

            def gate_exp(r, at):
                act.wait_ge(sem("best_shifted"), r + 1)
                act.sem_inc(sem("exp_granted"), 1)
                x = gates[:, bass.ds(at, PR * TOPK)]
                act.activation(x, x, ACT.Exp).then_inc(sem("best_exp"), 1)

            for r in range(2):
                gate_exp(r, r * PR * TOPK)
            for b in range(NB):
                parts = ((0, NR, True),) if b < NB - 1 else ((0, NR - 2, True), (NR - 2, NR, False))
                for first, last, more in parts:
                    with act.Fori(first, last) as it:
                        for o in range(PR):
                            g = it * PR + (b * PH + o)
                            act.wait_ge(sem("drow_free"), g * TOPK + (DSLOTS + TOPK))
                            act.activation(gelu[:, o, :], dots[:, o, :], ACT.Gelu).then_inc(sem("gelu_done"), 1)
                            act.wait_ge(sem("wgt_ready"), g + 1)
                            for k in range(TOPK):
                                act.wait_ge(sem("row_free"), g * TOPK + (TOPK + k - 3))
                                act.activation(diag[:, k % 4, :], ident[:], ACT.Copy, scale=wgt[:, o, k:k + 1]).then_inc(sem("diag_ready"), 1)
                        if more:
                            gate_exp(it + (b * NR + 2), it * (PR * TOPK) + (b * NR + 2) * PR * TOPK)
                act.wait_ge(sem("row_free"), TOPK + (b + 1) * PH * TOPK)
                act.activation(xres[:, b, :], ps[:, 6 - 2 * b:8 - 2 * b, :].rearrange("p a b -> p (a b)"), ACT.Copy).then_inc(sem("x3_ready"), 1)
            norm_act(act, 2, "x3_ready", NB, NPEER)

            def leave2(n, g):
                nm = chunks[n][0]
                c = n - NPEER
                h = 2 * c + g
                act.wait_ge(sem("unit_used"), unit[n, g] + 2)
                bank = ps[:, h % LB, :]
                bank2 = bank.rearrange("p (a b) -> p a b", a=2)
                if nm == "sb":
                    ins = act.activation(p2[:, :, c * CW + g * HC2:c * CW + (g + 1) * HC2], bank.rearrange("p (b c) -> p b c", b=NB), ACT.Copy)
                elif nm == "hv":
                    ins = act.activation(hv[:, :, g * HC2:(g + 1) * HC2], bank.rearrange("p (b c) -> p b c", b=NB), ACT.Copy)
                elif nm == "g2":
                    t = 4 * (c - 7) + 2 * g
                    ins = act.activation(sg2[:, t:t + 2, :], bank2, ACT.Sigmoid)
                else:
                    dst = {"hq": hq, "hf": hf, "hg": hg}[nm]
                    ins = act.activation(dst[:, 2 * g:2 * g + 2, :], bank2, ACT.Sigmoid if nm == "hf" else ACT.Silu)
                ins.then_inc(sem("p2_evac"), 1)

            def turn_sb(_):
                act.wait_ge(sem("lb_shifted"), 1)
                act.activation(lbs[:, 1:3, :], lbs[:, 1:3, :], ACT.Exp).then_inc(sem("lb_exp"), 1)
                for b in range(NB):
                    act.wait_ge(sem("sb_ms"), b + 1)
                    act.activation(hst2[:, 1, :], hst2[:, 0, :], ACT.Sqrt).then_inc(sem("sb_root"), 1)
                act.wait_ge(sem("sb_turned"), 1)
                for j in range(4):
                    ins = act.activation(qkT2[:, 2 * j:2 * j + 2, :], ps[:, 4 + j, :].rearrange("p (a b) -> p a b", a=2), ACT.Copy,
                                         scale=sbgain[:, j // 2:j // 2 + 1])
                ins.then_inc(sem("sbT_ready"), 1)

            def stick(k):
                if 1 <= k <= BATCHES:
                    act.wait_ge(sem("logw_ready"), k)
                    act.activation(wT[:, (k - 1) % 2, :, :], zm[:, (k - 1) % 2, :, :], ACT.Exp).then_inc(sem("w_ready"), 1)
                if k < BATCHES:
                    z, e = zm[:, k % 2, :, :], sp_[:, k % 2, :, :]
                    act.wait_ge(sem("zm_ready"), k + 1)
                    link(act.activation(e, z, ACT.Abs))
                    link(act.activation(e, e, ACT.Exp, scale=-1.0))
                    act.activation(e, e, ACT.Ln, bias=1.0).then_inc(sem("sp_ln"), 1)
                if k >= 2:
                    act.wait_ge(sem("osb_done"), k - 1)
                    act.activation(osbT[:, k - 2, :], ps[:, 3, 0:S], ACT.Copy).then_inc(sem("osb_evac"), 1)

            x4 = [xbuf[:, i, :, :].rearrange("p h (c r) -> p (h c) r", r=HC) for i in range(2)]

            def pairs(j0):
                if j0 == 0:
                    act.wait_ge(sem("f_ready"), 1)
                    act.activation(hf, hf, ACT.Ln).then_inc(sem("logf_ready"), 1)
                    act.wait_ge(sem("bb_ready"), 1)
                    act.activation(qe, bb, ACT.Exp)
                    act.activation(dec[:].rearrange("p h c -> p (h c)"), bb.rearrange("p h (c r) -> p (h c) r", r=HC)[:, :, HC - 1], ACT.Exp).then_inc(sem("eb_ready"), 1)
                    act.wait_ge(sem("left_ready"), 1)
                    act.activation(keT, keT, ACT.Exp).then_inc(sem("eleft_ready"), 1)
                for j in range(j0, j0 + 2):
                    act.wait_ge(sem("diff_ready"), j + 1)
                    act.activation(x4[j % 2][:, :, j:HC], x4[j % 2][:, :, j:HC], ACT.Exp).then_inc(sem("diff_exp"), 1)

            def turn_ke(_):
                act.wait_ge(sem("ke_turned"), 1)
                for b in range(NB):
                    ins = act.activation(ket[:, b, :, :], ps[:, 6 + b, :].rearrange("p (a b) -> p a b", a=HH), ACT.Copy)
                ins.then_inc(sem("ket_ready"), 1)

            do = {"turn_sb": turn_sb, "stick": stick, "pairs": pairs, "turn_ke": turn_ke}
            for what, n, *g in plan2:
                if what == "half":
                    leave2(n, g[0])
                    for half in next_half(n, g[0], N2):
                        upper_parts(act, *half)
                elif what in do:
                    do[what](n)
            act.wait_ge(sem("read_done"), NHC - 1)
            for b in range(NB):
                act.activation(osq[:, :, b, :], ps[:, 4 + b, :].rearrange("p (a b) -> p a b", a=HH), ACT.Square).then_inc(sem("osq_ready"), 1)
            act.wait_ge(sem("oms_ready"), 2)
            act.activation(orr, orr, ACT.Sqrt).then_inc(sem("oroot"), 1)
            norm_act(act, 3, "x4_ready", 4, NFFN)
            for c in range(NFF):
                act.wait_ge(sem("unit_used"), ffn_unit[c] + 2)
                if c >= 2:
                    act.wait_ge(sem("hid_ready"), c - 1)
                act.activation(silu[:, c % 2, :, :], ps[:, (2 * c) % 4, :].rearrange("p (a b) -> p a b", a=2), ACT.Silu).then_inc(sem("silu_ready"), 1)
                for g in range(2):
                    if c + 1 < NFF:
                        upper_parts(act, ffn_chunk[c + 1], g)

        @block.vector
        def _(dve):
            step = [0]

            def link(ins):
                step[0] += 1
                ins.then_inc(sem("dve_step"), 1)
                dve.wait_ge(sem("dve_step"), step[0])

            norm_dve(dve, link, 0)
            dve.wait_ge(sem("small_loaded"), NSMALL * 16)
            link(dve.tensor_copy(posf[:], pos_i[:]))
            for b in range(NB):
                link(dve.tensor_scalar(ang[:, 0, b, :], freq[:], posf[:, b:b + 1], None, ALU.mult))
            flat = [ang[:, k, :, :].rearrange("p a b -> p (a b)") for k in range(4)]
            link(dve.tensor_scalar(flat[1], flat[0], 1.0 / (2 * np.pi), MAGIC, ALU.mult, ALU.add))
            link(dve.tensor_scalar(flat[1], flat[1], MAGIC, None, ALU.subtract))
            for part in TWO_PI_PARTS:
                link(dve.scalar_tensor_tensor(out=flat[0], in0=flat[1], scalar=-part, in1=flat[0], op0=ALU.mult, op1=ALU.add))
            link(dve.tensor_scalar(flat[1], flat[0], np.pi / 2, None, ALU.add))
            link(dve.tensor_scalar(flat[2], flat[1], np.pi, -2 * np.pi, ALU.is_gt, ALU.mult))
            link(dve.tensor_tensor(flat[1], flat[1], flat[2], ALU.add))
            link(dve.tensor_scalar(flat[2], flat[1], PI_IN, -PI_IN, ALU.min, ALU.max))
            dve.tensor_scalar(flat[3], flat[0], PI_IN, -PI_IN, ALU.min, ALU.max).then_inc(sem("angles"), 1)
            dve.wait_ge(sem("p1_evac"), 6)
            NH = AH + AKV
            for b in range(NB):
                qk = p1[:, b, 0:NH * AD]
                qk3 = qk.rearrange("p (h d) -> p h d", d=AD)
                sq3 = sq.rearrange("p (h d) -> p h d", d=AD)
                link(dve.tensor_tensor(sq, qk, qk, ALU.mult))
                link(dve.tensor_reduce(hst[:, 0, :], sq3, AX, ALU.add))
                dve.tensor_scalar(hst[:, 0, :], hst[:, 0, :], 1.0 / AD, EPS, ALU.mult, ALU.add).then_inc(sem("qk_ms"), 1)
                dve.wait_ge(sem("qk_root"), b + 1)
                link(dve.reciprocal(hst[:, 2, :], hst[:, 1, :]))
                link(dve.tensor_tensor(qk3, qk3, hst[:, 2, :].unsqueeze(2).broadcast_to([P, NH, AD]), ALU.mult))
                dve.tensor_tensor(qk3[:, 0:AH, :], qk3[:, 0:AH, :], qkgain[:, 0:1, :].broadcast_to([P, AH, AD]), ALU.mult)
                link(dve.tensor_tensor(qk3[:, AH:NH, :], qk3[:, AH:NH, :], qkgain[:, 1:2, :].broadcast_to([P, AKV, AD]), ALU.mult))
                if b == 0:
                    dve.wait_ge(sem("sines"), 1)
                x1, x2 = qk3[:, :, 0:RH], qk3[:, :, RH:ROPE]
                co = cs[:, 0, b:b + 1, :].broadcast_to([P, NH, RH])
                si = cs[:, 1, b:b + 1, :].broadcast_to([P, NH, RH])
                dve.tensor_tensor(rt[:, 0, :, :], x1, co, ALU.mult)
                dve.tensor_tensor(rt[:, 1, :, :], x2, si, ALU.mult)
                dve.tensor_tensor(rt[:, 2, :, :], x2, co, ALU.mult)
                link(dve.tensor_tensor(rt[:, 3, :, :], x1, si, ALU.mult))
                dve.tensor_tensor(x1, rt[:, 0, :, :], rt[:, 1, :, :], ALU.subtract)
                link(dve.tensor_tensor(x2, rt[:, 2, :, :], rt[:, 3, :, :], ALU.add))
                kk = p1[:, b, AK0:AV0].rearrange("p (h d) -> p h d", d=AD)
                kdv = kd[:, b, :].rearrange("p (h two d) -> p h two d", two=2, d=AD)
                dve.tensor_copy(kdv[:, :, 0, :], kk)
                dve.tensor_copy(kdv[:, :, 1, :], kk).then_inc(sem("qk_rotated"), 1)
            def scores_in(k):
                b, q = k // 4, k % 4
                nk = P * (b + 1)
                m3 = mask_band[:, 1 - b:2, :].rearrange("p a b -> p (a b)").unsqueeze(1)
                x, a_ = sm[:, k % 2, :, :], am[:, k % 2, :, :]
                dve.wait_ge(sem("scores"), k + 1)
                if k >= 2:
                    dve.wait_ge(sem("probs_turned"), k - 1)
                for i in range(2):
                    ins = dve.scalar_tensor_tensor(out=x[:, i::2, 0:nk], in0=ps[:, 4 + i, :].rearrange("p (a b) -> p a b", a=2)[:, :, 0:nk],
                                                   scalar=AD ** -0.5, in1=m3.broadcast_to([P, 2, nk]), op0=ALU.mult, op1=ALU.add)
                ins.then_inc(sem("scores_read"), 1)
                dve.wait_ge(sem("scores_read"), k + 1)
                link(dve.tensor_reduce(a_[:, 0, :], x[:, :, 0:nk], AX, ALU.max))
                snk = sinks[:, 4 * q:4 * q + 4]
                link(dve.tensor_tensor(a_[:, 0, :], a_[:, 0, :], snk, ALU.max))
                dve.tensor_scalar(a_[:, 1, :], a_[:, 0, :], -1.0, None, ALU.mult)
                dve.tensor_tensor(a_[:, 3, :], snk, a_[:, 0, :], ALU.subtract).then_inc(sem("row_max"), 1)
                dve.wait_ge(sem("exps"), k + 1)
                link(dve.tensor_tensor(a_[:, 5, :], a_[:, 2, :], a_[:, 4, :], ALU.add))
                link(dve.reciprocal(a_[:, 0, :], a_[:, 5, :]))
                dve.tensor_tensor(x[:, :, 0:nk], x[:, :, 0:nk], a_[:, 0, :].unsqueeze(2).broadcast_to([P, 4, nk]),
                                  ALU.mult).then_inc(sem("probs"), 1)

            for k in range(GROUPS):
                scores_in(k)
            mif = p1[:, :, AV0 + AKV * AD:AV0 + AKV * AD + 2 * MH]
            for k in range(2):
                ins = dve.tensor_tensor(gt[:, k, :, :], mif[:, :, k * MH:(k + 1) * MH], ifbias[:, k:k + 1, :].broadcast_to([P, NB, MH]), ALU.add)
            ins.then_inc(sem("gates_raw"), 1)
            dve.wait_ge(sem("gates_tanh"), 1)
            dve.tensor_scalar(gt[:, 0:2, :, :], gt[:, 2:4, :, :], CAP, None, ALU.mult).then_inc(sem("gates_cap"), 1)
            dve.wait_ge(sem("gates_soft"), 1)
            dve.tensor_scalar(gt[:, 1, :, :], gt[:, 3, :, :], -1.0, None, ALU.mult).then_inc(sem("gates_tok"), 1)
            dve.wait_ge(sem("rows_gates"), 1)
            link(dve.tensor_tensor_scan(rows[:, 2, :], ones[0:MH, 0:1].broadcast_to([MH, S]), rows[:, 1, :], 0.0, ALU.mult, ALU.add))
            link(dve.tensor_tensor(rows[:, 3, :], rows[:, 0, :], rows[:, 2, :], ALU.subtract))
            link(dve.tensor_tensor_scan(rows[:, 4, :], rows[:, 3, :], rows[:, 3, :], 0.0, ALU.max, ALU.max))
            link(dve.tensor_tensor(rows[:, 5, :], rows[:, 2, :], rows[:, 4, :], ALU.add))
            dve.tensor_scalar(rows[:, 4, :], rows[:, 4, :], -1.0, None, ALU.mult).then_inc(sem("m_rows"), 1)
            dve.wait_ge(sem("m_spread"), 1)
            mi3 = mask_inc[:].unsqueeze(1)
            for j in range(4):
                bank = ps[:, 4 + j, :].rearrange("p (h b c) -> p h b c", h=2, b=2)
                dve.tensor_tensor(wl[:, 2 * j:2 * j + 2, 0, :], bank[:, :, 0, :], mi3.broadcast_to([P, 2, P]), ALU.add)
                ins = dve.tensor_tensor(wl[:, 2 * j:2 * j + 2, 2, :], bank[:, :, 1, :], mi3.broadcast_to([P, 2, P]), ALU.add)
            ins.then_inc(sem("wl_masked"), 1)

            def mix(k):
                dve.wait_ge(sem("br_done"), k + 1)
                bank = ps[:, k % LB, :].rearrange("p (a b) -> p a b", a=2)
                t = slice(2 * (k % 4), 2 * (k % 4) + 2)
                if k < 4:
                    dve.wait_ge(sem("p1_evac"), 2 * NW1)
                    dve.tensor_tensor(mixT[:, t, :], bank, sga[:, t, :], ALU.mult).then_inc(sem("br_evac"), 1)
                else:
                    link(dve.tensor_tensor(tmpT[:, t, :], bank, sgm[:, t, :], ALU.mult))
                    dve.tensor_tensor(mixT[:, t, :], mixT[:, t, :], tmpT[:, t, :], ALU.add).then_inc(sem("br_evac"), 1)

            mixed = 0
            for what, n, *g in plan1:
                if what == "half" and n >= NW1:
                    mix(mixed)
                    mixed += 1
                if what == "memory" and n < MH:
                    h = n
                    dve.wait_ge(sem("wl_ready"), h + 1)
                    dve.wait_ge(sem("ml_qk"), h + 1)
                    if h >= 2:
                        dve.wait_ge(sem("num_done"), h - 1)
                    dve.scalar_tensor_tensor(out=cw[:, h % 2, :], in0=ps[:, 4 + h % 2, 0:3 * P], scalar=MQ ** -0.5,
                                             in1=wl[:, h, :, :].rearrange("p a b -> p (a b)"), op0=ALU.mult,
                                             op1=ALU.mult).then_inc(sem("cw_ready"), 1)
            dve.wait_ge(sem("num_evac"), MH)
            dn = hraw[:, :, :, MV]
            link(dve.scalar_tensor_tensor(out=den[:, 0, :, :], in0=dn, scalar=-1.0, in1=dn, op0=ALU.mult, op1=ALU.max))
            link(dve.tensor_tensor(den[:, 0, :, :], den[:, 0, :, :], em[:], ALU.max))
            link(dve.reciprocal(den[:, 1, :, :], den[:, 0, :, :]))
            for b in range(NB):
                link(dve.tensor_tensor(hs[:, b, :, :], hraw[:, b, :, 0:MV], den[:, 1, b, :].unsqueeze(2).broadcast_to([P, MH, MV]), ALU.mult))
            link(dve.tensor_tensor(hsq, hs, hs, ALU.mult))
            link(dve.tensor_reduce(den[:, 0, :, :], hsq, AX, ALU.add))
            dve.tensor_scalar(den[:, 1, :, :], den[:, 0, :, :], 1.0 / MV, EPS, ALU.mult, ALU.add).then_inc(sem("hm_ms"), 1)
            dve.wait_ge(sem("hm_root"), 1)
            link(dve.reciprocal(den[:, 0, :, :], den[:, 2, :, :]))
            for b in range(NB):
                link(dve.tensor_tensor(hs[:, b, :, :], hs[:, b, :, :], den[:, 0, b, :].unsqueeze(2).broadcast_to([P, MH, MV]), ALU.mult))
            dve.tensor_tensor(hs, hs, mo.rearrange("p b (h v) -> p b h v", h=MH), ALU.mult).then_inc(sem("hm_tok"), 1)
            for k in range(4, 8):
                mix(k)
            for c in range(2):
                for b in range(NB):
                    dve.wait_ge(sem("out_done"), 2 * c + b + 1)
                    dve.tensor_tensor(xres[:, b, c * CW:(c + 1) * CW], xres[:, b, c * CW:(c + 1) * CW],
                                      ps[:, (2 * c + b) % LB, :], ALU.add).then_inc(sem("x2_ready"), 1)

            norm_dve(dve, link, 1)
            def top16(values, vals, where, rows):
                for half in range(2):
                    e = slice(8 * half, 8 * half + 8)
                    for r in range(rows):
                        ins = dve.max(vals[r][:, e], values[r])
                    link(ins)
                    for r in range(rows):
                        ins = dve.max_index(where[r][:, e], vals[r][:, e], values[r])
                    link(ins)
                    if half == 0:
                        for r in range(rows):
                            ins = dve.match_replace(values[r], vals[r][:, e], values[r], -3.0e38)
                        link(ins)

            gate4 = gates[:].rearrange("p (r h k) -> p r h k", h=PR, k=TOPK)

            def route(r):
                b, h0 = r // NR, r % NR * PR
                dve.wait_ge(sem("scr_ready"), 2 * b + h0 // 4 + 1)
                hp = [(h, p) for h in range(PR) for p in range(2)]
                top16([scr[b][:, h0 + h, p, :] for h, p in hp], [tv[:, h, p, :] for h, p in hp], [ti[:, h, p, :] for h, p in hp], len(hp))
                flat = "p a b c -> p (a b c)"
                link(dve.tensor_copy(tif.rearrange(flat), ti.rearrange(flat)))
                cand = scr[b][:, h0:h0 + PR, :, :].rearrange("p h q k -> p h (q k)")
                c4 = cand.rearrange("p h (i j) -> p h i j", i=TOPK)
                link(dve.tensor_tensor(c4, tv[:, :, 0, :].unsqueeze(3).broadcast_to([P, PR, TOPK, TOPK]),
                                       tv[:, :, 1, :].unsqueeze(2).broadcast_to([P, PR, TOPK, TOPK]), ALU.add))
                top16([cand[:, h, :] for h in range(PR)], [bv[:, h, :] for h in range(PR)], [bp[:, h, :] for h in range(PR)], PR)
                bpf = bp.rearrange("p a b -> p (a b)")
                dve.tensor_scalar(bij[:, 0, :], bpf, 4, None, ALU.logical_shift_right)
                link(dve.tensor_scalar(bij[:, 1, :], bpf, TOPK - 1, None, ALU.bitwise_and))
                link(dve.tensor_copy(bijf.rearrange("p a b -> p (a b)"), bij.rearrange("p a b -> p (a b)")))
                for p in range(2):
                    hot3 = hot.rearrange("p h k i -> p (h k) i")
                    link(dve.tensor_tensor(hot3, bijf[:, p, :].unsqueeze(2).broadcast_to([P, PR * TOPK, TOPK]),
                                           iota16[:].unsqueeze(1).broadcast_to([P, PR * TOPK, TOPK]), ALU.is_equal))
                    link(dve.tensor_tensor(picked, hot, tif[:, :, p, :].unsqueeze(2).broadcast_to([P, PR, TOPK, TOPK]), ALU.mult))
                    link(dve.tensor_reduce(exf[:, p, :], picked.rearrange("p h k i -> p (h k) i"), AX, ALU.add))
                link(dve.scalar_tensor_tensor(out=exf[:, 2, :], in0=exf[:, 0, :], scalar=float(NKEY), in1=exf[:, 1, :], op0=ALU.mult, op1=ALU.add))
                dve.tensor_copy(idx[:, b, h0 * TOPK:(h0 + PR) * TOPK], exf[:, 2, :]).then_inc(sem("routed"), 1)
                dve.tensor_tensor(gate4[:, r, :, :], bv, bv[:, :, 0:1].broadcast_to([P, PR, TOPK]), ALU.subtract).then_inc(sem("best_shifted"), 1)

            def finish_gates(r):
                dve.wait_ge(sem("best_exp"), r + 1)
                link(dve.tensor_reduce(gsum[:, 0, :], gate4[:, r, :, :], AX, ALU.add))
                link(dve.reciprocal(gsum[:, 1, :], gsum[:, 0, :]))
                link(dve.tensor_tensor(gate4[:, r, :, :], gate4[:, r, :, :], gsum[:, 1, :].unsqueeze(2).broadcast_to([P, PR, TOPK]), ALU.mult))

            dve.wait_ge(sem("masks2_ready"), 1)
            dve.memset(dots[:], 0.0).then_inc(sem("drow_free"), DSLOTS)
            dve.wait_ge(sem("drow_free"), DSLOTS)
            route(0)
            route(1)
            for r in range(NB * NR):
                b = r // NR
                finish_gates(r)
                for o in range(PR):
                    g = r * PR + o
                    for k in range(TOPK):
                        dve.wait_ge(sem(f"drow{k % DSLOTS}"), g * 32 + (16 + 16 * (k // DSLOTS)))
                        row = rows_d[:, k % DSLOTS, :]
                        dve.tensor_tensor_reduce(row, row, h2[:, b, :], 1.0, 0.0, ALU.mult, ALU.add,
                                                 dots[:, o, k:k + 1]).then_inc(sem("drow_free"), 1)
                    dve.wait_ge(sem("gelu_done"), g + 1)
                    dve.tensor_tensor(wgt[:, o, :], gelu[:, o, :], gate4[:, r, o, :], ALU.mult).then_inc(sem("wgt_ready"), 1)
                if r + 2 < NB * NR:
                    route(r + 2)

            norm_dve(dve, link, 2)
            link(dve.tensor_tensor(lbs[:, 0, :], lbt[:, 0, :], lbt[:, 1, :], ALU.max))
            dve.tensor_tensor(lbs[:, 1:3, :], lbt[:], lbs[:, 0:1, :].broadcast_to([P, 2, HH]), ALU.subtract).then_inc(sem("lb_shifted"), 1)
            dve.wait_ge(sem("p2_evac"), 6)
            for b in range(NB):
                qk = p2[:, b, 0:2 * SBW]
                qk3 = qk.rearrange("p (h d) -> p h d", d=SD)
                sqs = zm.rearrange("p a b c -> p (a b c)")[:, 0:2 * SBW]
                link(dve.tensor_tensor(sqs, qk, qk, ALU.mult))
                link(dve.tensor_reduce(hst2[:, 0, :], sqs.rearrange("p (h d) -> p h d", d=SD), AX, ALU.add))
                dve.tensor_scalar(hst2[:, 0, :], hst2[:, 0, :], 1.0 / SD, EPS, ALU.mult, ALU.add).then_inc(sem("sb_ms"), 1)
                dve.wait_ge(sem("sb_root"), b + 1)
                link(dve.reciprocal(hst2[:, 2, :], hst2[:, 1, :]))
                ins = dve.tensor_tensor(qk3, qk3, hst2[:, 2, :].unsqueeze(2).broadcast_to([P, 2 * SH, SD]), ALU.mult)
                if b == 0:
                    link(ins)
                else:
                    ins.then_inc(sem("sb_normed"), 1)
            ms3 = mask_str[:].unsqueeze(1).broadcast_to([P, 2, P])
            sc = SD ** -0.5
            for k in range(BATCHES + 1):
                if k < BATCHES:
                    z = zm[:, k % 2, :, :]
                    dve.wait_ge(sem("z_done"), k + 1)
                    if k >= 2:
                        dve.wait_ge(sem("w_ready"), k - 1)
                    for c0 in (0, S):
                        dve.scalar_tensor_tensor(out=z[:, :, c0:c0 + P], in0=ps[:, 4:6, c0:c0 + P], scalar=sc, in1=ms3, op0=ALU.mult, op1=ALU.add)
                    dve.tensor_scalar(z[:, :, P:S], ps[:, 4:6, P:S], sc, None, ALU.mult).then_inc(sem("zm_ready"), 1)
                if k >= 1:
                    z = zm[:, (k - 1) % 2, :, :]
                    dve.wait_ge(sem("rest_done"), k)
                    dve.tensor_tensor(z, z, ps[:, 6:8, 0:3 * P], ALU.subtract).then_inc(sem("logw_ready"), 1)
                if k < BATCHES:
                    z, e = zm[:, k % 2, :, :], sp_[:, k % 2, :, :]
                    dve.wait_ge(sem("sp_ln"), k + 1)
                    fz = "p a b -> p (a b)"
                    dve.scalar_tensor_tensor(out=e.rearrange(fz), in0=z.rearrange(fz), scalar=0.0, in1=e.rearrange(fz), op0=ALU.max, op1=ALU.add).then_inc(sem("sp_ready"), 1)
            dve.wait_ge(sem("lb_exp"), 1)
            link(dve.tensor_tensor(lbs[:, 3, :], lbs[:, 1, :], lbs[:, 2, :], ALU.add))
            link(dve.reciprocal(lbs[:, 4, :], lbs[:, 3, :]))
            link(dve.tensor_tensor(lbs[:, 0, :], lbs[:, 1, :], lbs[:, 4, :], ALU.mult))
            link(dve.tensor_scalar(lbs[:, 3, :], lbs[:, 0, :], -1.0, 1.0, ALU.mult, ALU.add))
            dve.wait_ge(sem("osb_done"), BATCHES)
            dve.wait_ge(sem("p2_evac"), 14)
            for h in range(HH):
                ins = dve.tensor_scalar(hf[:, h, :], hf[:, h, :], lbs[:, 3, h:h + 1], lbs[:, 0, h:h + 1], ALU.mult, ALU.add)
            link(ins)
            fl = "p a b -> p (a b)"
            dve.tensor_scalar(key.rearrange(fl), hf.rearrange(fl), -1.0, 1.0, ALU.mult, ALU.add).then_inc(sem("f_ready"), 1)
            for o in range(2):
                ins = dve.tensor_scalar(vpar[:, o, :, :].rearrange(fl), hv.rearrange(fl), par[:, o:o + 1], None, ALU.mult)
            ins.then_inc(sem("vpar_ready"), 1)
            dve.memset(xbuf, 0.0)
            dve.wait_ge(sem("logf_ready"), 1)
            dve.tensor_tensor_scan(bb.rearrange(fl), restart[:], hf.rearrange(fl), 0.0, ALU.mult, ALU.add).then_inc(sem("bb_ready"), 1)
            dve.wait_ge(sem("bb_ready"), 1)
            b4 = bb.rearrange("p h (c r) -> p (h c) r", r=HC)
            k4 = keT.rearrange("p h (c r) -> p (h c) r", r=HC)
            key4 = key.rearrange("p h (c r) -> p (h c) r", r=HC)
            q4 = hq.rearrange("p h (c r) -> p (h c) r", r=HC)
            dve.tensor_tensor(k4, b4[:, :, HC - 1:HC].broadcast_to([P, HH * NHC, HC]), b4, ALU.subtract).then_inc(sem("left_ready"), 1)
            dve.wait_ge(sem("eb_ready"), 1)
            dve.tensor_tensor(qe, qe, hq, ALU.mult)
            dve.wait_ge(sem("eleft_ready"), 1)
            dve.tensor_tensor(keT, keT, key, ALU.mult).then_inc(sem("keT_ready"), 1)
            x4 = [xbuf[:, i, :, :].rearrange("p h (c r) -> p (h c) r", r=HC) for i in range(2)]

            def diff(j):
                if j >= 2:
                    dve.wait_ge(sem("pairs_summed"), j - 1)
                dve.tensor_tensor(x4[j % 2][:, :, j:HC], b4[:, :, j:HC], b4[:, :, j:j + 1].broadcast_to([P, HH * NHC, HC - j]),
                                  ALU.subtract).then_inc(sem("diff_ready"), 1)

            diff(0)
            for j in range(HC):
                if j + 1 < HC:
                    diff(j + 1)
                x = x4[j % 2][:, :, j:HC]
                dve.wait_ge(sem("diff_exp"), j + 1)
                link(dve.tensor_tensor(x, x, q4[:, :, j:HC], ALU.mult))
                dve.tensor_tensor(x, x, key4[:, :, j:j + 1].broadcast_to([P, HH * NHC, HC - j]), ALU.mult).then_inc(sem("pairs_ready"), 1)
            dve.wait_ge(sem("pairs_summed"), HC)
            for c in range(2):
                ins = dve.tensor_tensor(AT[:, 2 * c:2 * c + 2, :, :].rearrange("p h b t -> p (h b) t"), ps[:, 4 + c, :].rearrange("p (a b) -> p a b", b=P),
                                        m16[:].unsqueeze(1).broadcast_to([P, 4, P]), ALU.mult)
            ins.then_inc(sem("AT_ready"), 1)
            for c in range(NHC - 1):
                dve.wait_ge(sem("inc_done"), c + 1)
                if c >= 3:
                    dve.wait_ge(sem("read_done"), c - 2)
                for h in range(HH):
                    new = state[:, (c + 1) % 3, h, :]
                    inc = ps[:, 6 + c % 2, h * P:(h + 1) * P]
                    if c == 0:
                        ins = dve.tensor_copy(new, inc)
                    else:
                        ins = dve.scalar_tensor_tensor(out=new, in0=state[:, c % 3, h, :], scalar=dec[:, h, c:c + 1], in1=inc, op0=ALU.mult, op1=ALU.add)
                ins.then_inc(sem("state_ready"), 1)
                dve.wait_ge(sem("state_ready"), c + 1)
            dve.wait_ge(sem("osq_summed"), 1)
            for b in range(NB):
                dve.tensor_scalar(orr[:, :, b, :], ps[:, 6 + b, :].rearrange("p (a b) -> p a b", a=HH), 1.0 / HV, EPS, ALU.mult, ALU.add).then_inc(sem("oms_ready"), 1)
            dve.wait_ge(sem("oroot"), 1)
            link(dve.reciprocal(orr, orr))
            for b in range(NB):
                ins = dve.scalar_tensor_tensor(out=ohgT[:, :, b * P:(b + 1) * P], in0=ps[:, 4 + b, :].rearrange("p (a b) -> p a b", a=HH), scalar=hgain[:, 0:1],
                                               in1=orr[:, :, b, :], op0=ALU.mult, op1=ALU.mult)
            link(ins)
            dve.tensor_tensor(ohgT, ohgT, hg, ALU.mult).then_inc(sem("ohg_ready"), 1)
            for k in range(8):
                dve.wait_ge(sem("br2_done"), k + 1)
                bank = ps[:, k % LB, :]
                dve.tensor_tensor(mixT2[:, k, :], bank[:, 0:S], sg2[:, k, :], ALU.mult)
                link(dve.tensor_tensor(tmp2[:, 0, :], bank[:, S:2 * S], sg2[:, KT + k, :], ALU.mult))
                dve.tensor_tensor(mixT2[:, k, :], mixT2[:, k, :], tmp2[:, 0, :], ALU.add).then_inc(sem("br2_evac"), 1)
                dve.wait_ge(sem("br2_evac"), k + 1)
            for c in range(2):
                for b in range(NB):
                    dve.wait_ge(sem("out2_done"), 2 * c + b + 1)
                    dve.tensor_tensor(xres[:, b, c * CW:(c + 1) * CW], xres[:, b, c * CW:(c + 1) * CW],
                                      ps[:, (2 * c + b) % LB, :], ALU.add).then_inc(sem("x4_ready"), 1)
            norm_dve(dve, link, 3)
            for c in range(NFF):
                dve.wait_ge(sem("unit_used"), ffn_unit[c] + 4)
                dve.wait_ge(sem("silu_ready"), c + 1)
                if c >= 4:
                    dve.wait_ge(sem("down_done"), (c - 4) // 2 + 1)
                dve.tensor_tensor(hid[:, c % 4, :, :], silu[:, c % 2, :, :], ps[:, (2 * c + 1) % 4, :].rearrange("p (a b) -> p a b", a=2),
                                  ALU.mult).then_inc(sem("hid_ready"), 1)
            dve.wait_ge(sem("down_done"), (NFF + 1) // 2)
            for b in range(NB):
                for c in range(2):
                    dve.tensor_tensor(xres[:, b, c * CW:(c + 1) * CW], xres[:, b, c * CW:(c + 1) * CW],
                                      ps[:, 4 + 2 * b + c, :], ALU.add).then_inc(sem("x5_ready"), 1)


def lay_out(inp):
    c = np.ascontiguousarray
    f = lambda k: np.asarray(inp[k])
    col = lambda v: v.reshape(KT, P).T
    rep = lambda v: np.broadcast_to(v, (P,) + v.shape)
    return {
        "x": c(f("x")[0]),
        "w_in": c(f("w_in")[0]),
        "w_branch_attn": c(f("w_branch_attn")[0]),
        "w_branch_mlstm": c(f("w_branch_mlstm")[0]),
        "w_out": c(f("w_out")[0]),
        "gcol": c(np.stack([col(f(k)[0]) for k in ("norm1_gain", "norm2_gain", "norm1_g_2", "norm2_g_2")], 1)),
        "mlgain": c(col(f("ml_out_norm_gain")[0])),
        "qkgain": c(rep(np.stack([f("q_norm_gain")[0], f("k_norm_gain")[0]]))),
        "sinks": c(rep(f("attn_sinks")[0])),
        "ifbias": c(rep(np.stack([f("ml_i_bias")[0], f("ml_f_bias")[0]]))),
        "pos": c(f("positions").reshape(NB, P).T.astype(np.int32)),
        "freq": c(rep(inv_freq())),
        "peer_w_query": c(f("peer_w_query")[0]),
        "sub_keys": c(f("peer_sub_keys")[0].transpose(1, 3, 0, 2).reshape(P, PH, NKEY)),
        "n2row": c(rep(f("norm2_gain")[0])),
        "peer_down": c(f("peer_down")[0]),
        "peer_up": c(f("peer_up")[0]),
        "w_in_2": c(f("w_in_2")[0]),
        "w_branch_2": c(f("w_branch_2")[0]),
        "w_out_2": c(f("w_out_2")[0]),
        "w_ffn_gate_2": c(f("w_ffn_gate_2")[0]),
        "w_ffn_up_2": c(f("w_ffn_up_2")[0]),
        "w_ffn_down_2": c(f("w_ffn_down_2")[0]),
        "sbgain": c(np.stack([np.tile(f(k)[0], 2) for k in ("q_norm_g_2", "k_norm_g_2")], 1)),
        "hgain": c(f("hg_norm_g_2")[0].reshape(P, 1)),
        "lbt": c(f("lb_table_2").reshape(2, HH, HK).transpose(2, 0, 1)),
    }


def kernel(**inputs):
    import concourse.bacc as bacc
    from concourse.bass_utils import run_bass_kernel_spmd

    nc = bacc.Bacc("TRN2", target_bir_lowering=False, num_devices=1)
    arrays = lay_out(inputs)
    aps = {k: nc.dram_tensor(k + "_in", v.shape, mybir.dt.from_np(v.dtype), kind="ExternalInput").ap() for k, v in arrays.items()}
    out = nc.dram_tensor("out", (S, D), F32, kind="ExternalOutput").ap()
    build(nc, aps, out)
    r = run_bass_kernel_spmd(nc, [{k + "_in": v for k, v in arrays.items()}], core_ids=[0])
    return r.results[0]["out"].reshape(1, S, D)
```

```python
from contextlib import ExitStack

import numpy as np
import concourse.bass as bass
from concourse import mybir

F32 = mybir.dt.float32
R32 = mybir.dt.float32r
U32 = mybir.dt.uint32
I32 = mybir.dt.int32
ALU = mybir.AluOpType
ACT = mybir.ActivationFunctionType
AX = mybir.AxisListType.X

P = 128
S = 256
NB = S // P
D = 1024
KT = D // P
EPS = 1e-6
NEG = -1e30

AH, AKV, AD = 16, 2, 64
ROPE = AD // 4
RH = ROPE // 2
ROPE_THETA = 500000.0
MH, MQ, MV = 8, 64, 128
CAP = 15.0
PH, NKEY, TOPK = 8, 128, 16
PR = 2
NR = PH // PR
AQ0 = 0
AK0 = AQ0 + AH * AD
AV0 = AK0 + AKV * AD
MQ0 = AV0 + AKV * AD
MK0 = MQ0 + MH * MQ
MV0 = MK0 + MH * MQ
MI0 = MV0 + MH * MV
MF0 = MI0 + MH
MO0 = MF0 + MH
GA0 = MO0 + MH * MV
GM0 = GA0 + D
W1N = GM0 + D

SH, SD = 8, 64
HH, HK, HV = 4, 128, 128
HC = 16
NHC = S // HC
SBW = SH * SD
HGW = HH * HV
FF = -(-8 * D // (3 * 256)) * 256
W2N = 3 * SBW + 2 * HH * HK + 2 * HGW + 2 * D

CW = 512
LB = 3
DSLOTS = 8
HALF = CW // 2
SLOTS = 2
KU = KT // 2

TWO_PI_PARTS = (6.28125, 0.0019352436065673828, 6.357301884918343e-08)
MAGIC = 12582912.0
PI_IN = 3.1415925


def inv_freq():
    return (np.float32(ROPE_THETA) ** (-np.arange(0, ROPE, 2, dtype=np.float32) / np.float32(ROPE))).astype(np.float32)


def build(nc, a, out):
    ctx = ExitStack()
    with ctx:
        def sb(name, shape, dt=F32):
            return ctx.enter_context(nc.sbuf_tensor(name, shape, dt))

        made = {}

        def sem(name):
            if name not in made:
                made[name] = ctx.enter_context(nc.semaphore(name))
            return made[name]

        NSMALL = 10
        with ExitStack() as shared:
            rows_u = shared.enter_context(nc.sbuf_tensor("rows_u", [P, TOPK, D], F32))
        ring = sb("ring", [P, SLOTS, KT, CW])
        w_hi = sb("w_hi", [P, 2, KT, HALF], R32)
        w_lo = sb("w_lo", [P, 2, KT, HALF], R32)
        xres = sb("xres", [P, NB, D])
        with ExitStack() as shared:
            xn = shared.enter_context(nc.sbuf_tensor("xn", [P, NB, D], F32))
        hT_lo = sb("hT_lo", [P, KT, S], R32)
        hT_hi = sb("hT_hi", [P, KT, S], R32)
        with ExitStack() as shared:
            arena_r = shared.enter_context(nc.sbuf_tensor("arena_r", [P, 23808], R32))
        arena = sb("arena", [P, 23808])
        ps = ctx.enter_context(nc.psum_tensor("ps", [P, 8, 512], F32))

        class Area:
            def __init__(self, at=0):
                self.at = at

            def take(self, *shape, dt=F32):
                n = int(np.prod(shape))
                v = (arena_r if dt == R32 else arena)[:, self.at:self.at + n]
                self.at += n
                assert self.at <= 23808, self.at
                if dt not in (F32, R32):
                    v = v.bitcast(dt)
                if len(shape) > 1:
                    names = "abcdef"[:len(shape)]
                    v = v.rearrange(f"p ({' '.join(names)}) -> p {' '.join(names)}",
                                    **{k: s for k, s in zip(names[1:], shape[1:])})
                return v

        ident = sb("ident", [P, P])
        ones = sb("ones", [P, P])
        mask_band = sb("mask_band", [P, NB, P])
        mask_inc = sb("mask_inc", [P, P])
        sel = sb("sel", [P, MH, P])
        gcol = sb("gcol", [P, 4, KT])
        mlgain = sb("mlgain", [P, KT])
        qkgain = sb("qkgain", [P, 2, AD])
        sinks = sb("sinks", [P, AH])
        ifbias = sb("ifbias", [P, 2, MH])
        pos_i = sb("pos_i", [P, NB], I32)
        freq = sb("freq", [P, RH])
        ss = sb("ss", [P, NB])
        ms = sb("ms", [P, NB])
        sd = sb("sd", [P, NB])
        rr = sb("rr", [P, NB])

        one = Area()
        p1 = one.take(NB, AH * AD + 2 * AKV * AD + 2 * MH)
        sga = one.take(KT, S)
        sgm = one.take(KT, S)
        mo = one.take(NB, MH * MV)
        mva = one.take(NB, MH, MV + 1)
        mqT = one.take(MH // 2, S)
        mkT = one.take(MH // 2, S)
        qT = one.take(KT, S)
        kT = one.take(AKV, S)
        attT = one.take(KT, S)
        wl = one.take(MH, 3, P)
        cw = one.take(2, 3 * P)
        at_sm = one.at
        sm = one.take(2, 4, S)
        pt = Area(at_sm - 768 - 3072 + 1024).take(NB, 4, P)
        sq = Area(at_sm).take((AH + AKV) * AD)
        hraw = Area(0).take(NB, MH, MV + 1)
        off_q = NB * 1296 + 2 * KT * S + NB * D + NB * MH * (MV + 1)
        hmT_hi = Area(off_q).take(KT, S, dt=R32)
        hmT_lo = Area(0).take(KT, S, dt=R32)
        hs = Area(at_sm).take(NB, MH, MV)
        mixT = Area(off_q + 2048).take(KT, S)
        mixT_hi = Area(at_sm).take(KT, S, dt=R32)
        mixT_lo = Area(NB * 1296).take(KT, S, dt=R32)
        hsq = Area(off_q + 2048 + 2048 + 512 + 2048).take(NB, MH, MV)
        tmpT = hsq.rearrange("p a b c -> p (a b c)").rearrange("p (a b) -> p a b", b=S)

        two = Area()
        h2 = two.take(NB, D)
        sk = two.take(PH, NKEY)
        qpT = two.take(PH, S)
        scr = [two.take(PH, 2, NKEY), qpT.rearrange("p h (c k) -> p h c k", c=2)]
        hot = two.take(PR, TOPK, TOPK)
        picked = two.take(PR, TOPK, TOPK)
        n2row = Area(two.at - D).take(D)
        tv = two.take(PR, 2, TOPK)
        ti = two.take(PR, 2, TOPK, dt=U32)
        tif = two.take(PR, 2, TOPK)
        bv = two.take(PR, TOPK)
        bp = two.take(PR, TOPK, dt=U32)
        bij = two.take(2, PR * TOPK, dt=U32)
        bijf = two.take(2, PR * TOPK)
        exf = two.take(3, PR * TOPK)
        gates = two.take(NB * PH * TOPK)
        idx = two.take(NB, PH * TOPK, dt=U32)
        rows_d = two.take(DSLOTS, D)
        iota16 = sb("iota16", [P, TOPK])
        idx_st = sb("idx_st", [P, 2, TOPK], U32)
        dots = sb("dots", [P, 2, TOPK])
        gelu = sb("gelu", [P, 2, TOPK])
        wgt = sb("wgt", [P, 2, TOPK])
        diag = sb("diag", [P, 4, P])
        gsum = sb("gsum", [P, 2, PR])

        thr = Area()
        p2 = thr.take(NB, 3 * SBW)
        qkT2 = thr.take(8, S)
        zm = thr.take(2, 2, 3 * P)
        sp_ = thr.take(2, 2, 3 * P)
        wT = thr.take(2, 2, 3 * P)
        end_sb = thr.at
        hv = thr.take(NB, HGW)
        hq = thr.take(HH, S)
        hf = thr.take(HH, S)
        hg = thr.take(HH, S)
        sg2 = thr.take(2 * KT, S)
        osbT = thr.take(SBW // P, S)
        ohgT = thr.take(HGW // P, S)
        far = thr.at
        hgp = Area(0)
        key = hgp.take(HH, S)
        bb = hgp.take(HH, S)
        qe = hgp.take(HH, S)
        keT = hgp.take(HH, S)
        ket = hgp.take(NB, HH, P)
        vpar = hgp.take(2, NB, HGW)
        AT = hgp.take(HH, NB, P)
        state = hgp.take(3, HH, P)
        assert hgp.at <= end_sb
        far_end = Area(far)
        xbuf = far_end.take(2, HH, S)
        osbT_hi = far_end.take(SBW // P, S, dt=R32)
        osbT_lo = Area(far - 2 * 1024).take(SBW // P, S, dt=R32)
        ohgT_hi = Area(far).take(HGW // P, S, dt=R32)
        ohgT_lo = Area(far + 1024).take(HGW // P, S, dt=R32)
        osq = key.rearrange("p h (b t) -> p h b t", b=NB)
        orr = bb.rearrange("p h (b t) -> p h b t", b=NB)
        mixT2 = Area(0).take(KT, S)
        tmp2 = Area(2048).take(2, S)
        mixT2_hi = Area(3072).take(KT, S, dt=R32)
        mixT2_lo = Area(3072 + 2048).take(KT, S, dt=R32)
        silu = Area(3072).take(2, 2, S)
        hidden = Area(3072 + 1024)
        hid_hi = hidden.take(4, 2, S, dt=R32)
        hid_lo = hidden.take(4, 2, S, dt=R32)
        mask_str = sb("mask_str", [P, P])
        tri = sb("tri", [P, P])
        every16 = sb("every16", [P, P + HC])
        m16 = sb("m16", [P, P])
        restart = sb("restart", [P, HH * S])
        par = sb("par", [P, 2])
        sbgain = sb("sbgain", [P, 2])
        hgain = sb("hgain", [P, 1])
        lbt = sb("lbt", [P, 2, HH])
        lbs = sb("lbs", [P, 5, HH])
        dec = sb("dec", [P, HH, NHC])
        hst2 = sb("hst2", [P, 3, 2 * SH])

        kd = Area(at_sm + 1152).take(NB, 2 * AKV * AD)
        ang = sb("ang", [P, 4, NB, RH])
        cs = sb("cs", [P, 2, NB, RH])
        posf = sb("posf", [P, NB])
        hst = sb("hst", [P, 3, AH + AKV])
        rt = Area(at_sm - 768 - 3072).take(4, AH + AKV, RH)
        am = sb("am", [P, 2, 6, 4])
        gt = sb("gt", [P, 4, NB, MH])
        aT = sb("aT", [P, NB, MH])
        em = sb("em", [P, NB, MH])
        rows = sb("rows", [MH, 6, S])
        den = sb("den", [P, 4, NB, MH])

        block = ctx.enter_context(nc.Block())

        def wview(w):
            return w.rearrange("(t p) n -> p t n", p=P)

        w1 = wview(a["w_in"])
        chunks = []

        done_count = {}
        used = []
        halves = []

        def add(name, view, done, n=2):
            done_count[done] = done_count.get(done, 0) + n
            used.append((done, done_count[done]))
            chunks.append((name, (view,)))

        def add_split(name, *views):
            for g in range(len(views)):
                halves.append((len(chunks), g))
            used.append(None)
            chunks.append((name, views))

        def add_columns(name, w, c0):
            add_split(name, *[w[:, :, c0 + g * HALF:c0 + (g + 1) * HALF] for g in range(2)])

        for c in range(2):
            add_columns("aq", w1, AQ0 + c * CW)
        add_split("kv", w1[:, :, AK0:MQ0], w1[:, :, MI0:MO0])
        for nm, c0, c1 in (("mq", MQ0, MK0), ("mk", MK0, MV0), ("mv", MV0, MI0), ("mo", MO0, GA0), ("gates", GA0, W1N)):
            for c in range(c0, c1, CW):
                add_columns(nm, w1, c)
        NW1 = len(chunks)
        v = wview(a["w_branch_attn"])
        for c in range(2):
            add("w_branch_attn", v[:, :, c * CW:(c + 1) * CW], "br_done")
        NML = len(chunks)
        for nm in ("w_branch_mlstm", "w_out"):
            for c in range(2):
                add_columns(nm, wview(a[nm]), c * CW)
        v = wview(a["peer_w_query"])
        NQUERY = len(chunks)
        for c in range(2):
            add_columns("query", v, c * CW)
        NPEER = len(chunks)
        w2 = wview(a["w_in_2"])
        for c, nm in enumerate(("sb", "sb", "sb", "hq", "hf", "hv", "hg", "g2", "g2", "g2", "g2")):
            add_columns(nm, w2, c * CW)
        N2 = len(chunks)
        v = wview(a["w_branch_2"])
        for c in range(2):
            add_columns("branch_2", v, c * CW)
        v = wview(a["w_out_2"])
        for c in range(2):
            add_columns("out_2", v, c * CW)
        NFFN = len(chunks)
        fg, fu = wview(a["w_ffn_gate_2"]), wview(a["w_ffn_up_2"])
        fd = wview(a["w_ffn_down_2"])
        NFF = FF // S
        for c in range(NFF):
            add_split("gate_up", fg[:, :, c * S:(c + 1) * S], fu[:, :, c * S:(c + 1) * S])
            if c % 2 or c == NFF - 1:
                c0 = c - c % 2
                add_split("down", *[fd[:, 2 * e:2 * (e + 1), :] for e in range(c0, c + 1)])
        ffn_chunk = [n for n in range(NFFN, len(chunks)) if chunks[n][0] == "gate_up"]
        unit = {half: 2 * u for u, half in enumerate(halves)}
        ffn_halves = [half for half in halves if half[0] >= NFFN]
        down_half = [half for half in ffn_halves if chunks[half[0]][0] == "down"]
        ffn_unit = [unit[n, 0] for n in ffn_chunk]
        loads = {}
        per_slot = {}
        for n, (nm, views) in enumerate(chunks):
            for g in range(len(views)):
                per_slot[n % SLOTS, g] = per_slot.get((n % SLOTS, g), 0) + 16
                loads[n, g] = per_slot[n % SLOTS, g]

        def slot_sem(n, g):
            return sem(f"w_loaded{n % SLOTS}{'ab'[g]}")

        def raw_half(n, g):
            half = ring[:, n % SLOTS, :, :].rearrange("p t c -> p (t c)")[:, g * KT * HALF:(g + 1) * KT * HALF]
            return half.rearrange("p (t c) -> p t c", c=HALF)

        def split_units(n, g):
            cols = HALF if chunks[n][0] == "down" else chunks[n][1][g].shape[2]
            return [(unit[n, g] + v, slice(v * KU, (v + 1) * KU), cols) for v in range(2)]

        def upper_parts(act, n, g):
            act.wait_ge(slot_sem(n, g), loads[n, g])
            for u, t, cols in split_units(n, g):
                if u >= 4:
                    act.wait_ge(sem("unit_used"), u - 3)
                act.activation(w_hi[:, u // 2 % 2, t, 0:cols], raw_half(n, g)[:, t, 0:cols], ACT.Copy).then_inc(sem("hi_ready"), 1)

        def lower_parts(pool, n, g):
            for u, t, cols in split_units(n, g):
                pool.wait_ge(sem("hi_ready"), u + 1)
                pool.tensor_tensor(w_lo[:, u // 2 % 2, t, 0:cols], raw_half(n, g)[:, t, 0:cols], w_hi[:, u // 2 % 2, t, 0:cols].bitcast(F32),
                                   ALU.subtract).then_inc(sem("lo_ready"), 1)

        def next_half(n, g, last):
            return [(n + 1, g)] if n + 1 < last else []

        def steps_after(halves, steps, skip, per=1):
            order, left = [], list(steps)
            for i, half in enumerate(halves):
                order.append(("half",) + half)
                if i >= skip:
                    order += left[:per]
                    left = left[per:]
            return order + left

        def halves_of(first, last):
            return [(n, g) for n in range(first, last) for g in range(2)]

        GROUPS = NB * 4
        att_steps = [("turn_qk", 0), ("turn_qk", 1)]
        for g in range(GROUPS + 2):
            att_steps.append(("attend", g))
        att_steps += [("gate_rows", 0), ("spread", 0)] + [("memory", h) for h in range(MH + 1)]
        plan1 = steps_after(halves_of(0, NW1 + 2), att_steps, 6)

        BATCHES = SH // 2
        hg_steps = [("turn_sb", 0)] + [("stick", q) for q in range(BATCHES + 2)]
        hg_steps += [("pairs", j) for j in range(0, HC, 2)] + [("turn_ke", 0)] + [("state", c) for c in range(0, NHC, 2)]
        plan2 = steps_after(halves_of(NPEER, N2), hg_steps, 6)

        @block.sync
        def _(sp):
            sp.dma_start(xres[:], a["x"].rearrange("(b p) n -> p b n", p=P)).then_inc(sem("x_loaded"), 16)
            sp.wait_ge(sem("x_loaded"), 16)
            sp.wait_ge(sem("small_loaded"), NSMALL * 16)
            for n, (nm, views) in enumerate(chunks):
                if n == NPEER:
                    sp.wait_ge(sem("x2_ready"), 4)
                    sp.dma_start(sk, a["sub_keys"]).then_inc(sem("sk_loaded"), 16)
                    sp.dma_start(n2row, a["n2row"]).then_inc(sem("sk_loaded"), 16)
                    sp.wait_ge(sem("row_free"), TOPK * (1 + NB * PH))
                for g, v in enumerate(views):
                    m = n - SLOTS
                    if m >= 0 and used[m] is not None:
                        if g == 0:
                            sp.wait_ge(sem(used[m][0]), used[m][1])
                    elif m >= 0:
                        for half in (range(g, g + 1) if used[n] is None else range(2)):
                            sp.wait_ge(sem("lo_ready"), unit[m, half] + 2)
                    if nm == "down":
                        to = raw_half(n, g).rearrange("p (r t) c -> p r (t c)", r=2)
                    elif used[n] is None:
                        to = raw_half(n, g)[:, :, 0:v.shape[2]]
                    else:
                        to = ring[:, n % SLOTS, :, :]
                    sp.dma_start(to, v).then_inc(slot_sem(n, g), 16)
            sp.wait_ge(sem("x5_ready"), 4)
            sp.dma_start(out.rearrange("(b p) n -> p b n", p=P), xres[:]).then_inc(sem("stored"), 16)
            sp.wait_ge(sem("stored"), 16)

        @block.gpsimd
        def _(pool):
            step = [0]

            def link(ins):
                step[0] += 1
                ins.then_inc(sem("pool_step"), 1)
                pool.wait_ge(sem("pool_step"), step[0])

            link(pool.memset(ident[:], 0.0))
            pool.affine_select(out=ident[:], in_=ident[:], compare_op=ALU.not_equal, fill=1.0, base=0,
                               pattern=[[-1, P]], channel_multiplier=1).then_inc(sem("ident_ready"), 1)
            pool.memset(ones[:], 1.0)
            pool.memset(mask_band[:], 0.0)
            pool.memset(mask_inc[:], 0.0)
            link(pool.memset(sel[:], 0.0))
            pool.affine_select(out=mask_band[:, 0, :], in_=mask_band[:, 0, :], compare_op=ALU.is_gt, fill=NEG, base=0,
                               pattern=[[1, P]], channel_multiplier=-1)
            pool.affine_select(out=mask_band[:, 1, :], in_=mask_band[:, 1, :], compare_op=ALU.is_ge, fill=NEG, base=0,
                               pattern=[[-1, P]], channel_multiplier=1)
            pool.affine_select(out=mask_inc[:], in_=mask_inc[:], compare_op=ALU.is_ge, fill=NEG, base=0,
                               pattern=[[1, P]], channel_multiplier=-1)
            pool.affine_select(out=sel[:], in_=sel[:], compare_op=ALU.not_equal, fill=1.0, base=0,
                               pattern=[[-1, MH], [0, P]], channel_multiplier=1)
            pool.memset(mva[:, :, :, MV:MV + 1], 1.0).then_inc(sem("masks_ready"), 1)
            for n, g in halves_of(0, NW1):
                lower_parts(pool, n, g)
            pool.iota(iota16[:], [[1, TOPK]], base=0, channel_multiplier=0, allow_small_or_imprecise_dtypes=True)
            pool.memset(mask_str[:], 0.0)
            pool.memset(tri[:], 1.0)
            pool.memset(every16[:], 0.0)
            pool.memset(m16[:], 1.0)
            pool.memset(restart[:], 1.0)
            link(pool.memset(par[:], 0.0))
            pool.affine_select(out=mask_str[:], in_=mask_str[:], compare_op=ALU.is_gt, fill=NEG, base=0,
                               pattern=[[1, P]], channel_multiplier=-1)
            pool.affine_select(out=tri[:], in_=tri[:], compare_op=ALU.is_ge, fill=0.0, base=0,
                               pattern=[[-1, P]], channel_multiplier=1)
            pool.memset(every16[:].rearrange("p (a b) -> p a b", b=HC)[:, :, 0:1], 1.0)
            pool.memset(restart[:].rearrange("p (a b) -> p a b", b=HC)[:, :, 0:1], 0.0)
            m3 = m16[:].rearrange("p (a b) -> p a b", b=HC)
            link(pool.affine_select(out=m3, in_=m3, compare_op=ALU.is_ge, fill=0.0, base=0,
                                    pattern=[[-HC, P // HC], [0, HC]], channel_multiplier=1))
            link(pool.affine_select(out=m3, in_=m3, compare_op=ALU.is_ge, fill=0.0, base=HC - 1,
                                    pattern=[[HC, P // HC], [0, HC]], channel_multiplier=-1))
            link(pool.tensor_copy(par[:], m3[:, 0:2, 0]))
            for c in range(1, P // HC // 2):
                link(pool.tensor_tensor(par[:], par[:], m3[:, 2 * c:2 * c + 2, 0], ALU.add))
            pool.affine_select(out=m16[:], in_=m16[:], compare_op=ALU.is_ge, fill=0.0, base=0,
                               pattern=[[1, P]], channel_multiplier=-1).then_inc(sem("masks2_ready"), 1)

            for n, g in halves_of(NML, NPEER):
                lower_parts(pool, n, g)

            for b in range(NB):
                with pool.Fori(0, NR) as it:
                    pool.wait_ge(sem("routed"), it + (b * NR + 1))
                    for o in range(2):
                        g = it * 2 + (b * PH + o)
                        pool.wait_ge(sem("row_free"), g * TOPK + 1)
                        pool.tensor_copy(idx_st[:, o, :], idx[:, b, bass.ds(it * (2 * TOPK) + o * TOPK, TOPK)]).then_inc(sem("idx_staged"), 1)
                        pool.wait_ge(sem("idx_staged"), g + 1)
                        for k in range(TOPK):
                            pool.wait_ge(sem("drow_free"), g * TOPK + (k + 1))
                            pool.sem_inc(sem("slots_granted"), 1)
                            pool.indirect_dma_start(rows_d[:, k % DSLOTS, :], None, a["peer_down"],
                                                    bass.IndirectOffsetOnAxis(ap=idx_st[:, o, k:k + 1], axis=0)).then_inc(sem(f"drow{k % DSLOTS}"), 16)
                        for k in range(TOPK):
                            pool.wait_ge(sem("row_free"), g * TOPK + (k + 1))
                            pool.sem_inc(sem("slots_granted"), 1)
                            pool.indirect_dma_start(rows_u[:, k, :], None, a["peer_up"],
                                                    bass.IndirectOffsetOnAxis(ap=idx_st[:, o, k:k + 1], axis=0)).then_inc(sem(f"urow{k}"), 16)
            for n, g in halves_of(NPEER, NFFN) + ffn_halves:
                lower_parts(pool, n, g)

        def norm_act(act, k, ready, count, first):
            act.wait_ge(sem(ready), count)
            for b in range(NB):
                act.activation(xn[:, b, :], xres[:, b, :], ACT.Square, accum_out=ss[:, b:b + 1]).then_inc(sem("sumsq"), 1)
            act.wait_ge(sem("meansq"), k + 1)
            act.activation(sd[:], ms[:], ACT.Sqrt).then_inc(sem("root"), 1)
            upper_parts(act, first, 0)
            for t in range(KT):
                act.wait_ge(sem("turned"), KT // 2 * k + t // 2 + 1)
                act.activation(hT_hi[:, t, :], ps[:, t // 2, (t % 2) * S:(t % 2 + 1) * S], ACT.Copy,
                               scale=gcol[:, k, t:t + 1]).then_inc(sem("hT_hi_ready"), 1)
            upper_parts(act, first, 1)

        def norm_dve(dve, link, k):
            dve.wait_ge(sem("sumsq"), NB * (k + 1))
            dve.tensor_scalar(ms[:], ss[:], 1.0 / D, EPS, ALU.mult, ALU.add).then_inc(sem("meansq"), 1)
            dve.wait_ge(sem("root"), k + 1)
            link(dve.reciprocal(rr[:], sd[:]))
            for b in range(NB):
                dve.tensor_scalar(xn[:, b, :], xres[:, b, :], rr[:, b:b + 1], None, ALU.mult).then_inc(sem("xn_ready"), 1)
            if k == 1:
                dve.wait_ge(sem("sk_loaded"), 32)
                dve.wait_ge(sem("xn_ready"), 2 * NB)
                for b in range(NB):
                    ins = dve.tensor_tensor(h2[:, b, :], xn[:, b, :], n2row, ALU.mult)
                link(ins)
            dve.wait_ge(sem("turned"), KT // 2 * (k + 1))
            for t in range(KT):
                dve.wait_ge(sem("hT_hi_ready"), KT * k + t // 2 * 2 + 2)
                dve.scalar_tensor_tensor(out=hT_lo[:, t, :], in0=ps[:, t // 2, (t % 2) * S:(t % 2 + 1) * S], scalar=gcol[:, k, t:t + 1],
                                         in1=hT_hi[:, t, :].bitcast(F32), op0=ALU.mult, op1=ALU.subtract).then_inc(sem("hT_ready"), 1)

        def norm_pe(pe, k):
            for b in range(NB):
                pe.wait_ge(sem("xn_ready"), NB * k + b + 1)
                for t in range(KT):
                    ins = pe.transpose(ps[:, t // 2, (t % 2) * S + b * P:(t % 2) * S + (b + 1) * P],
                                       xn[:, b, t * P:(t + 1) * P], ident[:])
                    if b == NB - 1 and t % 2:
                        ins.then_inc(sem("turned"), 1)

        @block.tensor
        def _(pe):
            n_half = [0]

            def begin_half(evac, first):
                h = n_half[0]
                if h - first >= LB:
                    pe.wait_ge(sem(evac), h - first - LB + 1)
                n_half[0] += 1
                return ps[:, (h - first) % LB, :]

            def split_half(n, g, tok, bank, x_hi=hT_hi, x_lo=hT_lo):
                for u, ts, cols in split_units(n, g):
                    pe.wait_ge(sem("lo_ready"), u + 1)
                    hi, lo = w_hi[:, u // 2 % 2], w_lo[:, u // 2 % 2]
                    for t in range(ts.start, ts.stop):
                        for j in range(2):
                            js = slice(j * P, (j + 1) * P)
                            if tok:
                                to = bank[:, j * cols:(j + 1) * cols]
                                parts = ((x_hi[:, t, js], hi[:, t, 0:cols]), (x_hi[:, t, js], lo[:, t, 0:cols]), (x_lo[:, t, js], hi[:, t, 0:cols]))
                            else:
                                to = bank[:, j * S:(j + 1) * S]
                                parts = ((hi[:, t, js], x_hi[:, t, :]), (hi[:, t, js], x_lo[:, t, :]), (lo[:, t, js], x_hi[:, t, :]))
                            for e, (still, moving) in enumerate(parts):
                                ins = pe.matmul(to, still, moving, start=(t == 0 and j == 0 and e == 0), stop=(t == KT - 1 and e == 2),
                                                skip_group_check=True)
                    ins.then_inc(sem("unit_used"), 1)

            def half_whole(n, g, src, evac, done, first):
                if g == 0:
                    pe.wait_ge(slot_sem(n, 0), loads[n, 0])
                bank = begin_half(evac, first)
                for j in range(2):
                    for t in range(KT):
                        ins = pe.matmul(bank[:, j * S:(j + 1) * S],
                                        ring[:, n % SLOTS, t, (2 * g + j) * P:(2 * g + j + 1) * P], src[:, t, :],
                                        start=(t == 0), stop=(t == KT - 1))
                ins.then_inc(sem(done), 1)

            pe.wait_ge(sem("ident_ready"), 1)
            norm_pe(pe, 0)
            pe.wait_ge(sem("hT_ready"), KT)

            def turn_qk(b):
                pe.wait_ge(sem("qk_rotated"), b + 1)
                if b:
                    pe.wait_ge(sem("qkT_ready"), b)
                for j in range(10):
                    src = p1[:, b, j * P:(j + 1) * P] if j < 8 else kd[:, b, (j - 8) * P:(j - 7) * P]
                    ins = pe.transpose(ps[:, 4 + j // 4, (j % 4) * P:(j % 4 + 1) * P], src, ident[:])
                ins.then_inc(sem("qk_turned"), 1)

            def attend(k):
                if 1 <= k <= GROUPS:
                    b = (k - 1) // 4
                    pe.wait_ge(sem("probs"), k)
                    if k >= 2:
                        pe.wait_ge(sem("probsT"), k - 1)
                    for kb in range(b + 1):
                        for i in range(4):
                            ins = pe.transpose(ps[:, 6 + kb, i * P:(i + 1) * P], sm[:, (k - 1) % 2, i, kb * P:(kb + 1) * P], ident[:])
                    ins.then_inc(sem("probs_turned"), 1)
                if k < GROUPS:
                    b, q = k // 4, k % 4
                    if k == 0:
                        pe.wait_ge(sem("qkT_ready"), NB)
                        pe.wait_ge(sem("masks_ready"), 1)
                    else:
                        pe.wait_ge(sem("scores_read"), k)
                    for i in range(4):
                        h = 4 * q + i
                        r = slice((h % 2) * AD, (h % 2 + 1) * AD)
                        ins = pe.matmul(ps[:, 4 + i % 2, (i // 2) * S:(i // 2) * S + P * (b + 1)], qT[r, h // 2, b * P:(b + 1) * P],
                                        kT[r, h // (AH // AKV), 0:P * (b + 1)], start=True, stop=True)
                    ins.then_inc(sem("scores"), 1)
                if k >= 2:
                    b, q = (k - 2) // 4, (k - 2) % 4
                    pe.wait_ge(sem("probsT"), k - 1)
                    if k >= 3:
                        pe.wait_ge(sem("att_evac"), k - 2)
                    for i in range(2):
                        for kb in range(b + 1):
                            v = p1[:, kb, AV0 + q // 2 * AD:AV0 + (q // 2 + 1) * AD]
                            ins = pe.matmul(ps[i * AD:(i + 1) * AD, 3, 0:S], v, pt[:, kb, i::2, :], start=(kb == 0), stop=(kb == b))
                    ins.then_inc(sem("att_done"), 1)

            def gate_rows(_):
                pe.wait_ge(sem("gates_tok"), 1)
                pe.wait_ge(sem("att_evac"), GROUPS)
                for k in range(2):
                    for b in range(NB):
                        ins = pe.matmul(ps[0:MH, 3, k * S + b * P:k * S + (b + 1) * P], gt[:, k, b, :], ident[:],
                                        start=True, stop=True)
                ins.then_inc(sem("gates_turned"), 1)

            def spread(_):
                pe.wait_ge(sem("rows_ready"), 1)
                for b in range(NB):
                    for k, r in enumerate((3, 5)):
                        ins = pe.matmul(ps[:, 3, (2 * k + b) * MH:(2 * k + b + 1) * MH], rows[:, r, b * P:(b + 1) * P],
                                        ident[0:MH, 0:MH], start=True, stop=True)
                for h in range(MH):
                    ins = pe.matmul(ps[:, 4 + h // 2, (h % 2) * S:(h % 2 + 1) * S], sel[0:MH, h, :], rows[:, 4, :], start=True, stop=True)
                ins.then_inc(sem("m_spread"), 1)

            def memory(h):
                if h >= 1:
                    g = h - 1
                    pe.wait_ge(sem("cw_ready"), g + 1)
                    if g >= 2:
                        pe.wait_ge(sem("num_evac"), g - 1)
                    bank = ps[:, 6 + g % 2, :]
                    w = MV + 1
                    pe.matmul(bank[:, 0:w], cw[:, g % 2, 0:P], mva[:, 0, g, :], start=True, stop=True)
                    pe.matmul(bank[:, w:2 * w], cw[:, g % 2, P:2 * P], mva[:, 0, g, :], start=True, stop=False)
                    pe.matmul(bank[:, w:2 * w], cw[:, g % 2, 2 * P:3 * P], mva[:, 1, g, :], start=False,
                              stop=True).then_inc(sem("num_done"), 1)
                if h < MH:
                    r = slice((h % 2) * MQ, (h % 2 + 1) * MQ)
                    if h >= 2:
                        pe.wait_ge(sem("cw_ready"), h - 1)
                    else:
                        pe.wait_ge(sem("wl_ready"), MH)
                    bank = ps[:, 4 + h % 2, :]
                    pe.matmul(bank[:, 0:S], mkT[r, h // 2, 0:P], mqT[r, h // 2, :], start=True, stop=True)
                    pe.matmul(bank[:, S:S + P], mkT[r, h // 2, P:S], mqT[r, h // 2, P:S],
                              start=True, stop=True).then_inc(sem("ml_qk"), 1)

            do = {"turn_qk": turn_qk, "attend": attend, "gate_rows": gate_rows, "spread": spread, "memory": memory}
            for what, n, *g in plan1:
                if what != "half":
                    do[what](n)
                elif n >= NW1:
                    if n == NW1 and g[0] == 0:
                        pe.wait_ge(sem("att_evac"), GROUPS)
                        pe.wait_ge(sem("p1_evac"), 2 * NW1)
                    half_whole(n, g[0], attT, "br_evac", "br_done", 2 * NW1)
                else:
                    split_half(n, g[0], chunks[n][0] in ("aq", "kv", "mv", "mo"), begin_half("p1_evac", 0))
            pe.wait_ge(sem("hm_tok"), 1)
            for t in range(KT):
                for b in range(NB):
                    ins = pe.transpose(ps[:, 4 + t // 2, (t % 2) * S + b * P:(t % 2) * S + (b + 1) * P], hs[:, b, t, :], ident[:])
                if t % 2:
                    ins.then_inc(sem("hm_turned"), 1)
            pe.wait_ge(sem("hmT_ready"), KT)
            for n, g in halves_of(NML, NML + 2):
                split_half(n, g, False, begin_half("br_evac", 2 * NW1), hmT_hi, hmT_lo)
            pe.wait_ge(sem("br_evac"), 8)
            f = n_half[0]
            for n, g in halves_of(NML + 2, NQUERY):
                split_half(n, g, True, begin_half("x2_ready", f), mixT_hi, mixT_lo)

            pe.wait_ge(sem("x2_ready"), 4)
            norm_pe(pe, 1)
            pe.wait_ge(sem("hT_ready"), 2 * KT)
            f = n_half[0]

            def key_scores(r):
                b, i = r // NR, r % NR
                pe.wait_ge(sem("q_evac"), i + 1)
                if r >= 2:
                    pe.wait_ge(sem("scr_ready"), r - 1)
                for h in range(PR):
                    for p in range(2):
                        half = slice(p * (P // 2), (p + 1) * (P // 2))
                        ins = pe.matmul(ps[:, 4 + 2 * (r % 2) + p, h * NKEY:(h + 1) * NKEY],
                                        qpT[half, i * PR + h, b * P:(b + 1) * P], sk[half, i * PR + h, :], start=True, stop=True)
                ins.then_inc(sem("key_scores"), 1)

            for r, (n, g) in enumerate(halves_of(NQUERY, NPEER)):
                split_half(n, g, False, begin_half("q_evac", f))
                if r == 0:
                    pe.wait_ge(sem("sk_loaded"), 32)
                key_scores(r)
            for r in range(NR, NB * NR):
                key_scores(r)
            for b in range(NB):
                pe.wait_ge(sem("scr_ready"), NB * NR)
                acc = ps[:, 6 - 2 * b:8 - 2 * b, :]
                for c in range(2):
                    ins = pe.matmul(acc[:, c, :], ident[:], xres[:, b, c * CW:(c + 1) * CW], start=True, stop=True)
                if b == 0:
                    ins.then_inc(sem("row_free"), TOPK)
                with pe.Fori(0, PH // 2) as it:
                    for o in range(2):
                        g = it * 2 + (b * PH + o)
                        for k in range(TOPK):
                            pe.wait_ge(sem("diag_ready"), g * TOPK + (k + 1))
                            pe.wait_ge(sem(f"urow{k}"), g * 16 + 16)
                            for c in range(2):
                                ins = pe.matmul(acc[:, c, :], diag[:, k % 4, :], rows_u[:, k, c * CW:(c + 1) * CW],
                                                start=False, stop=True, skip_group_check=True)
                            ins.then_inc(sem("row_free"), 1)

            pe.wait_ge(sem("x3_ready"), NB)
            norm_pe(pe, 2)
            pe.wait_ge(sem("hT_ready"), 3 * KT)

            def turn_sb(_):
                pe.wait_ge(sem("sb_normed"), 1)
                pe.wait_ge(sem("masks2_ready"), 1)
                for j in range(8):
                    for b in range(NB):
                        ins = pe.transpose(ps[:, 4 + j // 2, (j % 2) * S + b * P:(j % 2) * S + (b + 1) * P],
                                           p2[:, b, j * P:(j + 1) * P], ident[:])
                ins.then_inc(sem("sb_turned"), 1)

            def stick(k):
                if 1 <= k <= BATCHES:
                    q = (k - 1) % 2
                    pe.wait_ge(sem("sp_ready"), k)
                    if k >= 2:
                        pe.wait_ge(sem("logw_ready"), k - 1)
                    for i in range(2):
                        pe.matmul(ps[:, 6 + i, 0:3 * P], tri[:], sp_[:, q, i, :], start=True, stop=False)
                        ins = pe.matmul(ps[:, 6 + i, P:S], ones[:], sp_[:, q, i, S:3 * P], start=False, stop=True)
                    ins.then_inc(sem("rest_done"), 1)
                if k < BATCHES:
                    if k == 0:
                        pe.wait_ge(sem("sbT_ready"), 1)
                    else:
                        pe.wait_ge(sem("zm_ready"), k)
                    for i in range(2):
                        h = 2 * k + i
                        r = slice(i * SD, (i + 1) * SD)
                        pe.matmul(ps[:, 4 + i, 0:S], qkT2[r, 4 + h // 2, 0:P], qkT2[r, h // 2, :], start=True, stop=True)
                        ins = pe.matmul(ps[:, 4 + i, S:S + P], qkT2[r, 4 + h // 2, P:S], qkT2[r, h // 2, P:S], start=True, stop=True)
                    ins.then_inc(sem("z_done"), 1)
                if k >= 2:
                    pe.wait_ge(sem("w_ready"), k - 1)
                    if k >= 3:
                        pe.wait_ge(sem("osb_evac"), k - 2)
                    for i in range(2):
                        o = ps[i * SD:(i + 1) * SD, 3, 0:S]
                        v0 = 2 * SBW + (2 * (k - 2) + i) * SD
                        pe.matmul(o, p2[:, 0, v0:v0 + SD], wT[:, k % 2, i, 0:S], start=True, stop=False)
                        ins = pe.matmul(o[:, P:S], p2[:, 1, v0:v0 + SD], wT[:, k % 2, i, S:3 * P], start=False, stop=True)
                    ins.then_inc(sem("osb_done"), 1)

            def pairs(j0):
                for j in range(j0, j0 + 2):
                    pe.wait_ge(sem("pairs_ready"), j + 1)
                    for c in range(2):
                        ins = pe.matmul(ps[:, 4 + c, :].rearrange("p (c r) -> p c r", r=HC)[:, :, j:HC], every16[:, HC - j:HC - j + P],
                                        xbuf[:, j % 2, 2 * c:2 * c + 2, :].rearrange("p h (c r) -> p (h c) r", r=HC)[:, :, j:HC],
                                        start=(j == 0), stop=(j == HC - 1), skip_group_check=True)
                    ins.then_inc(sem("pairs_summed"), 1)

            def turn_ke(_):
                pe.wait_ge(sem("keT_ready"), 1)
                for b in range(NB):
                    for h in range(HH):
                        ins = pe.transpose(ps[:, 6 + b, h * P:(h + 1) * P], keT[:, h, b * P:(b + 1) * P], ident[:])
                ins.then_inc(sem("ke_turned"), 1)
                pe.wait_ge(sem("AT_ready"), 1)
                for b in range(NB):
                    for h in range(HH):
                        pe.matmul(ps[:, 4 + b, h * P:(h + 1) * P], hv[:, b, h * P:(h + 1) * P], AT[:, h, b, :],
                                  start=(h == 0), stop=True, skip_group_check=True)

            def state_pe(c0):
                def increment(c):
                    b, r0 = c // (P // HC), c % (P // HC) * HC
                    rb = slice(r0 // 32 * 32, r0 // 32 * 32 + 32)
                    for h in range(HH):
                        ins = pe.matmul(ps[:, 6 + c % 2, h * P:(h + 1) * P], ket[rb, b, h, :], vpar[rb, c % 2, b, h * P:(h + 1) * P],
                                        start=True, stop=True)
                    ins.then_inc(sem("inc_done"), 1)

                for c in range(c0, c0 + 2):
                    b, r0 = c // (P // HC), c % (P // HC) * HC
                    if c == 0:
                        pe.wait_ge(sem("ket_ready"), 1)
                        pe.wait_ge(sem("vpar_ready"), 1)
                        increment(0)
                    else:
                        pe.wait_ge(sem("state_ready"), c)
                    if c + 1 < NHC - 1:
                        increment(c + 1)
                    if c >= 1:
                        for h in range(HH):
                            ins = pe.matmul(ps[:, 4 + b, h * P + r0:h * P + r0 + HC], state[:, c % 3, h, :], qe[:, h, b * P + r0:b * P + r0 + HC],
                                            start=False, stop=True, skip_group_check=True)
                        ins.then_inc(sem("read_done"), 1)

            f = n_half[0]
            do = {"turn_sb": turn_sb, "stick": stick, "pairs": pairs, "turn_ke": turn_ke, "state": state_pe}
            for what, n, *g in plan2:
                if what != "half":
                    do[what](n)
                else:
                    split_half(n, g[0], chunks[n][0] in ("sb", "hv"), begin_half("p2_evac", f))
            pe.wait_ge(sem("osq_ready"), 2)
            for b in range(NB):
                ins = pe.matmul(ps[:, 6 + b, :], ones[:], osq[:, :, b, :], start=True, stop=True)
            ins.then_inc(sem("osq_summed"), 1)
            pe.wait_ge(sem("ohg_ready"), 1)
            pe.wait_ge(sem("p2_evac"), 2 * (N2 - NPEER))
            for i, (n, g) in enumerate(halves_of(N2, N2 + 2)):
                if i >= 2:
                    pe.wait_ge(sem("br2_evac"), 2 * i - 2)
                for v, (x_hi, x_lo) in enumerate(((osbT_hi, osbT_lo), (ohgT_hi, ohgT_lo))):
                    u = unit[n, g] + v
                    pe.wait_ge(sem("lo_ready"), u + 1)
                    for j in range(2):
                        bank = ps[:, (2 * i + j) % 4, v * S:(v + 1) * S]
                        js = slice(j * P, (j + 1) * P)
                        for t in range(KU):
                            hi, lo = w_hi[:, u // 2 % 2, v * KU + t, js], w_lo[:, u // 2 % 2, v * KU + t, js]
                            for e, (still, moving) in enumerate(((hi, x_hi[:, t, :]), (hi, x_lo[:, t, :]), (lo, x_hi[:, t, :]))):
                                ins = pe.matmul(bank, still, moving, start=(v == 0 and t == 0 and e == 0), stop=(t == KU - 1 and e == 2),
                                                skip_group_check=True)
                    ins.then_inc(sem("unit_used"), 1)
            pe.wait_ge(sem("br2_evac"), 8)
            f = n_half[0]
            for n, g in halves_of(N2 + 2, NFFN):
                split_half(n, g, True, begin_half("x4_ready", f), mixT2_hi, mixT2_lo)
            pe.wait_ge(sem("x4_ready"), 4)
            norm_pe(pe, 3)
            pe.wait_ge(sem("hT_ready"), 4 * KT)
            f = n_half[0]

            def down(c):
                n, g = down_half[c]
                pe.wait_ge(sem("hid_ready"), c + 1)
                for u, _, _ in split_units(n, g):
                    j = u % 2
                    pe.wait_ge(sem("lo_ready"), u + 1)
                    hi, lo = [w[:, u // 2 % 2].rearrange("p (r t) c -> p r (t c)", r=2)[:, j, :] for w in (w_hi, w_lo)]
                    for b in range(NB):
                        for e in range(2):
                            h_hi, h_lo = hid_hi[:, c % 4, j, b * P:(b + 1) * P], hid_lo[:, c % 4, j, b * P:(b + 1) * P]
                            es = slice(e * CW, (e + 1) * CW)
                            for m, (still, moving) in enumerate(((h_hi, hi[:, es]), (h_hi, lo[:, es]), (h_lo, hi[:, es]))):
                                ins = pe.matmul(ps[:, 4 + 2 * b + e, :], still, moving, start=(c == 0 and j == 0 and m == 0),
                                                stop=(c == NFF - 1 and j == 1 and m == 2), skip_group_check=True)
                    ins.then_inc(sem("unit_used"), 1)

            for c, n in enumerate(ffn_chunk):
                if c >= 2:
                    pe.wait_ge(sem("hid_ready"), c - 1)
                for g in range(2):
                    split_half(n, g, False, ps[:, (2 * c + g) % 4, :])
                if c % 2 or c == NFF - 1:
                    for e in range(c - c % 2, c + 1):
                        down(e)

        @block.scalar
        def _(act):
            step = [0]

            def link(ins):
                step[0] += 1
                ins.then_inc(sem("act_step"), 1)
                act.wait_ge(sem("act_step"), step[0])

            for n, (t, v) in enumerate((("gcol", gcol[:]), ("mlgain", mlgain[:]), ("qkgain", qkgain[:]), ("sinks", sinks[:]),
                         ("ifbias", ifbias[:]), ("pos", pos_i[:]), ("freq", freq[:]), ("sbgain", sbgain[:]), ("hgain", hgain[:]), ("lbt", lbt[:]))):
                act.dma_start(v, a[t]).then_inc(sem("small_loaded"), 16)
            act.wait_ge(sem("small_loaded"), NSMALL * 16)
            norm_act(act, 0, "x_loaded", 16, 0)
            act.wait_ge(sem("masks_ready"), 1)
            seen = [chunks[n][0] for n in range(N2)]

            def leave1(n, g):
                h = 2 * n + g
                nm = chunks[n][0]
                c = seen[:n].count(nm)
                act.wait_ge(sem("unit_used"), unit[n, g] + 2)
                bank = ps[:, h % LB, :]
                col = c * CW + g * HALF
                by_block = bank.rearrange("p (b c) -> p b c", b=NB)
                if nm == "aq":
                    ins = act.activation(p1[:, :, col:col + HALF], by_block, ACT.Copy)
                elif nm == "kv" and g == 0:
                    ins = act.activation(p1[:, :, AK0:MQ0], by_block, ACT.Copy)
                elif nm == "kv":
                    ins = act.activation(p1[:, :, MQ0:MQ0 + 2 * MH], bank[:, 0:NB * 2 * MH].rearrange("p (b c) -> p b c", b=NB), ACT.Copy)
                elif nm in ("mq", "mk"):
                    dst = mqT if nm == "mq" else mkT
                    ins = act.activation(dst[:, 2 * g:2 * g + 2, :], bank.rearrange("p (a b) -> p a b", a=2), ACT.Copy)
                elif nm == "mv":
                    ins = act.activation(mva[:, :, 4 * c + 2 * g:4 * c + 2 * g + 2, 0:MV], bank.rearrange("p (b h v) -> p b h v", b=NB, v=MV), ACT.Copy)
                elif nm == "mo":
                    ins = act.activation(mo[:, :, col:col + HALF], by_block, ACT.Sigmoid)
                else:
                    dst = sga if c < 2 else sgm
                    t = 4 * (c % 2) + 2 * g
                    ins = act.activation(dst[:, t:t + 2, :], bank.rearrange("p (a b) -> p a b", a=2), ACT.Sigmoid)
                ins.then_inc(sem("p1_evac"), 1)

            def turn_qk(b):
                if b == 0:
                    act.wait_ge(sem("angles"), 1)
                    act.activation(cs[:], ang[:, 2:4, :, :], ACT.Sin).then_inc(sem("sines"), 1)
                    for k in range(NB):
                        act.wait_ge(sem("qk_ms"), k + 1)
                        act.activation(hst[:, 1, :], hst[:, 0, :], ACT.Sqrt).then_inc(sem("qk_root"), 1)
                act.wait_ge(sem("qk_turned"), b + 1)
                for j in range(2):
                    act.activation(qT[:, 4 * j:4 * j + 4, b * P:(b + 1) * P], ps[:, 4 + j, :].rearrange("p (a b) -> p a b", a=4), ACT.Copy)
                act.activation(kT[:, :, b * P:(b + 1) * P], ps[:, 6, 0:S].rearrange("p (a b) -> p a b", a=2), ACT.Copy).then_inc(sem("qkT_ready"), 1)

            def attend(k):
                if k < GROUPS:
                    nk = P * (k // 4 + 1)
                    act.wait_ge(sem("row_max"), k + 1)
                    for i in range(4):
                        x = sm[:, k % 2, i, 0:nk]
                        act.activation(x, x, ACT.Exp, bias=am[:, k % 2, 1, i:i + 1], accum_out=am[:, k % 2, 2, i:i + 1])
                    act.activation(am[:, k % 2, 4, :], am[:, k % 2, 3, :], ACT.Exp).then_inc(sem("exps"), 1)
                if k >= 2:
                    b, q = (k - 2) // 4, (k - 2) % 4
                    act.wait_ge(sem("att_done"), k - 1)
                    for i in range(2):
                        ins = act.activation(attT[i * AD:(i + 1) * AD, 2 * q:2 * q + 2, b * P:(b + 1) * P],
                                             ps[i * AD:(i + 1) * AD, 3, 0:S].rearrange("p (a b) -> p a b", a=2), ACT.Copy)
                    ins.then_inc(sem("att_evac"), 1)
                if 1 <= k <= GROUPS:
                    act.wait_ge(sem("probs_turned"), k)
                    for kb in range((k - 1) // 4 + 1):
                        ins = act.activation(pt[:, kb, :, :], ps[:, 6 + kb, :].rearrange("p (a b) -> p a b", a=4), ACT.Copy)
                    ins.then_inc(sem("probsT"), 1)

            def gate_rows(_):
                act.wait_ge(sem("gates_raw"), 1)
                act.activation(gt[:, 2:4, :, :], gt[:, 0:2, :, :], ACT.Tanh, scale=1.0 / CAP).then_inc(sem("gates_tanh"), 1)
                act.wait_ge(sem("gates_cap"), 1)
                link(act.activation(gt[:, 2, :, :], gt[:, 1, :, :], ACT.Exp, scale=-1.0))
                act.activation(gt[:, 3, :, :], gt[:, 2, :, :], ACT.Ln, bias=1.0).then_inc(sem("gates_soft"), 1)
                act.wait_ge(sem("gates_turned"), 1)
                act.activation(rows[:, 0:2, :], ps[0:MH, 3, :].rearrange("p (a b) -> p a b", a=2), ACT.Copy).then_inc(sem("rows_gates"), 1)
                act.wait_ge(sem("m_rows"), 1)
                act.activation(rows[:, 5, :], rows[:, 5, :], ACT.Exp, scale=-1.0).then_inc(sem("rows_ready"), 1)

            def spread(_):
                act.wait_ge(sem("m_spread"), 1)
                act.activation(aT[:], ps[:, 3, 0:NB * MH].rearrange("p (a b) -> p a b", a=NB), ACT.Copy)
                link(act.activation(em[:], ps[:, 3, NB * MH:2 * NB * MH].rearrange("p (a b) -> p a b", a=NB), ACT.Copy))
                act.wait_ge(sem("wl_masked"), 1)
                for h in range(MH):
                    act.activation(wl[:, h, 0, :], wl[:, h, 0, :], ACT.Exp, bias=aT[:, 0, h:h + 1])
                    act.activation(wl[:, h, 1, :], ps[:, 4 + h // 2, (h % 2) * S + P:(h % 2 + 1) * S], ACT.Exp, bias=aT[:, 0, h:h + 1])
                    act.activation(wl[:, h, 2, :], wl[:, h, 2, :], ACT.Exp, bias=aT[:, 1, h:h + 1]).then_inc(sem("wl_ready"), 1)

            def memory(h):
                if h >= 1:
                    act.wait_ge(sem("num_done"), h)
                    act.activation(hraw[:, :, h - 1, :], ps[:, 6 + (h - 1) % 2, 0:2 * (MV + 1)].rearrange("p (a b) -> p a b", a=2),
                                   ACT.Copy).then_inc(sem("num_evac"), 1)

            do = {"turn_qk": turn_qk, "attend": attend, "gate_rows": gate_rows, "spread": spread, "memory": memory}
            for what, n, *g in plan1:
                if what != "half":
                    do[what](n)
                elif n < NW1:
                    leave1(n, g[0])
                    for half in next_half(n, g[0], NW1):
                        upper_parts(act, *half)
            for n, g in halves_of(NML, NML + 1):
                upper_parts(act, n, g)
            act.wait_ge(sem("hm_ms"), 1)
            act.activation(den[:, 2, :, :], den[:, 1, :, :], ACT.Sqrt).then_inc(sem("hm_root"), 1)
            for t in range(KT):
                act.wait_ge(sem("hm_turned"), t // 2 + 1)
                act.activation(hmT_hi[:, t, :], ps[:, 4 + t // 2, (t % 2) * S:(t % 2 + 1) * S], ACT.Copy,
                               scale=mlgain[:, t:t + 1]).then_inc(sem("hmT_hi_ready"), 1)
            for n, g in halves_of(NML + 1, NQUERY):
                upper_parts(act, n, g)

            norm_act(act, 1, "x2_ready", 4, NQUERY)

            def leave_scores(r):
                act.wait_ge(sem("key_scores"), r + 1)
                h = r % NR * PR
                act.activation(scr[r // NR][:, h:h + PR, :, :].rearrange("p h q k -> p q h k"),
                               ps[:, 4 + 2 * (r % 2):6 + 2 * (r % 2), 0:PR * NKEY].rearrange("p q (h k) -> p q h k", h=PR),
                               ACT.Copy).then_inc(sem("scr_ready"), 1)

            for r, (n, g) in enumerate(halves_of(NQUERY, NPEER)):
                act.wait_ge(sem("unit_used"), unit[n, g] + 2)
                act.activation(qpT[:, PR * r:PR * (r + 1), :], ps[:, r % LB, :].rearrange("p (a b) -> p a b", a=PR),
                               ACT.Copy).then_inc(sem("q_evac"), 1)
                leave_scores(r)
                for half in next_half(n, g, NPEER):
                    upper_parts(act, *half)
            for r in range(NR, NB * NR):
                leave_scores(r)

            def gate_exp(r, at):
                act.wait_ge(sem("best_shifted"), r + 1)
                act.sem_inc(sem("exp_granted"), 1)
                x = gates[:, bass.ds(at, PR * TOPK)]
                act.activation(x, x, ACT.Exp).then_inc(sem("best_exp"), 1)

            for r in range(2):
                gate_exp(r, r * PR * TOPK)
            for b in range(NB):
                parts = ((0, NR, True),) if b < NB - 1 else ((0, NR - 2, True), (NR - 2, NR, False))
                for first, last, more in parts:
                    with act.Fori(first, last) as it:
                        for o in range(PR):
                            g = it * PR + (b * PH + o)
                            act.wait_ge(sem("drow_free"), g * TOPK + (DSLOTS + TOPK))
                            act.activation(gelu[:, o, :], dots[:, o, :], ACT.Gelu).then_inc(sem("gelu_done"), 1)
                            act.wait_ge(sem("wgt_ready"), g + 1)
                            for k in range(TOPK):
                                act.wait_ge(sem("row_free"), g * TOPK + (TOPK + k - 3))
                                act.activation(diag[:, k % 4, :], ident[:], ACT.Copy, scale=wgt[:, o, k:k + 1]).then_inc(sem("diag_ready"), 1)
                        if more:
                            gate_exp(it + (b * NR + 2), it * (PR * TOPK) + (b * NR + 2) * PR * TOPK)
                act.wait_ge(sem("row_free"), TOPK + (b + 1) * PH * TOPK)
                act.activation(xres[:, b, :], ps[:, 6 - 2 * b:8 - 2 * b, :].rearrange("p a b -> p (a b)"), ACT.Copy).then_inc(sem("x3_ready"), 1)
            norm_act(act, 2, "x3_ready", NB, NPEER)

            def leave2(n, g):
                nm = chunks[n][0]
                c = n - NPEER
                h = 2 * c + g
                act.wait_ge(sem("unit_used"), unit[n, g] + 2)
                bank = ps[:, h % LB, :]
                bank2 = bank.rearrange("p (a b) -> p a b", a=2)
                if nm == "sb":
                    ins = act.activation(p2[:, :, c * CW + g * HALF:c * CW + (g + 1) * HALF], bank.rearrange("p (b c) -> p b c", b=NB), ACT.Copy)
                elif nm == "hv":
                    ins = act.activation(hv[:, :, g * HALF:(g + 1) * HALF], bank.rearrange("p (b c) -> p b c", b=NB), ACT.Copy)
                elif nm == "g2":
                    t = 4 * (c - 7) + 2 * g
                    ins = act.activation(sg2[:, t:t + 2, :], bank2, ACT.Sigmoid)
                else:
                    dst = {"hq": hq, "hf": hf, "hg": hg}[nm]
                    ins = act.activation(dst[:, 2 * g:2 * g + 2, :], bank2, ACT.Sigmoid if nm == "hf" else ACT.Silu)
                ins.then_inc(sem("p2_evac"), 1)

            def turn_sb(_):
                act.wait_ge(sem("lb_shifted"), 1)
                act.activation(lbs[:, 1:3, :], lbs[:, 1:3, :], ACT.Exp).then_inc(sem("lb_exp"), 1)
                for b in range(NB):
                    act.wait_ge(sem("sb_ms"), b + 1)
                    act.activation(hst2[:, 1, :], hst2[:, 0, :], ACT.Sqrt).then_inc(sem("sb_root"), 1)
                act.wait_ge(sem("sb_turned"), 1)
                for j in range(4):
                    ins = act.activation(qkT2[:, 2 * j:2 * j + 2, :], ps[:, 4 + j, :].rearrange("p (a b) -> p a b", a=2), ACT.Copy,
                                         scale=sbgain[:, j // 2:j // 2 + 1])
                ins.then_inc(sem("sbT_ready"), 1)

            def stick(k):
                if 1 <= k <= BATCHES:
                    act.wait_ge(sem("logw_ready"), k)
                    act.activation(wT[:, (k - 1) % 2, :, :], zm[:, (k - 1) % 2, :, :], ACT.Exp).then_inc(sem("w_ready"), 1)
                if k < BATCHES:
                    z, e = zm[:, k % 2, :, :], sp_[:, k % 2, :, :]
                    act.wait_ge(sem("zm_ready"), k + 1)
                    link(act.activation(e, z, ACT.Abs))
                    link(act.activation(e, e, ACT.Exp, scale=-1.0))
                    act.activation(e, e, ACT.Ln, bias=1.0).then_inc(sem("sp_ln"), 1)
                if k >= 2:
                    act.wait_ge(sem("osb_done"), k - 1)
                    act.activation(osbT[:, k - 2, :], ps[:, 3, 0:S], ACT.Copy).then_inc(sem("osb_evac"), 1)

            x4 = [xbuf[:, i, :, :].rearrange("p h (c r) -> p (h c) r", r=HC) for i in range(2)]

            def pairs(j0):
                if j0 == 0:
                    act.wait_ge(sem("f_ready"), 1)
                    act.activation(hf, hf, ACT.Ln).then_inc(sem("logf_ready"), 1)
                    act.wait_ge(sem("bb_ready"), 1)
                    act.activation(qe, bb, ACT.Exp)
                    act.activation(dec[:].rearrange("p h c -> p (h c)"), bb.rearrange("p h (c r) -> p (h c) r", r=HC)[:, :, HC - 1], ACT.Exp).then_inc(sem("eb_ready"), 1)
                    act.wait_ge(sem("left_ready"), 1)
                    act.activation(keT, keT, ACT.Exp).then_inc(sem("eleft_ready"), 1)
                for j in range(j0, j0 + 2):
                    act.wait_ge(sem("diff_ready"), j + 1)
                    act.activation(x4[j % 2][:, :, j:HC], x4[j % 2][:, :, j:HC], ACT.Exp).then_inc(sem("diff_exp"), 1)

            def turn_ke(_):
                act.wait_ge(sem("ke_turned"), 1)
                for b in range(NB):
                    ins = act.activation(ket[:, b, :, :], ps[:, 6 + b, :].rearrange("p (a b) -> p a b", a=HH), ACT.Copy)
                ins.then_inc(sem("ket_ready"), 1)

            do = {"turn_sb": turn_sb, "stick": stick, "pairs": pairs, "turn_ke": turn_ke}
            order = list(plan2)
            for i in range(1, len(order)):
                if order[i][0] == "pairs" and order[i][1] > 0 and order[i - 1][0] == "half":
                    order[i - 1], order[i] = order[i], order[i - 1]
            for what, n, *g in order:
                if what == "half":
                    leave2(n, g[0])
                    for half in next_half(n, g[0], N2):
                        upper_parts(act, *half)
                elif what in do:
                    do[what](n)
            for n, g in halves_of(N2, N2 + 1):
                upper_parts(act, n, g)
            act.wait_ge(sem("read_done"), NHC - 1)
            for b in range(NB):
                act.activation(osq[:, :, b, :], ps[:, 4 + b, :].rearrange("p (a b) -> p a b", a=HH), ACT.Square).then_inc(sem("osq_ready"), 1)
            act.wait_ge(sem("oms_ready"), 2)
            act.activation(orr, orr, ACT.Sqrt).then_inc(sem("oroot"), 1)
            for n, g in halves_of(N2 + 1, NFFN):
                upper_parts(act, n, g)
            norm_act(act, 3, "x4_ready", 4, NFFN)
            c = 0
            for i, (n, g) in enumerate(ffn_halves):
                if chunks[n][0] == "gate_up" and g == 0:
                    act.wait_ge(sem("unit_used"), ffn_unit[c] + 2)
                    if c >= 2:
                        act.wait_ge(sem("hid_ready"), c - 1)
                    act.activation(silu[:, c % 2, :, :], ps[:, (2 * c) % 4, :].rearrange("p (a b) -> p a b", a=2), ACT.Silu).then_inc(sem("silu_ready"), 1)
                    c += 1
                for half in ffn_halves[i + 2:i + 3]:
                    upper_parts(act, *half)

        @block.vector
        def _(dve):
            step = [0]

            def link(ins):
                step[0] += 1
                ins.then_inc(sem("dve_step"), 1)
                dve.wait_ge(sem("dve_step"), step[0])

            norm_dve(dve, link, 0)
            dve.wait_ge(sem("small_loaded"), NSMALL * 16)
            link(dve.tensor_copy(posf[:], pos_i[:]))
            for b in range(NB):
                link(dve.tensor_scalar(ang[:, 0, b, :], freq[:], posf[:, b:b + 1], None, ALU.mult))
            flat = [ang[:, k, :, :].rearrange("p a b -> p (a b)") for k in range(4)]
            link(dve.tensor_scalar(flat[1], flat[0], 1.0 / (2 * np.pi), MAGIC, ALU.mult, ALU.add))
            link(dve.tensor_scalar(flat[1], flat[1], MAGIC, None, ALU.subtract))
            for part in TWO_PI_PARTS:
                link(dve.scalar_tensor_tensor(out=flat[0], in0=flat[1], scalar=-part, in1=flat[0], op0=ALU.mult, op1=ALU.add))
            link(dve.tensor_scalar(flat[1], flat[0], np.pi / 2, None, ALU.add))
            link(dve.tensor_scalar(flat[2], flat[1], np.pi, -2 * np.pi, ALU.is_gt, ALU.mult))
            link(dve.tensor_tensor(flat[1], flat[1], flat[2], ALU.add))
            link(dve.tensor_scalar(flat[2], flat[1], PI_IN, -PI_IN, ALU.min, ALU.max))
            dve.tensor_scalar(flat[3], flat[0], PI_IN, -PI_IN, ALU.min, ALU.max).then_inc(sem("angles"), 1)
            dve.wait_ge(sem("p1_evac"), 6)
            NH = AH + AKV
            for b in range(NB):
                qk = p1[:, b, 0:NH * AD]
                qk3 = qk.rearrange("p (h d) -> p h d", d=AD)
                sq3 = sq.rearrange("p (h d) -> p h d", d=AD)
                link(dve.tensor_tensor(sq, qk, qk, ALU.mult))
                link(dve.tensor_reduce(hst[:, 0, :], sq3, AX, ALU.add))
                dve.tensor_scalar(hst[:, 0, :], hst[:, 0, :], 1.0 / AD, EPS, ALU.mult, ALU.add).then_inc(sem("qk_ms"), 1)
                dve.wait_ge(sem("qk_root"), b + 1)
                link(dve.reciprocal(hst[:, 2, :], hst[:, 1, :]))
                link(dve.tensor_tensor(qk3, qk3, hst[:, 2, :].unsqueeze(2).broadcast_to([P, NH, AD]), ALU.mult))
                dve.tensor_tensor(qk3[:, 0:AH, :], qk3[:, 0:AH, :], qkgain[:, 0:1, :].broadcast_to([P, AH, AD]), ALU.mult)
                link(dve.tensor_tensor(qk3[:, AH:NH, :], qk3[:, AH:NH, :], qkgain[:, 1:2, :].broadcast_to([P, AKV, AD]), ALU.mult))
                if b == 0:
                    dve.wait_ge(sem("sines"), 1)
                x1, x2 = qk3[:, :, 0:RH], qk3[:, :, RH:ROPE]
                co = cs[:, 0, b:b + 1, :].broadcast_to([P, NH, RH])
                si = cs[:, 1, b:b + 1, :].broadcast_to([P, NH, RH])
                dve.tensor_tensor(rt[:, 0, :, :], x1, co, ALU.mult)
                dve.tensor_tensor(rt[:, 1, :, :], x2, si, ALU.mult)
                dve.tensor_tensor(rt[:, 2, :, :], x2, co, ALU.mult)
                link(dve.tensor_tensor(rt[:, 3, :, :], x1, si, ALU.mult))
                dve.tensor_tensor(x1, rt[:, 0, :, :], rt[:, 1, :, :], ALU.subtract)
                link(dve.tensor_tensor(x2, rt[:, 2, :, :], rt[:, 3, :, :], ALU.add))
                kk = p1[:, b, AK0:AV0].rearrange("p (h d) -> p h d", d=AD)
                kdv = kd[:, b, :].rearrange("p (h two d) -> p h two d", two=2, d=AD)
                dve.tensor_copy(kdv[:, :, 0, :], kk)
                dve.tensor_copy(kdv[:, :, 1, :], kk).then_inc(sem("qk_rotated"), 1)
            def scores_in(k):
                b, q = k // 4, k % 4
                nk = P * (b + 1)
                m3 = mask_band[:, 1 - b:2, :].rearrange("p a b -> p (a b)").unsqueeze(1)
                x, a_ = sm[:, k % 2, :, :], am[:, k % 2, :, :]
                dve.wait_ge(sem("scores"), k + 1)
                if k >= 2:
                    dve.wait_ge(sem("probs_turned"), k - 1)
                for i in range(2):
                    ins = dve.scalar_tensor_tensor(out=x[:, i::2, 0:nk], in0=ps[:, 4 + i, :].rearrange("p (a b) -> p a b", a=2)[:, :, 0:nk],
                                                   scalar=AD ** -0.5, in1=m3.broadcast_to([P, 2, nk]), op0=ALU.mult, op1=ALU.add)
                ins.then_inc(sem("scores_read"), 1)
                dve.wait_ge(sem("scores_read"), k + 1)
                link(dve.tensor_reduce(a_[:, 0, :], x[:, :, 0:nk], AX, ALU.max))
                snk = sinks[:, 4 * q:4 * q + 4]
                link(dve.tensor_tensor(a_[:, 0, :], a_[:, 0, :], snk, ALU.max))
                dve.tensor_scalar(a_[:, 1, :], a_[:, 0, :], -1.0, None, ALU.mult)
                dve.tensor_tensor(a_[:, 3, :], snk, a_[:, 0, :], ALU.subtract).then_inc(sem("row_max"), 1)
                dve.wait_ge(sem("exps"), k + 1)
                link(dve.tensor_tensor(a_[:, 5, :], a_[:, 2, :], a_[:, 4, :], ALU.add))
                link(dve.reciprocal(a_[:, 0, :], a_[:, 5, :]))
                dve.tensor_tensor(x[:, :, 0:nk], x[:, :, 0:nk], a_[:, 0, :].unsqueeze(2).broadcast_to([P, 4, nk]),
                                  ALU.mult).then_inc(sem("probs"), 1)

            for k in range(GROUPS):
                scores_in(k)
            mif = p1[:, :, AV0 + AKV * AD:AV0 + AKV * AD + 2 * MH]
            for k in range(2):
                ins = dve.tensor_tensor(gt[:, k, :, :], mif[:, :, k * MH:(k + 1) * MH], ifbias[:, k:k + 1, :].broadcast_to([P, NB, MH]), ALU.add)
            ins.then_inc(sem("gates_raw"), 1)
            dve.wait_ge(sem("gates_tanh"), 1)
            dve.tensor_scalar(gt[:, 0:2, :, :], gt[:, 2:4, :, :], CAP, None, ALU.mult).then_inc(sem("gates_cap"), 1)
            dve.wait_ge(sem("gates_soft"), 1)
            dve.tensor_scalar(gt[:, 1, :, :], gt[:, 3, :, :], -1.0, None, ALU.mult).then_inc(sem("gates_tok"), 1)
            dve.wait_ge(sem("rows_gates"), 1)
            link(dve.tensor_tensor_scan(rows[:, 2, :], ones[0:MH, 0:1].broadcast_to([MH, S]), rows[:, 1, :], 0.0, ALU.mult, ALU.add))
            link(dve.tensor_tensor(rows[:, 3, :], rows[:, 0, :], rows[:, 2, :], ALU.subtract))
            link(dve.tensor_tensor_scan(rows[:, 4, :], rows[:, 3, :], rows[:, 3, :], 0.0, ALU.max, ALU.max))
            link(dve.tensor_tensor(rows[:, 5, :], rows[:, 2, :], rows[:, 4, :], ALU.add))
            dve.tensor_scalar(rows[:, 4, :], rows[:, 4, :], -1.0, None, ALU.mult).then_inc(sem("m_rows"), 1)
            dve.wait_ge(sem("m_spread"), 1)
            mi3 = mask_inc[:].unsqueeze(1)
            for j in range(4):
                bank = ps[:, 4 + j, :].rearrange("p (h b c) -> p h b c", h=2, b=2)
                dve.tensor_tensor(wl[:, 2 * j:2 * j + 2, 0, :], bank[:, :, 0, :], mi3.broadcast_to([P, 2, P]), ALU.add)
                ins = dve.tensor_tensor(wl[:, 2 * j:2 * j + 2, 2, :], bank[:, :, 1, :], mi3.broadcast_to([P, 2, P]), ALU.add)
            ins.then_inc(sem("wl_masked"), 1)

            def mix(k):
                if k < 4:
                    dve.wait_ge(sem("br_done"), k + 1)
                else:
                    dve.wait_ge(sem("unit_used"), unit[NML, 0] + 2 * (k - 4) + 2)
                bank = ps[:, k % LB, :].rearrange("p (a b) -> p a b", a=2)
                t = slice(2 * (k % 4), 2 * (k % 4) + 2)
                if k < 4:
                    dve.wait_ge(sem("p1_evac"), 2 * NW1)
                    dve.tensor_tensor(mixT[:, t, :], bank, sga[:, t, :], ALU.mult).then_inc(sem("br_evac"), 1)
                else:
                    link(dve.tensor_tensor(tmpT[:, t, :], bank, sgm[:, t, :], ALU.mult))
                    link(dve.tensor_tensor(mixT[:, t, :], mixT[:, t, :], tmpT[:, t, :], ALU.add))
                    link(dve.tensor_copy(mixT_hi[:, t, :], mixT[:, t, :]))
                    dve.tensor_tensor(mixT_lo[:, t, :], mixT[:, t, :], mixT_hi[:, t, :].bitcast(F32), ALU.subtract).then_inc(sem("br_evac"), 1)

            mixed = 0
            for what, n, *g in plan1:
                if what == "half" and n >= NW1:
                    mix(mixed)
                    mixed += 1
                if what == "memory" and n < MH:
                    h = n
                    dve.wait_ge(sem("wl_ready"), h + 1)
                    dve.wait_ge(sem("ml_qk"), h + 1)
                    if h >= 2:
                        dve.wait_ge(sem("num_done"), h - 1)
                    dve.scalar_tensor_tensor(out=cw[:, h % 2, :], in0=ps[:, 4 + h % 2, 0:3 * P], scalar=MQ ** -0.5,
                                             in1=wl[:, h, :, :].rearrange("p a b -> p (a b)"), op0=ALU.mult,
                                             op1=ALU.mult).then_inc(sem("cw_ready"), 1)
            dve.wait_ge(sem("num_evac"), MH)
            dn = hraw[:, :, :, MV]
            link(dve.scalar_tensor_tensor(out=den[:, 0, :, :], in0=dn, scalar=-1.0, in1=dn, op0=ALU.mult, op1=ALU.max))
            link(dve.tensor_tensor(den[:, 0, :, :], den[:, 0, :, :], em[:], ALU.max))
            link(dve.reciprocal(den[:, 1, :, :], den[:, 0, :, :]))
            for b in range(NB):
                link(dve.tensor_tensor(hs[:, b, :, :], hraw[:, b, :, 0:MV], den[:, 1, b, :].unsqueeze(2).broadcast_to([P, MH, MV]), ALU.mult))
            link(dve.tensor_tensor(hsq, hs, hs, ALU.mult))
            link(dve.tensor_reduce(den[:, 0, :, :], hsq, AX, ALU.add))
            dve.tensor_scalar(den[:, 1, :, :], den[:, 0, :, :], 1.0 / MV, EPS, ALU.mult, ALU.add).then_inc(sem("hm_ms"), 1)
            dve.wait_ge(sem("hm_root"), 1)
            link(dve.reciprocal(den[:, 0, :, :], den[:, 2, :, :]))
            for b in range(NB):
                link(dve.tensor_tensor(hs[:, b, :, :], hs[:, b, :, :], den[:, 0, b, :].unsqueeze(2).broadcast_to([P, MH, MV]), ALU.mult))
            dve.tensor_tensor(hs, hs, mo.rearrange("p b (h v) -> p b h v", h=MH), ALU.mult).then_inc(sem("hm_tok"), 1)
            for t in range(KT):
                dve.wait_ge(sem("hmT_hi_ready"), t // 2 * 2 + 2)
                dve.scalar_tensor_tensor(out=hmT_lo[:, t, :], in0=ps[:, 4 + t // 2, (t % 2) * S:(t % 2 + 1) * S], scalar=mlgain[:, t:t + 1],
                                         in1=hmT_hi[:, t, :].bitcast(F32), op0=ALU.mult, op1=ALU.subtract).then_inc(sem("hmT_ready"), 1)
            for k in range(4, 8):
                mix(k)

            def add_half(i, n, g, ready):
                dve.wait_ge(sem("unit_used"), unit[n, g] + 2)
                x = xres[:, :, i * HALF:(i + 1) * HALF]
                dve.tensor_tensor(x, x, ps[:, i % LB, :].rearrange("p (b c) -> p b c", b=NB), ALU.add).then_inc(sem(ready), 1)

            for i, (n, g) in enumerate(halves_of(NML + 2, NQUERY)):
                add_half(i, n, g, "x2_ready")

            norm_dve(dve, link, 1)
            def top16(values, vals, where, rows):
                for half in range(2):
                    e = slice(8 * half, 8 * half + 8)
                    for r in range(rows):
                        ins = dve.max(vals[r][:, e], values[r])
                    link(ins)
                    for r in range(rows):
                        ins = dve.max_index(where[r][:, e], vals[r][:, e], values[r])
                    link(ins)
                    if half == 0:
                        for r in range(rows):
                            ins = dve.match_replace(values[r], vals[r][:, e], values[r], -3.0e38)
                        link(ins)

            gate4 = gates[:].rearrange("p (r h k) -> p r h k", h=PR, k=TOPK)

            def route(r):
                b, h0 = r // NR, r % NR * PR
                dve.wait_ge(sem("scr_ready"), r + 1)
                hp = [(h, p) for h in range(PR) for p in range(2)]
                top16([scr[b][:, h0 + h, p, :] for h, p in hp], [tv[:, h, p, :] for h, p in hp], [ti[:, h, p, :] for h, p in hp], len(hp))
                flat = "p a b c -> p (a b c)"
                link(dve.tensor_copy(tif.rearrange(flat), ti.rearrange(flat)))
                cand = scr[b][:, h0:h0 + PR, :, :].rearrange("p h q k -> p h (q k)")
                c4 = cand.rearrange("p h (i j) -> p h i j", i=TOPK)
                link(dve.tensor_tensor(c4, tv[:, :, 0, :].unsqueeze(3).broadcast_to([P, PR, TOPK, TOPK]),
                                       tv[:, :, 1, :].unsqueeze(2).broadcast_to([P, PR, TOPK, TOPK]), ALU.add))
                top16([cand[:, h, :] for h in range(PR)], [bv[:, h, :] for h in range(PR)], [bp[:, h, :] for h in range(PR)], PR)
                bpf = bp.rearrange("p a b -> p (a b)")
                dve.tensor_scalar(bij[:, 0, :], bpf, 4, None, ALU.logical_shift_right)
                link(dve.tensor_scalar(bij[:, 1, :], bpf, TOPK - 1, None, ALU.bitwise_and))
                link(dve.tensor_copy(bijf.rearrange("p a b -> p (a b)"), bij.rearrange("p a b -> p (a b)")))
                for p in range(2):
                    hot3 = hot.rearrange("p h k i -> p (h k) i")
                    link(dve.tensor_tensor(hot3, bijf[:, p, :].unsqueeze(2).broadcast_to([P, PR * TOPK, TOPK]),
                                           iota16[:].unsqueeze(1).broadcast_to([P, PR * TOPK, TOPK]), ALU.is_equal))
                    link(dve.tensor_tensor(picked, hot, tif[:, :, p, :].unsqueeze(2).broadcast_to([P, PR, TOPK, TOPK]), ALU.mult))
                    link(dve.tensor_reduce(exf[:, p, :], picked.rearrange("p h k i -> p (h k) i"), AX, ALU.add))
                link(dve.scalar_tensor_tensor(out=exf[:, 2, :], in0=exf[:, 0, :], scalar=float(NKEY), in1=exf[:, 1, :], op0=ALU.mult, op1=ALU.add))
                dve.tensor_copy(idx[:, b, h0 * TOPK:(h0 + PR) * TOPK], exf[:, 2, :]).then_inc(sem("routed"), 1)
                dve.tensor_tensor(gate4[:, r, :, :], bv, bv[:, :, 0:1].broadcast_to([P, PR, TOPK]), ALU.subtract).then_inc(sem("best_shifted"), 1)

            def finish_gates(r):
                dve.wait_ge(sem("best_exp"), r + 1)
                link(dve.tensor_reduce(gsum[:, 0, :], gate4[:, r, :, :], AX, ALU.add))
                link(dve.reciprocal(gsum[:, 1, :], gsum[:, 0, :]))
                link(dve.tensor_tensor(gate4[:, r, :, :], gate4[:, r, :, :], gsum[:, 1, :].unsqueeze(2).broadcast_to([P, PR, TOPK]), ALU.mult))

            dve.wait_ge(sem("masks2_ready"), 1)
            dve.memset(dots[:], 0.0).then_inc(sem("drow_free"), DSLOTS)
            dve.wait_ge(sem("drow_free"), DSLOTS)
            route(0)
            route(1)
            for r in range(NB * NR):
                b = r // NR
                finish_gates(r)
                for o in range(PR):
                    g = r * PR + o
                    for k in range(TOPK):
                        dve.wait_ge(sem(f"drow{k % DSLOTS}"), g * 32 + (16 + 16 * (k // DSLOTS)))
                        row = rows_d[:, k % DSLOTS, :]
                        dve.tensor_tensor_reduce(row, row, h2[:, b, :], 1.0, 0.0, ALU.mult, ALU.add,
                                                 dots[:, o, k:k + 1]).then_inc(sem("drow_free"), 1)
                    dve.wait_ge(sem("gelu_done"), g + 1)
                    dve.tensor_tensor(wgt[:, o, :], gelu[:, o, :], gate4[:, r, o, :], ALU.mult).then_inc(sem("wgt_ready"), 1)
                if r + 2 < NB * NR:
                    route(r + 2)

            norm_dve(dve, link, 2)
            link(dve.tensor_tensor(lbs[:, 0, :], lbt[:, 0, :], lbt[:, 1, :], ALU.max))
            dve.tensor_tensor(lbs[:, 1:3, :], lbt[:], lbs[:, 0:1, :].broadcast_to([P, 2, HH]), ALU.subtract).then_inc(sem("lb_shifted"), 1)
            dve.wait_ge(sem("p2_evac"), 6)
            for b in range(NB):
                qk = p2[:, b, 0:2 * SBW]
                qk3 = qk.rearrange("p (h d) -> p h d", d=SD)
                sqs = zm.rearrange("p a b c -> p (a b c)")[:, 0:2 * SBW]
                link(dve.tensor_tensor(sqs, qk, qk, ALU.mult))
                link(dve.tensor_reduce(hst2[:, 0, :], sqs.rearrange("p (h d) -> p h d", d=SD), AX, ALU.add))
                dve.tensor_scalar(hst2[:, 0, :], hst2[:, 0, :], 1.0 / SD, EPS, ALU.mult, ALU.add).then_inc(sem("sb_ms"), 1)
                dve.wait_ge(sem("sb_root"), b + 1)
                link(dve.reciprocal(hst2[:, 2, :], hst2[:, 1, :]))
                ins = dve.tensor_tensor(qk3, qk3, hst2[:, 2, :].unsqueeze(2).broadcast_to([P, 2 * SH, SD]), ALU.mult)
                if b == 0:
                    link(ins)
                else:
                    ins.then_inc(sem("sb_normed"), 1)
            ms3 = mask_str[:].unsqueeze(1).broadcast_to([P, 2, P])
            sc = SD ** -0.5
            for k in range(BATCHES + 1):
                if k < BATCHES:
                    z = zm[:, k % 2, :, :]
                    dve.wait_ge(sem("z_done"), k + 1)
                    if k >= 2:
                        dve.wait_ge(sem("w_ready"), k - 1)
                    for c0 in (0, S):
                        dve.scalar_tensor_tensor(out=z[:, :, c0:c0 + P], in0=ps[:, 4:6, c0:c0 + P], scalar=sc, in1=ms3, op0=ALU.mult, op1=ALU.add)
                    dve.tensor_scalar(z[:, :, P:S], ps[:, 4:6, P:S], sc, None, ALU.mult).then_inc(sem("zm_ready"), 1)
                if k >= 1:
                    z = zm[:, (k - 1) % 2, :, :]
                    dve.wait_ge(sem("rest_done"), k)
                    dve.tensor_tensor(z, z, ps[:, 6:8, 0:3 * P], ALU.subtract).then_inc(sem("logw_ready"), 1)
                if k < BATCHES:
                    z, e = zm[:, k % 2, :, :], sp_[:, k % 2, :, :]
                    dve.wait_ge(sem("sp_ln"), k + 1)
                    fz = "p a b -> p (a b)"
                    dve.scalar_tensor_tensor(out=e.rearrange(fz), in0=z.rearrange(fz), scalar=0.0, in1=e.rearrange(fz), op0=ALU.max, op1=ALU.add).then_inc(sem("sp_ready"), 1)
            dve.wait_ge(sem("lb_exp"), 1)
            link(dve.tensor_tensor(lbs[:, 3, :], lbs[:, 1, :], lbs[:, 2, :], ALU.add))
            link(dve.reciprocal(lbs[:, 4, :], lbs[:, 3, :]))
            link(dve.tensor_tensor(lbs[:, 0, :], lbs[:, 1, :], lbs[:, 4, :], ALU.mult))
            link(dve.tensor_scalar(lbs[:, 3, :], lbs[:, 0, :], -1.0, 1.0, ALU.mult, ALU.add))
            dve.wait_ge(sem("osb_evac"), BATCHES)
            link(dve.tensor_copy(osbT_hi, osbT))
            dve.tensor_tensor(osbT_lo, osbT, osbT_hi.bitcast(F32), ALU.subtract).then_inc(sem("osb_split"), 1)
            dve.wait_ge(sem("osb_split"), 1)
            dve.wait_ge(sem("p2_evac"), 14)
            for h in range(HH):
                ins = dve.tensor_scalar(hf[:, h, :], hf[:, h, :], lbs[:, 3, h:h + 1], lbs[:, 0, h:h + 1], ALU.mult, ALU.add)
            link(ins)
            fl = "p a b -> p (a b)"
            dve.tensor_scalar(key.rearrange(fl), hf.rearrange(fl), -1.0, 1.0, ALU.mult, ALU.add).then_inc(sem("f_ready"), 1)
            for o in range(2):
                ins = dve.tensor_scalar(vpar[:, o, :, :].rearrange(fl), hv.rearrange(fl), par[:, o:o + 1], None, ALU.mult)
            ins.then_inc(sem("vpar_ready"), 1)
            dve.wait_ge(sem("logf_ready"), 1)
            dve.tensor_tensor_scan(bb.rearrange(fl), restart[:], hf.rearrange(fl), 0.0, ALU.mult, ALU.add).then_inc(sem("bb_ready"), 1)
            dve.wait_ge(sem("bb_ready"), 1)
            b4 = bb.rearrange("p h (c r) -> p (h c) r", r=HC)
            k4 = keT.rearrange("p h (c r) -> p (h c) r", r=HC)
            key4 = key.rearrange("p h (c r) -> p (h c) r", r=HC)
            q4 = hq.rearrange("p h (c r) -> p (h c) r", r=HC)
            dve.tensor_tensor(k4, b4[:, :, HC - 1:HC].broadcast_to([P, HH * NHC, HC]), b4, ALU.subtract).then_inc(sem("left_ready"), 1)
            dve.wait_ge(sem("eb_ready"), 1)
            dve.tensor_tensor(qe, qe, hq, ALU.mult)
            dve.wait_ge(sem("eleft_ready"), 1)
            dve.tensor_tensor(keT, keT, key, ALU.mult).then_inc(sem("keT_ready"), 1)
            x4 = [xbuf[:, i, :, :].rearrange("p h (c r) -> p (h c) r", r=HC) for i in range(2)]

            def diff(j):
                if j >= 2:
                    dve.wait_ge(sem("pairs_summed"), j - 1)
                dve.tensor_tensor(x4[j % 2][:, :, j:HC], b4[:, :, j:HC], b4[:, :, j:j + 1].broadcast_to([P, HH * NHC, HC - j]),
                                  ALU.subtract).then_inc(sem("diff_ready"), 1)

            diff(0)
            for j in range(HC):
                if j + 1 < HC:
                    diff(j + 1)
                x = x4[j % 2][:, :, j:HC]
                dve.wait_ge(sem("diff_exp"), j + 1)
                link(dve.tensor_tensor(x, x, q4[:, :, j:HC], ALU.mult))
                dve.tensor_tensor(x, x, key4[:, :, j:j + 1].broadcast_to([P, HH * NHC, HC - j]), ALU.mult).then_inc(sem("pairs_ready"), 1)
            dve.wait_ge(sem("pairs_summed"), HC)
            for c in range(2):
                ins = dve.tensor_tensor(AT[:, 2 * c:2 * c + 2, :, :].rearrange("p h b t -> p (h b) t"), ps[:, 4 + c, :].rearrange("p (a b) -> p a b", b=P),
                                        m16[:].unsqueeze(1).broadcast_to([P, 4, P]), ALU.mult)
            ins.then_inc(sem("AT_ready"), 1)
            for c in range(NHC - 1):
                dve.wait_ge(sem("inc_done"), c + 1)
                if c >= 3:
                    dve.wait_ge(sem("read_done"), c - 2)
                for h in range(HH):
                    new = state[:, (c + 1) % 3, h, :]
                    inc = ps[:, 6 + c % 2, h * P:(h + 1) * P]
                    if c == 0:
                        ins = dve.tensor_copy(new, inc)
                    else:
                        ins = dve.scalar_tensor_tensor(out=new, in0=state[:, c % 3, h, :], scalar=dec[:, h, c:c + 1], in1=inc, op0=ALU.mult, op1=ALU.add)
                ins.then_inc(sem("state_ready"), 1)
                dve.wait_ge(sem("state_ready"), c + 1)
            dve.wait_ge(sem("osq_summed"), 1)
            for b in range(NB):
                dve.tensor_scalar(orr[:, :, b, :], ps[:, 6 + b, :].rearrange("p (a b) -> p a b", a=HH), 1.0 / HV, EPS, ALU.mult, ALU.add).then_inc(sem("oms_ready"), 1)
            dve.wait_ge(sem("oroot"), 1)
            link(dve.reciprocal(orr, orr))
            for b in range(NB):
                ins = dve.scalar_tensor_tensor(out=ohgT[:, :, b * P:(b + 1) * P], in0=ps[:, 4 + b, :].rearrange("p (a b) -> p a b", a=HH), scalar=hgain[:, 0:1],
                                               in1=orr[:, :, b, :], op0=ALU.mult, op1=ALU.mult)
            link(ins)
            link(dve.tensor_tensor(ohgT, ohgT, hg, ALU.mult))
            link(dve.tensor_copy(ohgT_hi, ohgT))
            dve.tensor_tensor(ohgT_lo, ohgT, ohgT_hi.bitcast(F32), ALU.subtract).then_inc(sem("ohg_ready"), 1)
            for k in range(8):
                dve.wait_ge(sem("unit_used"), unit[N2, 0] + 2 * (k // 2) + 2)
                bank = ps[:, k % 4, :]
                dve.tensor_tensor(mixT2[:, k, :], bank[:, 0:S], sg2[:, k, :], ALU.mult)
                link(dve.tensor_tensor(tmp2[:, 0, :], bank[:, S:2 * S], sg2[:, KT + k, :], ALU.mult))
                link(dve.tensor_tensor(mixT2[:, k, :], mixT2[:, k, :], tmp2[:, 0, :], ALU.add))
                link(dve.tensor_copy(mixT2_hi[:, k, :], mixT2[:, k, :]))
                dve.tensor_tensor(mixT2_lo[:, k, :], mixT2[:, k, :], mixT2_hi[:, k, :].bitcast(F32), ALU.subtract).then_inc(sem("br2_evac"), 1)
                dve.wait_ge(sem("br2_evac"), k + 1)
            for i, (n, g) in enumerate(halves_of(N2 + 2, NFFN)):
                add_half(i, n, g, "x4_ready")
            norm_dve(dve, link, 3)
            for c in range(NFF):
                dve.wait_ge(sem("unit_used"), ffn_unit[c] + 4)
                dve.wait_ge(sem("silu_ready"), c + 1)
                if c >= 4:
                    dve.wait_ge(sem("unit_used"), unit[down_half[c - 4]] + 2)
                x = silu[:, c % 2, :, :]
                link(dve.tensor_tensor(x, x, ps[:, (2 * c + 1) % 4, :].rearrange("p (a b) -> p a b", a=2), ALU.mult))
                link(dve.tensor_copy(hid_hi[:, c % 4, :, :], x))
                dve.tensor_tensor(hid_lo[:, c % 4, :, :], x, hid_hi[:, c % 4, :, :].bitcast(F32), ALU.subtract).then_inc(sem("hid_ready"), 1)
            dve.wait_ge(sem("unit_used"), unit[down_half[NFF - 1]] + 2)
            for b in range(NB):
                for c in range(2):
                    dve.tensor_tensor(xres[:, b, c * CW:(c + 1) * CW], xres[:, b, c * CW:(c + 1) * CW],
                                      ps[:, 4 + 2 * b + c, :], ALU.add).then_inc(sem("x5_ready"), 1)


def lay_out(inp):
    c = np.ascontiguousarray
    f = lambda k: np.asarray(inp[k])
    col = lambda v: v.reshape(KT, P).T
    rep = lambda v: np.broadcast_to(v, (P,) + v.shape)
    return {
        "x": c(f("x")[0]),
        "w_in": c(f("w_in")[0]),
        "w_branch_attn": c(f("w_branch_attn")[0]),
        "w_branch_mlstm": c(f("w_branch_mlstm")[0]),
        "w_out": c(f("w_out")[0]),
        "gcol": c(np.stack([col(f(k)[0]) for k in ("norm1_gain", "norm2_gain", "norm1_g_2", "norm2_g_2")], 1)),
        "mlgain": c(col(f("ml_out_norm_gain")[0])),
        "qkgain": c(rep(np.stack([f("q_norm_gain")[0], f("k_norm_gain")[0]]))),
        "sinks": c(rep(f("attn_sinks")[0])),
        "ifbias": c(rep(np.stack([f("ml_i_bias")[0], f("ml_f_bias")[0]]))),
        "pos": c(f("positions").reshape(NB, P).T.astype(np.int32)),
        "freq": c(rep(inv_freq())),
        "peer_w_query": c(f("peer_w_query")[0]),
        "sub_keys": c(f("peer_sub_keys")[0].transpose(1, 3, 0, 2).reshape(P, PH, NKEY)),
        "n2row": c(rep(f("norm2_gain")[0])),
        "peer_down": c(f("peer_down")[0]),
        "peer_up": c(f("peer_up")[0]),
        "w_in_2": c(f("w_in_2")[0]),
        "w_branch_2": c(f("w_branch_2")[0]),
        "w_out_2": c(f("w_out_2")[0]),
        "w_ffn_gate_2": c(f("w_ffn_gate_2")[0]),
        "w_ffn_up_2": c(f("w_ffn_up_2")[0]),
        "w_ffn_down_2": c(f("w_ffn_down_2")[0]),
        "sbgain": c(np.stack([np.tile(f(k)[0], 2) for k in ("q_norm_g_2", "k_norm_g_2")], 1)),
        "hgain": c(f("hg_norm_g_2")[0].reshape(P, 1)),
        "lbt": c(f("lb_table_2").reshape(2, HH, HK).transpose(2, 0, 1)),
    }


def kernel(**inputs):
    import concourse.bacc as bacc
    from concourse.bass_utils import run_bass_kernel_spmd

    nc = bacc.Bacc("TRN2", target_bir_lowering=False, num_devices=1)
    arrays = lay_out(inputs)
    aps = {k: nc.dram_tensor(k + "_in", v.shape, mybir.dt.from_np(v.dtype), kind="ExternalInput").ap() for k, v in arrays.items()}
    out = nc.dram_tensor("out", (S, D), F32, kind="ExternalOutput").ap()
    build(nc, aps, out)
    r = run_bass_kernel_spmd(nc, [{k + "_in": v for k, v in arrays.items()}], core_ids=[0])
    return r.results[0]["out"].reshape(1, S, D)
```
